# Optimizing a Trainium2 kernel written in Bass

```python
import math
import jax, jax.numpy as jnp
from jax import lax
import numpy as np

D_MODEL = 1024
BATCH = 1
SEQ = 256
DEPTH = 2

N_HEADS = 4
V_WIDTH = D_MODEL
HEAD_V = V_WIDTH // N_HEADS
HEAD_K = HEAD_V // 2
QK_WIDTH = N_HEADS * HEAD_K
N_BRANCH = 3
CHUNK = 64
CONV_K = 4
ROPE_BASE = 10000.0
RET_DECAY_OFFSET = 5.0
N_EXPERTS = 16
N_GROUPS = 4
EXPERTS_PER_GROUP = N_EXPERTS // N_GROUPS
TOP_K = 2
D_EXPERT = D_MODEL // 2
ALPHA = (2 * DEPTH) ** 0.25
BETA = (8 * DEPTH) ** -0.25
LN_EPS = 1e-5
NORM_EPS = 1e-6
IN_WIDTHS = (
    QK_WIDTH, QK_WIDTH, V_WIDTH, V_WIDTH,
    2 * QK_WIDTH + V_WIDTH, V_WIDTH, N_HEADS, N_HEADS,
    QK_WIDTH, QK_WIDTH, V_WIDTH, V_WIDTH,
    N_BRANCH * D_MODEL,
)
N_IN = sum(IN_WIDTHS)

kernel_name = 'hybrid_retention_gdn_hgrn2_grouped_moe'

def _split_columns(t, widths):
    offs = np.cumsum(widths)[:-1].tolist()
    return jnp.split(t, offs, axis=-1)

def _heads(t, d):
    return t.reshape(t.shape[0], t.shape[1], -1, d)

def _to_chunks(t):
    b, s, h, e = t.shape
    return t.reshape(b, s // CHUNK, CHUNK, h, e).transpose(1, 0, 3, 2, 4)

def _from_chunks(t):
    n, b, h, c, e = t.shape
    return t.transpose(1, 0, 3, 2, 4).reshape(b, n * c, h, e)

def _layer_norm(x, g, b):
    xf = x.astype(jnp.float32)
    mu = jnp.mean(xf, axis=-1, keepdims=True)
    var = jnp.mean(jnp.square(xf - mu), axis=-1, keepdims=True)
    y = (xf - mu) * lax.rsqrt(var + LN_EPS) * g.astype(jnp.float32) + b.astype(jnp.float32)
    return y.astype(x.dtype)

def _head_groupnorm(o):
    mu = jnp.mean(o, axis=-1, keepdims=True)
    var = jnp.mean(jnp.square(o - mu), axis=-1, keepdims=True)
    return (o - mu) * lax.rsqrt(var + NORM_EPS)

def _head_rms(o, g):
    return o * lax.rsqrt(jnp.mean(jnp.square(o), axis=-1, keepdims=True) + NORM_EPS) * g.astype(jnp.float32)

def _l2norm(t):
    return t * lax.rsqrt(jnp.sum(jnp.square(t), axis=-1, keepdims=True) + NORM_EPS)

def _rotary(t, positions):
    half = HEAD_K // 2
    inv_freq = 1.0 / (ROPE_BASE ** jnp.linspace(0.0, 1.0, half, dtype=jnp.float32))
    ang = positions.astype(jnp.float32)[..., None, None] * inv_freq
    cos, sin = jnp.cos(ang), jnp.sin(ang)
    t1, t2 = t[..., :half], t[..., half:]
    return jnp.concatenate([t1 * cos - t2 * sin, t1 * sin + t2 * cos], axis=-1)

def _causal_conv(t, w):
    c = t.shape[-1]
    return lax.conv_general_dilated(t, w[:, None, :], window_strides=(1,),
                                    padding=((CONV_K - 1, 0),),
                                    dimension_numbers=('NWC', 'WIO', 'NWC'),
                                    feature_group_count=c)

def _retention(q, k, v):
    lg = jnp.log1p(-(2.0 ** (-RET_DECAY_OFFSET - jnp.arange(N_HEADS, dtype=jnp.float32))))
    idx = jnp.arange(CHUNK, dtype=jnp.float32)
    rel = idx[:, None] - idx[None, :]
    intra = jnp.exp(jnp.where(rel >= 0, rel[None] * lg[:, None, None], -jnp.inf))
    q_dec = jnp.exp(lg[:, None] * (idx + 1.0))[..., None]
    k_dec = jnp.exp(lg[:, None] * (CHUNK - 1.0 - idx))[..., None]
    c_dec = jnp.exp(lg * CHUNK)[:, None, None]

    def step(state, xs):
        qc, kc, vc = xs
        scores = jnp.einsum('bhtk,bhsk->bhts', qc, kc) * intra
        out = (jnp.einsum('bhts,bhsv->bhtv', scores, vc)
               + jnp.einsum('bhtk,bhkv->bhtv', qc * q_dec, state))
        state = c_dec * state + jnp.einsum('bhsk,bhsv->bhkv', kc * k_dec, vc)
        return state, out

    s0 = jnp.zeros((q.shape[0], N_HEADS, HEAD_K, HEAD_V), jnp.float32)
    _, out = lax.scan(step, s0, (_to_chunks(q), _to_chunks(k), _to_chunks(v)))
    return _from_chunks(out)

def _gated_delta(q, k, v, g, beta):
    tri = jnp.tril(jnp.ones((CHUNK, CHUNK), bool))
    strict = jnp.tril(jnp.ones((CHUNK, CHUNK), bool), k=-1)
    gch = _to_chunks(g[..., None])[..., 0]
    bch = _to_chunks(beta[..., None])[..., 0]

    def step(state, xs):
        qc, kc, vc, gc, bc = xs
        gcum = jnp.cumsum(gc, axis=-1)
        decay = jnp.exp(jnp.where(tri, gcum[..., :, None] - gcum[..., None, :], -jnp.inf))
        kb = kc * bc[..., None]
        a = jnp.where(strict, jnp.einsum('bhtk,bhsk->bhts', kb, kc) * decay, 0.0)
        rhs = jnp.concatenate([vc * bc[..., None], kb * jnp.exp(gcum)[..., None]], axis=-1)
        sol = lax.linalg.triangular_solve(a, rhs, left_side=True, lower=True, unit_diagonal=True)
        u, w = sol[..., :HEAD_V], sol[..., HEAD_V:]
        v_new = u - jnp.einsum('bhtk,bhkv->bhtv', w, state)
        attn = jnp.einsum('bhtk,bhsk->bhts', qc, kc) * decay
        out = (jnp.einsum('bhtk,bhkv->bhtv', qc * jnp.exp(gcum)[..., None], state)
               + jnp.einsum('bhts,bhsv->bhtv', attn, v_new))
        g_last = gcum[..., -1]
        state = (jnp.exp(g_last)[..., None, None] * state
                 + jnp.einsum('bhsk,bhsv->bhkv', kc * jnp.exp(g_last[..., None] - gcum)[..., None], v_new))
        return state, out

    s0 = jnp.zeros((q.shape[0], N_HEADS, HEAD_K, HEAD_V), jnp.float32)
    _, out = lax.scan(step, s0, (_to_chunks(q), _to_chunks(k), _to_chunks(v), gch, bch))
    return _from_chunks(out)

def _hgrn2(q, k, v, log_f):
    tri = jnp.tril(jnp.ones((CHUNK, CHUNK), bool))[:, :, None]

    def step(state, xs):
        qc, kc, vc, lf = xs
        gcum = jnp.cumsum(lf, axis=2)
        diff = gcum[:, :, :, None, :] - gcum[:, :, None, :, :]
        decay = jnp.exp(jnp.where(tri, diff, -jnp.inf))
        attn = jnp.einsum('bhtk,bhsk,bhtsk->bhts', qc, kc, decay)
        out = (jnp.einsum('bhts,bhsv->bhtv', attn, vc)
               + jnp.einsum('bhtk,bhkv->bhtv', qc * jnp.exp(gcum), state))
        g_last = gcum[:, :, -1]
        state = (jnp.exp(g_last)[..., None] * state
                 + jnp.einsum('bhsk,bhsv->bhkv', kc * jnp.exp(g_last[:, :, None] - gcum), vc))
        return state, out

    s0 = jnp.zeros((q.shape[0], N_HEADS, HEAD_K, HEAD_V), jnp.float32)
    _, out = lax.scan(step, s0, (_to_chunks(q), _to_chunks(k), _to_chunks(v), _to_chunks(log_f)))
    return _from_chunks(out)

def _token_mixer(x, positions, w_in, conv_w, a_log, dt_bias, gdn_g, lb, hg_g, merge_b, w_branch, w_out):
    b, s, _ = x.shape
    f32 = jnp.float32
    proj = x @ w_in
    (r_q, r_k, r_v, r_g, g_qkv, g_z, g_b, g_a,
     h_q, h_f, h_i, h_g, m_g) = _split_columns(proj, IN_WIDTHS)

    q = _rotary(_heads(r_q.astype(f32), HEAD_K), positions)
    k = _rotary(_heads(r_k.astype(f32), HEAD_K), positions) * HEAD_K ** -0.5
    o = _head_groupnorm(_retention(q, k, _heads(r_v.astype(f32), HEAD_V)))
    y_ret = jax.nn.silu(r_g.astype(f32)) * o.reshape(b, s, V_WIDTH)

    qkv = jax.nn.silu(_causal_conv(g_qkv, conv_w)).astype(f32)
    q, k, v = _split_columns(qkv, (QK_WIDTH, QK_WIDTH, V_WIDTH))
    q = _l2norm(_heads(q, HEAD_K)) * HEAD_K ** -0.5
    k = _l2norm(_heads(k, HEAD_K))
    beta = jax.nn.sigmoid(g_b.astype(f32))
    g = -jnp.exp(a_log.astype(f32)) * jax.nn.softplus(g_a.astype(f32) + dt_bias.astype(f32))
    o = _head_rms(_gated_delta(q, k, _heads(v, HEAD_V), g, beta), gdn_g)
    y_gdn = jax.nn.silu(g_z.astype(f32)) * o.reshape(b, s, V_WIDTH)

    hf = h_f.astype(f32)
    lb32 = lb.astype(f32)
    log_f = jnp.logaddexp(jax.nn.log_sigmoid(hf), jnp.log(lb32) + jax.nn.log_sigmoid(-hf))
    k = (1.0 - lb32) * jax.nn.sigmoid(-hf)
    o = _hgrn2(_heads(h_q.astype(f32), HEAD_K) * HEAD_K ** -0.5, _heads(k, HEAD_K),
               _heads(h_i.astype(f32), HEAD_V), _heads(log_f, HEAD_K))
    o = _head_rms(o, hg_g)
    y_hg = jax.nn.sigmoid(h_g.astype(f32)) * o.reshape(b, s, V_WIDTH)

    branches = jnp.stack([y_ret, y_gdn, y_hg], axis=2).astype(x.dtype)
    projected = jnp.einsum('bsnv,nvd->bsnd', branches, w_branch)
    gates = jax.nn.sigmoid(m_g + merge_b).reshape(b, s, N_BRANCH, D_MODEL)
    merged = jnp.sum(gates * projected, axis=2)
    return merged @ w_out

def _moe(x, router_w, router_b, w_gate, w_up, w_down):
    b, s, d = x.shape
    t = x.reshape(b * s, d)
    scores = jax.nn.sigmoid(t.astype(jnp.float32) @ router_w.astype(jnp.float32))
    biased = (scores + router_b.astype(jnp.float32)).reshape(-1, N_GROUPS, EXPERTS_PER_GROUP)
    group_score = jnp.sum(lax.top_k(biased, TOP_K)[0], axis=-1)
    best = jnp.argmax(group_score, axis=-1)
    in_group = jnp.take_along_axis(biased, best[:, None, None], axis=1)[:, 0]
    _, local = lax.top_k(in_group, TOP_K)
    idx = best[:, None] * EXPERTS_PER_GROUP + local
    sel = jnp.take_along_axis(scores, idx, axis=-1)
    wts = sel / jnp.sum(sel, axis=-1, keepdims=True)
    combine = jnp.einsum('tk,tke->te', wts, jax.nn.one_hot(idx, N_EXPERTS, dtype=jnp.float32)).astype(x.dtype)
    y = jnp.zeros_like(t)
    for e in range(N_EXPERTS):
        h = jax.nn.silu(t @ w_gate[e]) * (t @ w_up[e])
        y = y + combine[:, e:e + 1] * (h @ w_down[e])
    return y.reshape(b, s, d)

def setup_inputs(seed: int = 0) -> dict:
    key = jax.random.key(seed)
    ks = jax.random.split(key, 24)
    f32 = jnp.float32

    def nrm(k, shape, scale):
        return scale * jax.random.normal(k, shape, f32)

    x = jax.random.normal(ks[0], (BATCH, SEQ, D_MODEL), f32)
    positions = jnp.tile(jnp.arange(SEQ, dtype=jnp.int32)[None, :], (BATCH, 1))
    w_in = nrm(ks[1], (DEPTH, D_MODEL, N_IN), D_MODEL ** -0.5)
    gdn_conv_w = nrm(ks[2], (DEPTH, CONV_K, 2 * QK_WIDTH + V_WIDTH), CONV_K ** -0.5)
    gdn_a_log = jnp.log(jax.random.uniform(ks[3], (DEPTH, N_HEADS), f32, 1.0, 16.0))
    dt = jnp.exp(jax.random.uniform(ks[4], (DEPTH, N_HEADS), f32, math.log(1e-3), math.log(1e-1)))
    gdn_dt_bias = dt + jnp.log(-jnp.expm1(-dt))
    gdn_norm_g = 1.0 + nrm(ks[5], (DEPTH, HEAD_V), 0.02)
    hgrn_lb = nrm(ks[6], (DEPTH, QK_WIDTH), 0.1)
    hgrn_norm_g = 1.0 + nrm(ks[7], (DEPTH, HEAD_V), 0.02)
    merge_b = nrm(ks[8], (DEPTH, N_BRANCH * D_MODEL), 0.02)
    w_branch = nrm(ks[9], (DEPTH, N_BRANCH, V_WIDTH, D_MODEL), BETA * V_WIDTH ** -0.5)
    w_out = nrm(ks[10], (DEPTH, D_MODEL, D_MODEL), BETA * D_MODEL ** -0.5)
    ln1_g = 1.0 + nrm(ks[11], (DEPTH, D_MODEL), 0.02)
    ln1_b = nrm(ks[12], (DEPTH, D_MODEL), 0.02)
    router_w = nrm(ks[13], (D_MODEL, N_EXPERTS), D_MODEL ** -0.5)
    router_b = nrm(ks[14], (N_EXPERTS,), 0.01)
    moe_w_gate = nrm(ks[15], (DEPTH, N_EXPERTS, D_MODEL, D_EXPERT), D_MODEL ** -0.5)
    moe_w_up = nrm(ks[16], (DEPTH, N_EXPERTS, D_MODEL, D_EXPERT), D_MODEL ** -0.5)
    moe_w_down = nrm(ks[17], (DEPTH, N_EXPERTS, D_EXPERT, D_MODEL), BETA * D_EXPERT ** -0.5)
    ln2_g = 1.0 + nrm(ks[18], (DEPTH, D_MODEL), 0.02)
    ln2_b = nrm(ks[19], (DEPTH, D_MODEL), 0.02)
    return {'x': x, 'positions': positions, 'w_in': w_in, 'gdn_conv_w': gdn_conv_w,
            'gdn_a_log': gdn_a_log, 'gdn_dt_bias': gdn_dt_bias, 'gdn_norm_g': gdn_norm_g,
            'hgrn_lb': hgrn_lb, 'hgrn_norm_g': hgrn_norm_g, 'merge_b': merge_b,
            'w_branch': w_branch, 'w_out': w_out, 'ln1_g': ln1_g, 'ln1_b': ln1_b,
            'router_w': router_w, 'router_b': router_b, 'moe_w_gate': moe_w_gate,
            'moe_w_up': moe_w_up, 'moe_w_down': moe_w_down, 'ln2_g': ln2_g, 'ln2_b': ln2_b}

def reference(x, positions, w_in, gdn_conv_w, gdn_a_log, gdn_dt_bias, gdn_norm_g, hgrn_lb,
              hgrn_norm_g, merge_b, w_branch, w_out, ln1_g, ln1_b, router_w, router_b,
              moe_w_gate, moe_w_up, moe_w_down, ln2_g, ln2_b):
    lb_all = jnp.cumsum(jax.nn.softmax(hgrn_lb.astype(jnp.float32), axis=0), axis=0)
    lb_all = lb_all - lb_all[0]
    for l in range(DEPTH):
        h = _token_mixer(x, positions, w_in[l], gdn_conv_w[l], gdn_a_log[l], gdn_dt_bias[l],
                         gdn_norm_g[l], lb_all[l], hgrn_norm_g[l], merge_b[l], w_branch[l], w_out[l])
        x = _layer_norm(ALPHA * x + h, ln1_g[l], ln1_b[l])
        h = _moe(x, router_w, router_b, moe_w_gate[l], moe_w_up[l], moe_w_down[l])
        x = _layer_norm(ALPHA * x + h, ln2_g[l], ln2_b[l])
    return x


_drawn_inputs = setup_inputs


def setup_inputs(seed=0):
    import zlib

    import numpy as np

    out = dict(_drawn_inputs(seed))
    spreads = {}
    factors = {'gdn_norm_g': 2.891, 'hgrn_lb': 3.598, 'hgrn_norm_g': 3.92, 'merge_b': 8.0}
    for name, (base, spread) in spreads.items():
        noise = np.random.default_rng([zlib.crc32(name.encode()), seed]).standard_normal(out[name].shape)
        drawn = base * np.exp(spread * noise) if base else spread * noise
        out[name] = __import__('jax').numpy.asarray(drawn.astype(out[name].dtype))
    for name, factor in factors.items():
        out[name] = (out[name] * factor).astype(out[name].dtype)
    return out
```

```python
from contextlib import ExitStack

import numpy as np
import concourse.bass as bass
from concourse import mybir

F32 = mybir.dt.float32
F32R = mybir.dt.float32r
I32 = mybir.dt.int32
U8 = mybir.dt.uint8
ALU = mybir.AluOpType
ACT = mybir.ActivationFunctionType
AX = mybir.AxisListType

P = 128
D = 1024
T = 256
DEPTH = 2
H = 4
HK = 128
HV = 256
NE = 16
NG = 4
EG = 4
CONV = 4
DX = 512
KD = D // P
TT = T // P
ALPHA = (2 * DEPTH) ** 0.25
KSCALE = HK ** -0.5
LEVELS = 7
TINY = 2.0 ** -60

C_RQ, C_RK, C_RV, C_RG, C_GQKV = 0, 512, 1024, 2048, 3072
C_GZ, C_GB, C_HQ, C_HF, C_HI, C_HG, C_MG = 5120, 6144, 6152, 6664, 7176, 8200, 9224

BLOCKS = ([("in", C_GQKV + 512 * i) for i in range(4)]
          + [("in", C_HQ), ("in", C_HF), ("in", C_RQ), ("in", C_RK)]
          + [("in", C_RV + 512 * i) for i in range(2)] + [("in", C_RG + 512 * i) for i in range(2)]
          + [("in", C_MG), ("br", 0, 0), ("in", C_MG + 512), ("br", 0, 512)]
          + [("in", C_HI + 512 * i) for i in range(2)] + [("in", C_HG + 512 * i) for i in range(2)]
          + [("in", C_MG + 2 * D), ("br", 2, 0), ("in", C_MG + 2 * D + 512), ("br", 2, 512)]
          + [("in", C_MG + D), ("in", C_MG + D + 512)] + [("in", C_GZ + 512 * i) for i in range(2)]
          + [("br", 1, 0), ("br", 1, 512), ("out", 0), ("out", 512)])
NBLK = len(BLOCKS)
MIX_UNITS = 2 * NBLK
EXP_UNITS = 6
PASS_UNITS = EXP_UNITS * NE
LAYER_UNITS = MIX_UNITS + 2 * PASS_UNITS
RAW = 4
SPLIT = 4
CREDIT = 4

CORE = ([("conv_w", "v"), ("ba", "v"), ("gnorm", "a"), ("gvt", "v"), ("gcol", "v"), ("grow", "va"), ("gkt", "v"),
         ("rqkt", "a"), ("h0", "v"), ("rqk", "v"), ("gkk", "v"), ("h1", "v"), ("rout", "v"), ("x0", "a"), ("h2", "v"),
         ("yz0", "v"), ("h3", "v"), ("ryt", "a"), ("x1", "a"), ("h4", "v"), ("yz1", "v"), ("h5", "v"),
         ("x2", "a"), ("h6", "v"), ("yz2", "v"), ("h7", "a"), ("x3", "a"), ("h8", "v"), ("yz3", "v"), ("hout", "va"),
         ("x4", "a"), ("yz4", "v"), ("hyt", "a"), ("x5", "a"), ("yz5", "v"), ("x6", "a"), ("yz6", "v"),
         ("vn0", "a"), ("state", "a"), ("ks", "v"), ("vn1", "a"), ("gout", "va"), ("gyt", "a"), ("mt", "a"),
         ("x1t", "a"), ("router", "v"), ("pos", "v"), ("x2t", "a")])
NCORE = len(CORE)
CORE_AT = {name: i + 1 for i, (name, _) in enumerate(CORE)}
READ_AT = {e: {name: sum(e in who for _, who in CORE[:i + 1]) for i, (name, _) in enumerate(CORE)} for e in "va"}
READS = {e: sum(e in who for _, who in CORE) for e in "va"}

CONST_DMAS = 15
CONSTS = ["c_eye", "c_upper", "c_strict", "c_mask", "c_maskt", "c_eyeb", "c_decay", "c_iota", "c_invf", "c_tie"]


def constants():
    i = np.arange(P)
    rows, cols = i[:, None], i[None, :]
    f = np.float32
    mask = np.zeros((P, LEVELS, P), np.int32)
    for l in range(LEVELS):
        h = 2 ** l
        same = rows // (2 * h) == cols // (2 * h)
        mask[:, l] = same & (rows % (2 * h) >= h) & (cols % (2 * h) < h)
    maskt = np.ascontiguousarray(mask.transpose(2, 1, 0))
    lg = np.log1p(-(2.0 ** (-5.0 - np.arange(H))))
    rel = np.arange(T)[None, None, :] - i[:, None, None]
    decay = np.where(rel >= 0, np.exp(np.maximum(rel, 0) * lg[None, :, None]), 0.0) * KSCALE
    invf = (f(1.0) / (f(10000.0) ** np.linspace(0.0, 1.0, HK // 2, dtype=f))).astype(f)
    tie = np.zeros((P, EG, EG), f)
    tie[:] = np.arange(EG)[None, None, :] < np.arange(EG)[None, :, None]
    return {
        "c_eye": np.eye(P, dtype=f), "c_upper": (rows <= cols).astype(f), "c_strict": (rows < cols).astype(f),
        "c_mask": mask, "c_maskt": maskt, "c_eyeb": np.eye(P, dtype=np.int32),
        "c_decay": decay.astype(f),
        "c_iota": np.broadcast_to(np.arange(2 * P, dtype=f), (P, 2 * P)).copy(),
        "c_invf": np.broadcast_to(invf, (P, HK // 2)).copy(), "c_tie": tie,
    }


def build_decoder(nc, x_in, positions, w_in, conv_w, a_log, dt_bias, gdn_g, hgrn_lb, hgrn_g, merge_b, w_branch,
                  w_out, ln1_g, ln1_b, router_w, router_b, w_gate, w_up, w_down, ln2_g, ln2_b,
                  c_eye, c_upper, c_strict, c_mask, c_maskt, c_eyeb, c_decay, c_iota, c_invf, c_tie, out):
    with ExitStack() as ctx:
        def sb(name, shape, dt=F32, stack=ctx):
            return stack.enter_context(nc.sbuf_tensor(name, shape, dt))

        def sem(name):
            return ctx.enter_context(nc.semaphore(name))

        pb = ctx.enter_context(nc.psum_tensor("pb", [P, 4, 512], F32))
        pc = ctx.enter_context(nc.psum_tensor("pc", [P, 4, 512], F32))

        raw = sb("raw", [P, RAW, 4, 512])
        eye, upper, strict = sb("eye", [P, P]), sb("upper", [P, P]), sb("strict", [P, P])
        ones = sb("ones", [P, P])
        mask, maskt = sb("mask", [P, LEVELS, P], U8), sb("maskt", [P, LEVELS, P], U8)
        eyeb = sb("eyeb", [P, P], U8)
        decay = sb("decay", [P, H, T])
        iota = sb("iota", [P, 2 * P])
        tie = sb("tie", [P, EG, EG])
        cos, sin = sb("cos", [P, TT, 64]), sb("sin", [P, TT, 2, 64])
        eps = sb("eps", [P, 2])
        x = sb("x", [P, TT, D])
        xt = sb("xt", [P, KD, T])
        lng, lnb = sb("lng", [P, D]), sb("lnb", [P, D])
        lb, omlb = sb("lb", [P, DEPTH, H]), sb("omlb", [P, DEPTH, H])
        lbl, omlbl = sb("lbl", [P, H]), sb("omlbl", [P, H])
        rw, rb = sb("rw", [P, KD, NE]), sb("rb", [P, NE])
        stats, mv = sb("stats", [P, 8, 12]), sb("mv", [P, 8, 2])
        rstd = sb("rstd", [P, 8])
        ss = sb("ss", [P, 8])
        flag = sb("flag", [P, 1], I32)

        mix = ExitStack()
        m = lambda name, shape, dt=F32: sb(name, shape, dt, mix)
        convraw, cw = m("convraw", [CONV * 16, P]), m("cw", [P, CONV, 16])
        wba, ba = m("wba", [P, KD, 8]), m("ba", [P, TT, 8])
        alog, dtb = m("alog", [P, H]), m("dtb", [P, H])
        gng, hng = m("gng", [P, HV]), m("hng", [P, HV])
        mbias = m("mbias", [P, 2, 512])
        small = m("small", [P, 8, 8])
        cin = m("cin", [P, 4, CONV - 1 + T])
        gqkv = m("gqkv", [P, 16, T])
        vb = m("vb", [P, TT, D])
        dt_, at, attg = m("dt", [P, 8, P]), m("at", [P, 8, P]), m("attg", [P, 8, P])
        ti, ui, xi = m("ti", [P, 8, P]), m("ui", [P, 8, P]), m("xi", [P, 8, P])
        ke, qe = m("ke", [P, H, P]), m("qe", [P, H, P])
        hq, hk, hg = m("hq", [P, H, T]), m("hk", [P, H, T]), m("hg", [P, H, T])
        he, hf = m("he", [P, H, T]), m("hf", [P, H, T])
        atth, atth2 = m("atth", [P, 8, P]), m("atth2", [P, H, P])
        attr = gqkv[:, 8:12, :]
        attr2 = gqkv[:, 12:14, :].rearrange("p a (b t) -> p (a b) t", b=2)
        kd = gqkv[:, 14:16, :].rearrange("p a (b t) -> p (a b) t", b=2)
        val = m("val", [P, TT, D])
        gt, gate = m("gt", [P, 2, TT, 512]), m("gate", [P, 2, TT, 512])
        y, yt = m("y", [P, TT, D]), m("yt", [P, KD, T])
        merged = m("merged", [P, TT, D])
        rqk = merged
        sq = yt
        state = xi
        mix.close()

        pre = ExitStack()
        m = lambda name, shape, dt=F32: sb(name, shape, dt, pre)
        lbc = m("lbc", [P, DEPTH, H])
        lbr = m("lbr", [DEPTH * H, P])
        lbt = m("lbt", [P, 4, H])
        mask32, maskt32 = m("mask32", [P, LEVELS, P], I32), m("maskt32", [P, LEVELS, P], I32)
        eyeb32 = m("eyeb32", [P, P], I32)
        posi, posf = m("posi", [P, TT], I32), m("posf", [P, TT])
        invf = m("invf", [P, 64])
        ang, turns = m("ang", [P, TT, 64]), m("turns", [P, TT, 64])
        pre.close()

        moe = ExitStack()
        m = lambda name, shape, dt=F32: sb(name, shape, dt, moe)
        whi, wlo = m("whi", [P, SPLIT, 4, 512], F32R), m("wlo", [P, SPLIT, 4, 512], F32R)
        xh, xl = m("xh", [P, TT, D], F32R), m("xl", [P, TT, D], F32R)
        xgh, xgl = m("xgh", [P, 2, KD, P], F32R), m("xgl", [P, 2, KD, P], F32R)
        pick, pickt = m("pick", [P, 2, TT, P], F32R), m("pickt", [P, 2, T], F32R)
        hs = m("hs", [P, DX])
        hth, htl = m("hth", [P, 4, P], F32R), m("htl", [P, 4, P], F32R)
        yh, yl = m("yh", [P, D], F32R), m("yl", [P, D], F32R)
        zero = m("zero", [P, P])
        zeros512 = m("zeros512", [P, 512])
        scores, biased = m("scores", [P, TT, NE]), m("biased", [P, TT, NE])
        cmp, eq = m("cmp", [P, 8, EG, EG]), m("eq", [P, 8, EG, EG])
        rank, best = m("rank", [P, TT, NE]), m("best", [P, TT, NG])
        gsum = m("gsum", [P, TT, NG])
        chosen, wsum = m("chosen", [P, TT, NE]), m("wsum", [P, TT, 2])
        comb, posm = m("comb", [P, TT, NE]), m("posm", [P, TT, NE])
        pcol, ccol = m("pcol", [P, 2, TT]), m("ccol", [P, 2, TT])
        cslot = m("cslot", [P, 2])
        moe.close()

        consts_in = sem("consts_in")
        x_loaded = sem("x_loaded")
        params_in = sem("params_in")
        mbias_in = [sem(f"mbias_in{i}") for i in range(2)]
        ln_in = sem("ln_in")
        raw_in = [sem(f"raw_in{i}") for i in range(RAW)]
        half_done = sem("half_done")
        block_done = [sem(f"block_done{i}") for i in range(2)]
        block_read = [sem(f"block_read{i}") for i in range(2)]
        core_done = sem("core_done")
        core_read = {"v": sem("core_read_v"), "a": sem("core_read_a")}
        setup_v, setup_a, setup_p = sem("setup_v"), sem("setup_a"), sem("setup_p")
        chain_v, chain_a = sem("chain_v"), sem("chain_a")
        names = ["conv_out", "conv_silu", "gates_small", "sq_ready", "qk_normed", "beta_g", "lnexp_gn", "dt_raw", "dt_exp", "gkk_in",
                 "rope_done", "hf_parts", "hf_exp", "hf_den", "hf_lns", "h_diff", "h_exp", "h_fac",
                 "rvar", "rrstd", "y_done", "gate_raw", "gate_out", "rms_rstd", 
                 "merged_ready", "x_ready", "ln_var", "ln_rstd", "xh_ready", "layer_open", "logits", "score_out", "chosen_ready", "moe_ready",
                 "acc_done", "level_t", "ba_raw", "ba_exp"]
        s = {name: sem(name) for name in names}
        split_hi, split_lo, unit_done = sem("split_hi"), sem("split_lo"), sem("unit_done")
        e_names = ["pick_ready", "gh_done", "xgh_ready", "gl_done", "xgl_ready", "silu_h", "h_ready", "turned",
                   "hth_ready", "htl_ready", "pickt_ready", "yh_ready", "yl_ready", "scattered"]
        se = {name: sem(name) for name in e_names}
        flag_ready = sem("flag_ready")
        held = {e: sem(f"held_{e}") for e in ("sp", "pool", "pe", "act", "dve")}
        out_done = sem("out_done")

        mcast = lambda ap, n: ap[:, None, :].to_broadcast([P, n, ap.shape[-1]])

        def unit_source(block, half, lay):
            r = slice(512 * half, 512 * half + 512)
            if block[0] == "in":
                src = w_in[lay, r, block[1]:block[1] + 512]
            elif block[0] == "br":
                src = w_branch[lay, block[1], r, block[2]:block[2] + 512]
            else:
                src = w_out[lay, r, block[1]:block[1] + 512]
            return src.rearrange("(k p) n -> p k n", p=P)

        def expert_source(i, lay, e):
            if i < 4:
                src = (w_gate if i < 2 else w_up)[lay, e, 512 * (i % 2):512 * (i % 2) + 512, :]
            else:
                src = w_down[lay, e, :, 512 * (i - 4):512 * (i - 4) + 512]
            return src.rearrange("(k p) n -> p k n", p=P)

        class Engine:

            def __init__(self, eng, chain, held):
                self.held = held
                self.eng, self.chain, self.n, self.last = eng, chain, 0, None

            def do(self, ins, signal=None, value=None):
                if signal is None:
                    self.n += 1
                    signal, value = self.chain, self.n
                ins.then_inc(signal, 1)
                self.last = (signal, value)

            def settle(self):
                self.eng.wait_ge(*self.last)

            def tell(self, signal):
                self.settle()
                self.eng.sem_inc(signal, 1)

            def restart(self):
                self.settle()
                self.hold()
                self.eng.sem_clear(self.chain)
                self.n = 0

            def hold(self):
                self.eng.sem_inc(self.held, 1)

        block = ctx.enter_context(nc.Block())

        @block.sync
        def _(sp):
            sp.dma_start(x[:, :, :], x_in[0].rearrange("(t p) d -> p t d", p=P)).then_inc(x_loaded, 16)
            sp.sem_inc(split_lo, CREDIT)
            with sp.Fori(0, DEPTH) as lay:
                for u in range(MIX_UNITS):
                    if u < RAW:
                        sp.wait_ge(split_lo, lay * 2 * PASS_UNITS + u + 1)
                    elif u % 2 == 0:
                        sp.wait_ge(half_done, lay * NBLK + (u - RAW) // 2 + 1)
                    else:
                        b = (u - RAW) // 2
                        sp.wait_ge(block_done[b % 2], lay * (NBLK // 2) + b // 2 + 1)
                    sp.sem_inc(held["sp"], 1)
                    sp.dma_start(raw[:, u % RAW], unit_source(BLOCKS[u // 2], u % 2, lay)).then_inc(raw_in[u % RAW], 16)
                sp.wait_ge(half_done, lay * NBLK + NBLK)
                sp.sem_inc(held["sp"], 1)
                for i in range(2):
                    sp.wait_ge(block_done[i], lay * (NBLK // 2) + NBLK // 2)
                sp.sem_inc(held["sp"], 1)

                def stream_pass(p):
                    with sp.Fori(0, NE // 2) as it:
                        for j in range(2):
                            for i in range(EXP_UNITS):
                                c = EXP_UNITS * j + i
                                sp.wait_ge(split_lo, (lay * 2 + p) * PASS_UNITS + it * 2 * EXP_UNITS + c + CREDIT - RAW + 1)
                                sp.sem_inc(held["sp"], 1)
                                sp.dma_start(raw[:, c % RAW], expert_source(i, lay, 2 * it + j)).then_inc(raw_in[c % RAW], 16)

                stream_pass(0)
                sp.wait_ge(flag_ready, lay + 1)
                sp.sem_inc(held["sp"], 1)
                spill = sp.value_load(flag[0:1, 0:1], min_val=0, max_val=1)
                with sp.If(spill > 0):
                    stream_pass(1)
                with sp.Else():
                    for i in range(RAW):
                        sp.wait_ge(raw_in[i], 16 * (lay * (LAYER_UNITS // RAW) + (MIX_UNITS + PASS_UNITS) // RAW))
                        sp.sem_inc(raw_in[i], 16 * PASS_UNITS // RAW)
            sp.wait_ge(s["x_ready"], 2 * DEPTH)
            sp.dma_start(out[0].rearrange("(t p) d -> p t d", p=P), x[:, :, :]).then_inc(out_done, 16)
            sp.wait_ge(out_done, 16)

        @block.gpsimd
        def _(pool):
            for dst, src in ((eye, c_eye), (upper, c_upper), (strict, c_strict), (mask32, c_mask), (maskt32, c_maskt),
                             (eyeb32, c_eyeb), (decay, c_decay), (iota, c_iota), (invf, c_invf), (tie, c_tie)):
                pool.dma_start(dst[:], src).then_inc(consts_in, 16)
            for t in range(TT):
                pool.dma_start(posi[:, t:t + 1], positions[0, t * P:(t + 1) * P][:, None]).then_inc(consts_in, 16)
            pool.dma_start(lbr[:], hgrn_lb.rearrange("l (h p) -> (l h) p", p=P)).then_inc(consts_in, 16)
            pool.dma_start(rw[:], router_w.rearrange("(k p) e -> p k e", p=P)).then_inc(consts_in, 16)
            pool.dma_start(rb[:], router_b[None, :].partition_broadcast(P)).then_inc(consts_in, 16)
            with pool.Fori(0, DEPTH) as lay:
                pool.wait_ge(setup_v, 1)
                pool.wait_ge(s["acc_done"], lay + 1)
                pool.wait_ge(s["layer_open"], lay + 1)
                pool.sem_inc(held["pool"], 1)
                pool.dma_start(convraw[:], conv_w[lay].rearrange("j (c p) -> (j c) p", p=P)).then_inc(params_in, 16)
                pool.dma_start(wba[:], w_in[lay, :, C_GB:C_GB + 8].rearrange("(k p) n -> p k n", p=P)).then_inc(params_in, 16)
                pool.dma_start(alog[:], a_log[lay][None, :].partition_broadcast(P)).then_inc(params_in, 16)
                pool.dma_start(dtb[:], dt_bias[lay][None, :].partition_broadcast(P)).then_inc(params_in, 16)
                pool.dma_start(gng[:], gdn_g[lay][None, :].partition_broadcast(P)).then_inc(params_in, 16)
                pool.dma_start(hng[:], hgrn_g[lay][None, :].partition_broadcast(P)).then_inc(params_in, 16)
                pool.dma_start(lng[:], ln1_g[lay][None, :].partition_broadcast(P)).then_inc(ln_in, 16)
                pool.dma_start(lnb[:], ln1_b[lay][None, :].partition_broadcast(P)).then_inc(ln_in, 16)
                for i, base in enumerate((0, 512, 2 * D, 2 * D + 512, D, D + 512)):
                    if i >= 2:
                        pool.wait_ge(s["gate_raw"], lay * 6 + i - 1)
                        pool.sem_inc(held["pool"], 1)
                    pool.dma_start(mbias[:, i % 2, :], merge_b[lay, base:base + 512][None, :].partition_broadcast(P)).then_inc(mbias_in[i % 2], 16)
                pool.wait_ge(s["x_ready"], 2 * lay + 1)
                pool.sem_inc(held["pool"], 1)
                pool.dma_start(lng[:], ln2_g[lay][None, :].partition_broadcast(P)).then_inc(ln_in, 16)
                pool.dma_start(lnb[:], ln2_b[lay][None, :].partition_broadcast(P)).then_inc(ln_in, 16)

        @block.tensor
        def _(pe):
            mm = nc.tensor.matmul

            def turn(dst, src, n=P):
                return nc.tensor.transpose(dst, src, eye[0:n, 0:n])

            def turn16(src):
                for v in range(KD):
                    for t in range(TT):
                        last = turn(pc[:, v // 2, (v % 2) * T + t * P:(v % 2) * T + t * P + P], src[:, t, v * P:(v + 1) * P])
                return last

            pe.wait_ge(consts_in, 16 * CONST_DMAS)
            pe.wait_ge(x_loaded, 16)
            for i in range(2):
                pe.sem_inc(block_read[i], 1)
            pe.sem_inc(unit_done, CREDIT)
            turn(pc[:, 0, 0:DEPTH * H], lbr[:, :], DEPTH * H).then_inc(setup_p, 1)
            pe.wait_ge(setup_a, 1)
            turn16(x).then_inc(setup_p, 1)

            with pe.Fori(0, DEPTH) as lay:
                def core(name):
                    i = CORE_AT[name] - 1
                    for e in "va":
                        if i and e in "".join(w for _, w in CORE[:i]):
                            pe.wait_ge(core_read[e], lay * READS[e] + READ_AT[e][CORE[i - 1][0]])

                def need(name, k=1, per=1):
                    pe.wait_ge(s[name], lay * per + k)

                def project(b, lhs, rows=True):
                    pair = b % 2
                    pe.wait_ge(block_read[pair], lay * (NBLK // 2) + b // 2 + 1)
                    for half in range(2):
                        u = 2 * b + half
                        pe.wait_ge(raw_in[u % RAW], 16 * (lay * (LAYER_UNITS // RAW) + u // RAW + 1))
                        w = raw[:, u % RAW]
                        if rows:
                            for t in range(TT):
                                for k in range(4):
                                    kk = 4 * half + k
                                    last = mm(pb[:, 2 * pair + t, :], lhs[:, kk, t * P:(t + 1) * P], w[:, k, :],
                                              start=(kk == 0), stop=(kk == KD - 1))
                        else:
                            for k in range(4):
                                kk = 4 * half + k
                                for c in range(4):
                                    last = mm(pb[:, 2 * pair + c // 2, (c % 2) * T:(c % 2) * T + T],
                                              w[:, k, c * P:(c + 1) * P], lhs[:, kk, :],
                                              start=(kk == 0 and c % 2 == 0), stop=(kk == KD - 1), skip_group_check=True)
                        last.then_inc(half_done if half == 0 else block_done[pair], 1)

                def h_level(l):
                    core(f"h{l}")
                    need("h_fac", l + 1, 9)
                    if l == 7:
                        for h in range(H):
                            last = mm(pc[:, 2, h * P:(h + 1) * P], hf[:, h, 0:P], hf[:, h, P:T], start=True, stop=True)
                    else:
                        for t in range(TT):
                            for h in range(H):
                                a = (hk if l == 8 else hf)[:, h, t * P:(t + 1) * P]
                                bb = (hq if l == 8 else hf)[:, h, t * P:(t + 1) * P]
                                last = mm(pc[:, 2 + t, h * P:(h + 1) * P], a, bb, start=True, stop=True)
                    last.then_inc(core_done, 1)

                def inverse_x(l):
                    core(f"x{l}")
                    if l == 0:
                        need("gkk_in")
                    else:
                        need("level_t", l, LEVELS)
                    for i in range(8):
                        last = mm(pc[:, i // 4, (i % 4) * P:(i % 4) * P + P], at[:, i, :], ti[:, i, :], start=True, stop=True)
                    last.then_inc(core_done, 1)

                def inverse_yz(l):
                    core(f"yz{l}")
                    for i in range(8):
                        if l < LEVELS - 1:
                            mm(pc[:, i // 4, (i % 4) * P:(i % 4) * P + P], ui[:, i, :], xi[:, i, :], start=True, stop=True)
                        last = mm(pc[:, 2 + i // 4, (i % 4) * P:(i % 4) * P + P], xi[:, i, :], ui[:, i, :], start=True, stop=True)
                    last.then_inc(core_done, 1)

                pe.wait_ge(setup_a, 2)
                pe.wait_ge(s["acc_done"], lay + 1)
                core("conv_w")
                pe.wait_ge(params_in, 96 * lay + 96)
                pe.wait_ge(s["layer_open"], lay + 1)
                pe.sem_inc(held["pe"], 1)
                turn(pc[:, 0, 0:64], convraw[:, :], 64).then_inc(core_done, 1)
                for b in range(4):
                    project(b, xt, rows=False)
                core("ba")
                for t in range(TT):
                    for k in range(KD):
                        last = mm(pc[:, 0, t * 8:t * 8 + 8], xt[:, k, t * P:(t + 1) * P], wba[:, k, :],
                                  start=(t == 0 and k == 0), stop=(k == KD - 1), skip_group_check=True)
                last.then_inc(core_done, 1)
                project(4, xt, rows=False)
                core("gnorm")
                need("sq_ready")
                for j in range(4):
                    last = mm(pc[:, j, :], ones[:, :], sq[:, 2 * j:2 * j + 2, :], start=True, stop=True)
                last.then_inc(core_done, 1)
                project(5, xt, rows=False)
                core("gvt")
                need("conv_silu", 4, 4)
                for c in range(8):
                    for t in range(TT):
                        last = turn(pc[:, 2 * t + c // 4, (c % 4) * P:(c % 4) * P + P], gqkv[:, 8 + c, t * P:(t + 1) * P])
                last.then_inc(core_done, 1)
                project(6, xt)
                core("gcol")
                need("beta_g")
                mm(pc[:, 0, 0:8], upper[:, :], small[:, 0, :], start=True, stop=True).then_inc(core_done, 1)
                core("grow")
                for i in range(8):
                    mm(pc[:, i // 4, (i % 4) * P:(i % 4) * P + P], small[:, 0, i:i + 1].to_broadcast([P, P]), upper[:, :],
                       start=True, stop=True)
                for i in range(8):
                    last = mm(pc[:, 2 + i // 4, (i % 4) * P:(i % 4) * P + P], small[:, 1, i:i + 1].to_broadcast([P, P]), eye[:, :],
                              start=True, stop=True)
                last.then_inc(core_done, 1)
                project(7, xt)
                core("gkt")
                need("qk_normed")
                for h in range(H):
                    last = turn(pc[:, 0, h * P:(h + 1) * P], gqkv[:, 4 + h, 0:P])
                last.then_inc(core_done, 1)
                project(8, xt)
                core("rqkt")
                need("rope_done", 2, 2)
                turn16(rqk).then_inc(core_done, 1)
                h_level(0)
                project(9, xt)
                core("rqk")
                for h in range(H):
                    mm(pc[:, h // 2, (h % 2) * T:(h % 2) * T + T], yt[:, 4 + h, 0:P], yt[:, h, :], start=True, stop=True)
                for h in range(H):
                    last = mm(pc[:, 2, h * P:(h + 1) * P], yt[:, 4 + h, P:T], yt[:, h, P:T], start=True, stop=True)
                last.then_inc(core_done, 1)
                core("gkk")
                for i in range(8):
                    h, t = i % 4, i // 4
                    kt = gqkv[:, 4 + h, t * P:(t + 1) * P]
                    mm(pc[:, t, h * P:(h + 1) * P], kt, kt, start=True, stop=True)
                    last = mm(pc[:, 2 + t, h * P:(h + 1) * P], kt, gqkv[:, h, t * P:(t + 1) * P], start=True, stop=True)
                last.then_inc(core_done, 1)
                h_level(1)
                project(10, xt)

                def attend(name, same, across, v_ready):
                    core(name)
                    for b in v_ready:
                        pe.wait_ge(block_read[b % 2], lay * (NBLK // 2) + b // 2 + 2)
                    for h in range(H):
                        mm(pc[:, h // 2, (h % 2) * HV:(h % 2) * HV + HV], same(h, 0), val[:, 0, h * HV:(h + 1) * HV],
                           start=True, stop=True)
                    for h in range(H):
                        o = pc[:, 2 + h // 2, (h % 2) * HV:(h % 2) * HV + HV]
                        mm(o, across(h), val[:, 0, h * HV:(h + 1) * HV], start=True, stop=False)
                        last = mm(o, same(h, 1), val[:, 1, h * HV:(h + 1) * HV], start=False, stop=True)
                    last.then_inc(core_done, 1)

                attend("rout", lambda h, t: attr[:, h, 0:P] if t == 0 else attr2[:, h, :],
                       lambda h: attr[:, h, P:T], (8, 9))
                inverse_x(0)
                h_level(2)
                project(11, xt)
                inverse_yz(0)
                h_level(3)
                project(12, xt)
                core("ryt")
                need("y_done", 1, 3)
                turn16(y).then_inc(core_done, 1)
                inverse_x(1)
                h_level(4)
                pe.wait_ge(core_read["a"], lay * READS["a"] + READ_AT["a"]["ryt"])
                project(13, yt)
                inverse_yz(1)
                h_level(5)
                project(14, xt)
                inverse_x(2)
                h_level(6)
                project(15, yt)
                inverse_yz(2)
                h_level(7)
                project(16, xt)
                inverse_x(3)
                h_level(8)
                project(17, xt)
                inverse_yz(3)
                attend("hout", lambda h, t: atth[:, 4 * t + h, :], lambda h: atth2[:, h, :], (16, 17))
                project(18, xt)
                inverse_x(4)
                project(19, xt)
                inverse_yz(4)
                project(20, xt)
                core("hyt")
                need("y_done", 2, 3)
                turn16(y).then_inc(core_done, 1)
                inverse_x(5)
                pe.wait_ge(core_read["a"], lay * READS["a"] + READ_AT["a"]["hyt"])
                project(21, yt)
                inverse_yz(5)
                project(22, xt)
                inverse_x(6)
                project(23, yt)
                inverse_yz(6)
                project(24, xt)
                core("vn0")
                need("level_t", LEVELS, LEVELS)
                for h in range(H):
                    last = mm(pc[:, h // 2, (h % 2) * HV:(h % 2) * HV + HV], ui[:, h, :], vb[:, 0, h * HV:(h + 1) * HV],
                              start=True, stop=True)
                last.then_inc(core_done, 1)
                project(25, xt)
                core("state")
                for h in range(H):
                    last = mm(pc[:, h // 2, (h % 2) * HV:(h % 2) * HV + HV], kd[:, h, :], vb[:, 0, h * HV:(h + 1) * HV],
                              start=True, stop=True)
                last.then_inc(core_done, 1)
                project(26, xt)
                core("ks")
                for h in range(H):
                    last = mm(pc[:, h // 2, (h % 2) * HV:(h % 2) * HV + HV], ke[:, h, :], state[:, 2 * h:2 * h + 2, :],
                              start=True, stop=True)
                last.then_inc(core_done, 1)
                project(27, xt)
                core("vn1")
                for h in range(H):
                    last = mm(pc[:, h // 2, (h % 2) * HV:(h % 2) * HV + HV], ui[:, 4 + h, :], vb[:, 1, h * HV:(h + 1) * HV],
                              start=True, stop=True)
                last.then_inc(core_done, 1)
                core("gout")
                for h in range(H):
                    mm(pc[:, h // 2, (h % 2) * HV:(h % 2) * HV + HV], attg[:, h, :], vb[:, 0, h * HV:(h + 1) * HV],
                       start=True, stop=True)
                for h in range(H):
                    o = pc[:, 2 + h // 2, (h % 2) * HV:(h % 2) * HV + HV]
                    mm(o, qe[:, h, :], state[:, 2 * h:2 * h + 2, :], start=True, stop=False)
                    last = mm(o, attg[:, 4 + h, :], vb[:, 1, h * HV:(h + 1) * HV], start=False, stop=True)
                last.then_inc(core_done, 1)
                core("gyt")
                need("y_done", 3, 3)
                turn16(y).then_inc(core_done, 1)
                pe.wait_ge(core_read["a"], lay * READS["a"] + READ_AT["a"]["gyt"])
                project(28, yt)
                project(29, yt)
                core("mt")
                need("merged_ready", 6, 6)
                turn16(merged).then_inc(core_done, 1)
                pe.wait_ge(core_read["a"], lay * READS["a"] + READ_AT["a"]["mt"])
                project(30, yt)
                project(31, yt)
                core("x1t")
                need("x_ready", 1, 2)
                turn16(x).then_inc(core_done, 1)
                core("router")
                for t in range(TT):
                    for k in range(KD):
                        last = mm(pc[:, 0, t * NE:(t + 1) * NE], xt[:, k, t * P:(t + 1) * P], rw[:, k, :],
                                  start=(t == 0 and k == 0), stop=(k == KD - 1), skip_group_check=True)
                last.then_inc(core_done, 1)
                core("pos")
                need("chosen_ready")
                mm(pc[:, 0, 0:NE], strict[:, :], chosen[:, 0, :], start=True, stop=True)
                mm(pc[:, 0, NE:2 * NE], ones[:, :], chosen[:, 0, :], start=True, stop=False)
                mm(pc[:, 0, NE:2 * NE], strict[:, :], chosen[:, 1, :], start=False, stop=True)
                mm(pc[:, 0, 2 * NE:3 * NE], ones[:, :], chosen[:, 0, :], start=True, stop=False)
                mm(pc[:, 0, 2 * NE:3 * NE], ones[:, :], chosen[:, 1, :], start=False, stop=True).then_inc(core_done, 1)
                need("moe_ready")
                pe.wait_ge(core_read["v"], lay * READS["v"] + READ_AT["v"]["pos"])
                for i in range(4):
                    mm(pb[:, i, :], zero[:, :], zeros512[:, :], start=True, stop=False, skip_group_check=True)

                def expert_pass(p):
                    def gather(part, n, j):
                        for k in range(KD):
                            for t in range(TT):
                                last = mm(pc[:, 2 + k // 4, (k % 4) * P:(k % 4) * P + P], part[:, t, k * P:(k + 1) * P],
                                          pick[:, j, t, :], start=(t == 0), stop=(t == TT - 1))
                        return last

                    def gather_hi(n, j):
                        pe.wait_ge(se["pick_ready"], n + 1)
                        gather(xh, n, j).then_inc(se["gh_done"], 1)

                    def gather_lo(n, j):
                        pe.wait_ge(se["xgh_ready"], n + 1)
                        gather(xl, n, j).then_inc(se["gl_done"], 1)

                    def passes(dst, ah, al, c, base, first, last_):
                        pe.wait_ge(split_lo, base + c + 1 + CREDIT)
                        for k in range(4):
                            mm(dst, ah(k), whi[:, c % SPLIT, k, :], start=(first and k == 0), stop=False)
                            mm(dst, ah(k), wlo[:, c % SPLIT, k, :], start=False, stop=False)
                            ins = mm(dst, al(k), whi[:, c % SPLIT, k, :], start=False, stop=(last_ and k == 3))
                        ins.then_inc(unit_done, 1)

                    def scatter(n, j):
                        pe.wait_ge(se["yl_ready"], n + 1)
                        pe.wait_ge(se["pickt_ready"], n + 1)
                        for t in range(TT):
                            for cb in range(2):
                                for part in (yh, yl):
                                    last = mm(pb[:, 2 * t + cb, :], pickt[:, j, t * P:(t + 1) * P],
                                              part[:, cb * 512:(cb + 1) * 512], start=False, stop=False, skip_group_check=True)
                        last.then_inc(se["scattered"], 1)

                    def expert(n, base, j, first, last_):
                        g = EXP_UNITS * j
                        pe.wait_ge(se["xgl_ready"], n + 1)
                        if not first:
                            pe.wait_ge(se["hth_ready"], n)
                            pe.wait_ge(se["htl_ready"], n)
                        for i in range(2):
                            passes(pc[:, 0, :], lambda k: xgh[:, j, 4 * i + k, :], lambda k: xgl[:, j, 4 * i + k, :],
                                   g + i, base, i == 0, i == 1)
                        if not first:
                            pe.wait_ge(se["pickt_ready"], n)
                        for i in range(2):
                            passes(pc[:, 1, :], lambda k: xgh[:, j, 4 * i + k, :], lambda k: xgl[:, j, 4 * i + k, :],
                                   g + 2 + i, base, i == 0, i == 1)
                        if not last_:
                            if not first:
                                pe.wait_ge(se["yh_ready"], n)
                                pe.wait_ge(se["yl_ready"], n)
                            gather_hi(n + 1, 1 - j)
                        pe.wait_ge(se["h_ready"], n + 1)
                        for f in range(4):
                            turn(pc[:, 0, f * P:(f + 1) * P], hs[:, f * P:(f + 1) * P])
                        for t in range(TT):
                            turn(pc[:, 1, t * P:(t + 1) * P], pick[:, j, t, :].bitcast(F32))
                        for t in range(TT):
                            ins = mm(pc[:, 1, T:T + 1], pick[:, j, t, :].bitcast(F32), ccol[:, j, t:t + 1],
                                     start=(t == 0), stop=(t == TT - 1))
                        ins.then_inc(se["turned"], 1)
                        if not last_:
                            gather_lo(n + 1, 1 - j)
                        if not first:
                            scatter(n - 1, 1 - j)
                        pe.wait_ge(se["htl_ready"], n + 1)
                        if not last_:
                            pe.wait_ge(se["xgl_ready"], n + 2)
                        for i in range(2):
                            passes(pc[:, 2 + i, :], lambda k: hth[:, k, :], lambda k: htl[:, k, :], g + 4 + i, base, True, True)

                    n0 = (lay * 2 + p) * NE
                    u0 = (lay * 2 + p) * PASS_UNITS
                    gather_hi(n0, 0)
                    gather_lo(n0, 0)
                    expert(n0, u0, 0, True, False)
                    expert(n0 + 1, u0, 1, False, False)
                    with pe.Fori(1, NE // 2 - 1) as it:
                        for j in range(2):
                            expert(n0 + it * 2 + j, u0 + it * 2 * EXP_UNITS, j, False, False)
                    expert(n0 + NE - 2, u0 + (NE - 2) * EXP_UNITS, 0, False, False)
                    expert(n0 + NE - 1, u0 + (NE - 2) * EXP_UNITS, 1, False, True)
                    scatter(n0 + NE - 1, 1)

                expert_pass(0)
                pe.wait_ge(flag_ready, lay + 1)
                pe.sem_inc(held["pe"], 1)
                spill = pe.value_load(flag[0:1, 0:1], min_val=0, max_val=1)
                with pe.If(spill > 0):
                    expert_pass(1)
                with pe.Else():
                    pe.wait_ge(se["scattered"], (lay * 2 + 1) * NE)
                    for name in ("gh_done", "gl_done", "turned", "scattered"):
                        pe.sem_inc(se[name], NE)
                    pe.sem_inc(unit_done, PASS_UNITS)
                for i in range(4):
                    ins = mm(pb[:, i, :], zero[:, :], zeros512[:, :], start=False, stop=True, skip_group_check=True)
                ins.then_inc(s["acc_done"], 1)
                core("x2t")
                need("x_ready", 2, 2)
                turn16(x).then_inc(core_done, 1)
                pe.wait_ge(core_read["a"], lay * READS["a"] + READS["a"])

        @block.scalar
        def _(act):
            A = Engine(act, chain_a, held["act"])
            fn = nc.scalar.activation

            act.wait_ge(setup_p, 1)
            fn(lbc[:].rearrange("p l h -> p (l h)"), pc[:, 0, 0:DEPTH * H], ACT.Copy).then_inc(setup_a, 1)
            act.wait_ge(setup_p, 2)
            fn(xt[:].rearrange("p k t -> p (k t)"), pc[:].rearrange("p b n -> p (b n)"), ACT.Copy).then_inc(setup_a, 1)
            act.wait_ge(setup_v, 2)
            fn(lbt[:, 0:DEPTH, :], lbt[:, 0:DEPTH, :], ACT.Exp).then_inc(setup_a, 1)
            act.wait_ge(setup_v, 4)
            fn(cos[:], cos[:], ACT.Sin)
            fn(sin[:, :, 1, :], sin[:, :, 1, :], ACT.Sin).then_inc(setup_a, 1)

            with act.Fori(0, DEPTH) as lay:
                def need(name, k=1, per=1):
                    act.wait_ge(s[name], lay * per + k)

                def give(ins, name, k=1, per=1):
                    A.do(ins, s[name], lay * per + k)

                def core(name):
                    act.wait_ge(core_done, lay * NCORE + CORE_AT[name])

                def read(ins, name):
                    A.do(ins, core_read["a"], lay * READS["a"] + READ_AT["a"][name])

                def block_in(b):
                    act.wait_ge(block_done[b % 2], lay * (NBLK // 2) + b // 2 + 1)
                    return pb[:, 2 * (b % 2):2 * (b % 2) + 2, :]

                def block_out(ins, b):
                    A.do(ins, block_read[b % 2], lay * (NBLK // 2) + b // 2 + 2)

                def whole(dst, name):
                    core(name)
                    read(fn(dst[:].rearrange("p k t -> p (k t)"), pc[:].rearrange("p b n -> p (b n)"), ACT.Copy), name)

                def two(name):
                    core(name)
                    return pc[:, 0:2, :].rearrange("p b n -> p (b n)")

                act.wait_ge(setup_v, 5)
                act.wait_ge(s["acc_done"], lay + 1)
                for b in range(4):
                    src = block_in(b).rearrange("p b (c t) -> p (b c) t", c=2)
                    if b:
                        need("conv_out", b, 4)
                    block_out(fn(cin[:, :, CONV - 1:], src, ACT.Copy), b)
                    need("conv_out", b + 1, 4)
                    g = gqkv[:, 4 * b:4 * b + 4, :]
                    give(fn(g, g, ACT.Silu), "conv_silu", b + 1, 4)
                need("ba_raw")
                A.do(fn(small[:, 2, :], small[:, 2, :], ACT.Exp, scale=-1.0))
                A.do(fn(small[:, 4, :], small[:, 3, :], ACT.Abs))
                A.settle()
                A.do(fn(small[:, 4, :], small[:, 4, :], ACT.Exp, scale=-1.0))
                A.settle()
                A.do(fn(small[:, 4, :], small[:, 4, :], ACT.Ln, bias=1.0))
                give(fn(small[:, 5, 0:H], alog[:, :], ACT.Exp), "ba_exp")
                block_out(fn(hq[:].rearrange("p h t -> p (h t)"), block_in(4).rearrange("p b n -> p (b n)"), ACT.Copy, scale=KSCALE), 4)
                core("gnorm")
                read(fn(sq[:].rearrange("p k t -> p (k t)"), pc[:].rearrange("p b n -> p (b n)"), ACT.Ln, bias=eps[:, 0:1]), "gnorm")
                A.settle()
                give(fn(sq[:], sq[:], ACT.Exp, scale=-0.5), "lnexp_gn")
                need("hf_parts")
                A.do(fn(hg[:], hg[:], ACT.Exp))
                give(fn(he[:], he[:], ACT.Exp, scale=-1.0), "hf_exp")
                need("hf_den")
                A.do(fn(hg[:], hg[:], ACT.Ln))
                A.do(fn(hf[:], hf[:], ACT.Ln, bias=1.0))
                A.settle()
                give(fn(hk[:], hf[:], ACT.Exp, scale=-1.0), "hf_lns")
                core("grow")
                read(fn(kd.rearrange("p h t -> p (h t)"), pc[:, 1, :], ACT.Exp), "grow")
                need("dt_raw")
                give(fn(dt_[:], dt_[:], ACT.Exp), "dt_exp")

                def h_exp(l):
                    need("h_diff", l + 1, 8)
                    give(fn(he[:], he[:], ACT.Exp), "h_exp", l + 1, 8)

                def value_block(b, k):
                    for t in range(TT):
                        src = pb[:, 2 * (b % 2) + t, :]
                        if t == 0:
                            block_in(b)
                            act.wait_ge(core_done, lay * NCORE + CORE_AT["rout"]) if k >= 2 else None
                            fn(val[:, t, (k % 2) * 512:(k % 2) * 512 + 512], src, ACT.Copy)
                        else:
                            A.do(fn(val[:, t, (k % 2) * 512:(k % 2) * 512 + 512], src, ACT.Copy), block_read[b % 2],
                                 lay * (NBLK // 2) + b // 2 + 2)

                def inverse_x(l):
                    src = two(f"x{l}")
                    read(fn(xi[:].rearrange("p i t -> p (i t)"), src, ACT.Copy), f"x{l}")

                def activate(b, k, func, i):
                    src = block_in(b)
                    if i >= 2:
                        need("y_done", i // 2, 3)
                        need("merged_ready", i // 2 * 2, 6)
                    block_out(fn(gt[:, k, :, :], src, func), b)

                def gate_sigmoid(i):
                    need("gate_raw", i + 1, 6)
                    g = gate[:, i % 2, :, :]
                    give(fn(g, g, ACT.Sigmoid), "gate_out", i + 1, 6)

                def rms(name):
                    core(name)
                    for i in range(8):
                        src = pc[:, 2 * (i // 4) + (i % 4) // 2, (i % 2) * HV:(i % 2) * HV + HV]
                        ins = fn(y[:, i // 4, (i % 4) * HV:(i % 4) * HV + HV], src, ACT.Square, accum_out=ss[:, i:i + 1])
                    read(ins, name)
                    A.settle()
                    A.do(fn(ss[:, :], ss[:, :], ACT.Ln, scale=1.0 / HV, bias=eps[:, 0:1]))
                    A.settle()

                whole(yt, "rqkt")
                h_exp(0)
                value_block(8, 0)
                value_block(9, 1)
                h_exp(1)
                activate(10, 0, ACT.Silu, 0)
                h_exp(2)
                need("rvar")
                A.do(fn(rstd[:, :], rstd[:, :], ACT.Ln, bias=eps[:, 0:1]))
                A.settle()
                give(fn(rstd[:, :], rstd[:, :], ACT.Exp, scale=-0.5), "rrstd")
                inverse_x(0)
                activate(11, 1, ACT.Silu, 1)
                h_exp(3)
                h_exp(4)
                gate_sigmoid(0)
                whole(yt, "ryt")
                inverse_x(1)
                h_exp(5)
                h_exp(6)
                gate_sigmoid(1)
                inverse_x(2)
                h_exp(7)
                core("h7")
                read(fn(atth2[:].rearrange("p h t -> p (h t)"), pc[:, 2, :], ACT.Copy), "h7")
                inverse_x(3)
                value_block(16, 2)
                value_block(17, 3)
                activate(18, 0, ACT.Sigmoid, 2)
                rms("hout")
                give(fn(rstd[:, :], ss[:, :], ACT.Exp, scale=-0.5), "rms_rstd", 1, 2)
                inverse_x(4)
                activate(19, 1, ACT.Sigmoid, 3)
                gate_sigmoid(2)
                whole(yt, "hyt")
                inverse_x(5)
                gate_sigmoid(3)
                inverse_x(6)
                gate_sigmoid(4)
                read(fn(vb[:, 0, :], two("vn0"), ACT.Copy), "vn0")
                gate_sigmoid(5)
                read(fn(state[:].rearrange("p i t -> p (i t)"), two("state"), ACT.Copy), "state")
                activate(26, 0, ACT.Silu, 4)
                activate(27, 1, ACT.Silu, 5)
                read(fn(vb[:, 1, :], two("vn1"), ACT.Copy), "vn1")
                rms("gout")
                give(fn(rstd[:, :], ss[:, :], ACT.Exp, scale=-0.5), "rms_rstd", 2, 2)
                whole(yt, "gyt")
                whole(yt, "mt")

                def norm_scale(k):
                    need("ln_var", k, 2)
                    A.do(fn(rstd[:, 0:2], rstd[:, 0:2], ACT.Ln, bias=eps[:, 1:2]))
                    A.settle()
                    A.do(fn(rstd[:, 0:2], rstd[:, 0:2], ACT.Exp, scale=-0.5), s["ln_rstd"], lay * 2 + k)

                norm_scale(1)
                whole(xt, "x1t")
                need("x_ready", 1, 2)
                give(fn(xh[:], x[:], ACT.Copy), "xh_ready")
                need("logits")
                give(fn(scores[:], scores[:], ACT.Sigmoid), "score_out")

                def expert_pass(p):
                    def hi(c, base, raw_base):
                        act.wait_ge(raw_in[c % RAW], raw_base + 16 * (c // RAW) + 16)
                        act.wait_ge(unit_done, base + c + 1)
                        A.do(fn(whi[:, c % SPLIT], raw[:, c % RAW], ACT.Copy), split_hi, base + c + 1)

                    def gathered(n, j):
                        act.wait_ge(se["gh_done"], n + 1)
                        A.do(fn(xgh[:, j].rearrange("p k t -> p (k t)"), pc[:, 2:4, :].rearrange("p b n -> p (b n)"), ACT.Copy),
                             se["xgh_ready"], n + 1)

                    def expert(n, base, raw_base, j, last_):
                        g = EXP_UNITS * j
                        hi(g + 4, base, raw_base)
                        hi(g + 5, base, raw_base)
                        act.wait_ge(unit_done, base + g + 2 + CREDIT)
                        A.do(fn(hs[:, :], pc[:, 0, :], ACT.Silu), se["silu_h"], n + 1)
                        if not last_:
                            gathered(n + 1, 1 - j)
                        act.wait_ge(se["turned"], n + 1)
                        A.do(fn(hth[:].rearrange("p k t -> p (k t)"), pc[:, 0, :], ACT.Copy), se["hth_ready"], n + 1)
                        if not last_:
                            hi(g + 6, base, raw_base)
                            hi(g + 7, base, raw_base)
                        act.wait_ge(unit_done, base + g + 6 + CREDIT)
                        act.wait_ge(se["pickt_ready"], n + 1)
                        A.do(fn(yh[:, :], pc[:, 2:4, :].rearrange("p b n -> p (b n)"), ACT.Copy, scale=cslot[:, j:j + 1]),
                             se["yh_ready"], n + 1)
                        if not last_:
                            hi(g + 8, base, raw_base)
                            hi(g + 9, base, raw_base)

                    n0 = (lay * 2 + p) * NE
                    u0 = (lay * 2 + p) * PASS_UNITS
                    r0 = (lay * (LAYER_UNITS // RAW) + (MIX_UNITS + p * PASS_UNITS) // RAW) * 16
                    for c in range(4):
                        hi(c, u0, r0)
                    gathered(n0, 0)
                    with act.Fori(0, NE // 2 - 1) as it:
                        for j in range(2):
                            expert(n0 + it * 2 + j, u0 + it * 2 * EXP_UNITS, r0 + it * (32 * EXP_UNITS // RAW), j, False)
                    expert(n0 + NE - 2, u0 + (NE - 2) * EXP_UNITS, r0 + (NE - 2) * EXP_UNITS // RAW * 16, 0, False)
                    expert(n0 + NE - 1, u0 + (NE - 2) * EXP_UNITS, r0 + (NE - 2) * EXP_UNITS // RAW * 16, 1, True)

                expert_pass(0)
                act.wait_ge(flag_ready, lay + 1)
                act.sem_inc(held["act"], 1)
                spill = act.value_load(flag[0:1, 0:1], min_val=0, max_val=1)
                with act.If(spill > 0):
                    expert_pass(1)
                with act.Else():
                    act.wait_ge(se["yh_ready"], (lay * 2 + 1) * NE)
                    act.sem_inc(split_hi, PASS_UNITS)
                    for name in ("xgh_ready", "silu_h", "hth_ready", "yh_ready"):
                        act.sem_inc(se[name], NE)
                norm_scale(2)
                whole(xt, "x2t")
                A.restart()

        @block.vector
        def _(dve):
            V = Engine(dve, chain_v, held["dve"])
            v = nc.vector
            tt, ts, stt, cp = v.tensor_tensor, v.tensor_scalar, v.scalar_tensor_tensor, v.tensor_copy

            V.do(v.memset(ones[:], 1.0))
            V.do(v.memset(eps[:, 0:1], 1e-6))
            V.do(v.memset(eps[:, 1:2], 1e-5))
            V.tell(setup_v)
            dve.wait_ge(consts_in, 16 * CONST_DMAS)
            dve.wait_ge(setup_a, 1)
            top = lbt[:, 2, :]
            V.do(cp(top, lbc[:, 0, :]))
            for l in range(1, DEPTH):
                V.settle()
                V.do(tt(top, top, lbc[:, l, :], ALU.max))
            V.settle()
            for l in range(DEPTH):
                ins = tt(lbt[:, l, :], lbc[:, l, :], top, ALU.subtract)
                V.do(ins) if l < DEPTH - 1 else V.do(ins, setup_v, 2)
            dve.wait_ge(setup_a, 3)
            V.do(cp(top, lbt[:, 0, :]))
            for l in range(1, DEPTH):
                V.settle()
                V.do(tt(top, top, lbt[:, l, :], ALU.add))
            V.settle()
            V.do(v.reciprocal(top, top))
            V.settle()
            for l in range(DEPTH):
                V.do(tt(lbt[:, l, :], lbt[:, l, :], top, ALU.mult))
            V.settle()
            for l in range(1, DEPTH):
                V.do(tt(lbt[:, l, :], lbt[:, l, :], lbt[:, l - 1, :], ALU.add))
                V.settle()
            for l in range(DEPTH):
                V.do(tt(lb[:, l, :], lbt[:, l, :], lbt[:, 0, :], ALU.subtract))
            V.settle()
            V.do(ts(omlb[:], lb[:], -1.0, 1.0, ALU.mult, ALU.add))
            V.do(cp(mask[:], mask32[:]))
            V.do(cp(maskt[:], maskt32[:]))
            V.do(cp(eyeb[:], eyeb32[:]))
            V.do(cp(posf[:], posi[:]))
            V.settle()
            for t in range(TT):
                V.do(ts(ang[:, t, :], invf[:, :], posf[:, t:t + 1], None, ALU.mult))
            V.settle()
            magic, two_pi_hi = 12582912.0, 6.28125
            two_pi_lo = 2 * np.pi - two_pi_hi
            for quarter, dst in ((0.25, cos[:]), (0.0, sin[:, :, 1, :])):
                V.do(ts(turns[:], ang[:], float(1 / (2 * np.pi)), quarter, ALU.mult, ALU.add))
                V.settle()
                V.do(ts(turns[:], turns[:], magic, None, ALU.add))
                V.settle()
                V.do(ts(turns[:], turns[:], magic, None, ALU.subtract))
                V.settle()
                V.do(stt(dst, turns[:], -two_pi_hi, ang[:], ALU.mult, ALU.add))
                V.settle()
                V.do(stt(dst, turns[:], -float(two_pi_lo), dst, ALU.mult, ALU.add))
                V.settle()
                V.do(ts(dst, dst, float(quarter * 2 * np.pi), 3.1415925, ALU.add, ALU.min))
                V.settle()
                V.do(ts(dst, dst, -3.1415925, None, ALU.max), setup_v, 3 if quarter else 4)
            dve.wait_ge(setup_a, 4)
            V.do(ts(sin[:, :, 0, :], sin[:, :, 1, :], -1.0, None, ALU.mult), s["acc_done"], 1)
            V.tell(setup_v)
            V.tell(s["layer_open"])
            V.restart()

            with dve.Fori(0, DEPTH) as lay:
                def need(name, k=1, per=1):
                    dve.wait_ge(s[name], lay * per + k)

                def give(ins, name, k=1, per=1):
                    V.do(ins, s[name], lay * per + k)

                def core(name):
                    dve.wait_ge(core_done, lay * NCORE + CORE_AT[name])

                def read(ins, name):
                    V.do(ins, core_read["v"], lay * READS["v"] + READ_AT["v"][name])

                def block_in(b):
                    dve.wait_ge(block_done[b % 2], lay * (NBLK // 2) + b // 2 + 1)
                    return pb[:, 2 * (b % 2):2 * (b % 2) + 2, :]

                def block_out(ins, b):
                    V.do(ins, block_read[b % 2], lay * (NBLK // 2) + b // 2 + 2)

                flat = lambda ap: ap.rearrange("p a b -> p (a b)")
                dve.wait_ge(s["acc_done"], lay + 1)
                V.do(cp(lbl[:], lb[:, lay, :]))
                V.do(cp(omlbl[:], omlb[:, lay, :]))
                V.do(v.memset(cin[:, :, 0:CONV - 1], 0.0))
                core("conv_w")
                read(cp(cw[:].rearrange("p j c -> p (j c)"), pc[:, 0, 0:64]), "conv_w")
                V.settle()
                for b in range(4):
                    dve.wait_ge(block_read[b % 2], lay * (NBLK // 2) + b // 2 + 2)
                    for j in range(CONV):
                        for c in range(4):
                            ch = 4 * b + c
                            src, dst, w = cin[:, c, j:j + T], gqkv[:, ch, :], cw[:, j, ch:ch + 1]
                            ins = ts(dst, src, w, None, ALU.mult) if j == 0 else stt(dst, src, w, dst, ALU.mult, ALU.add)
                        if j < CONV - 1:
                            V.do(ins)
                            V.settle()
                        else:
                            give(ins, "conv_out", b + 1, 4)
                core("ba")
                part = lambda i: small[:, i, :].rearrange("p (t h) -> p t h", t=TT)
                bah = pc[:, 0, 0:16].rearrange("p (t n) -> p t n", t=TT)
                V.do(cp(part(2), bah[:, :, 0:H]))
                read(tt(part(3), bah[:, :, H:2 * H], mcast(dtb, TT), ALU.add), "ba")
                V.settle()
                give(ts(small[:, 6, :], small[:, 3, :], 0.0, None, ALU.max), "ba_raw")
                need("conv_silu", 2, 4)
                give(tt(sq[:], gqkv[:, 0:8, :], gqkv[:, 0:8, :], ALU.mult), "sq_ready")
                need("ba_exp")
                V.do(ts(small[:, 1, :], small[:, 2, :], 1.0, None, ALU.add))
                V.do(tt(small[:, 6, :], small[:, 6, :], small[:, 4, :], ALU.add))
                V.settle()
                V.do(v.reciprocal(small[:, 1, :], small[:, 1, :]))
                V.settle()
                V.do(ts(small[:, 7, :], small[:, 1, :], -1.0, None, ALU.mult))
                give(stt(part(0), part(6), -1.0, small[:, 5, None, 0:H].to_broadcast([P, TT, H]), ALU.mult, ALU.mult), "beta_g")
                need("lnexp_gn")
                V.do(stt(gqkv[:, 0:4, :], gqkv[:, 0:4, :], KSCALE, sq[:, 0:4, :], ALU.mult, ALU.mult))
                give(tt(gqkv[:, 4:8, :], gqkv[:, 4:8, :], sq[:, 4:8, :], ALU.mult), "qk_normed")
                src = block_in(5)
                V.do(ts(hg[:], src.rearrange("p b (h t) -> p (b h) t", h=2), 0.0, None, ALU.min))
                block_out(ts(he[:], src.rearrange("p b (h t) -> p (b h) t", h=2), 0.0, None, ALU.max), 5)
                V.settle()
                V.tell(s["hf_parts"])
                core("gvt")
                for i in range(8):
                    t, h = i // 4, i % 4
                    ins = ts(vb[:, t, h * HV:(h + 1) * HV], pc[:, 2 * t + h // 2, (h % 2) * HV:(h % 2) * HV + HV],
                             small[:, 1, i:i + 1], None, ALU.mult)
                    V.do(ins) if i < 7 else read(ins, "gvt")
                need("hf_exp")
                V.do(tt(hf[:], hg[:], he[:], ALU.mult))
                V.settle()
                for h in range(H):
                    V.do(stt(hg[:, h, :], he[:, h, :], lbl[:, h:h + 1], hg[:, h, :], ALU.mult, ALU.add))
                V.settle()
                give(ts(hg[:], hg[:], TINY, None, ALU.max), "hf_den")
                core("gcol")
                read(cp(small[:, 2, :], pc[:, 0, 0:8]), "gcol")
                V.settle()
                core("grow")
                V.do(stt(at[:], pc[:, 2:4, :].rearrange("p b (h t) -> p (b h) t", h=H), -1.0, mcast(strict, 8), ALU.mult, ALU.mult))
                for i in range(8):
                    if i == 4:
                        dve.wait_ge(core_read["a"], lay * READS["a"] + READ_AT["a"]["grow"])
                    ins = ts(dt_[:, i, :], pc[:, i // 4, (i % 4) * P:(i % 4) * P + P], small[:, 2, i:i + 1], 0.0, ALU.subtract, ALU.min)
                    V.do(ins) if i < 7 else read(ins, "grow")
                V.settle()
                V.tell(s["dt_raw"])
                need("hf_lns")
                for h in range(H):
                    V.do(stt(hk[:, h, :], hk[:, h, :], omlbl[:, h:h + 1], he[:, h, :], ALU.mult, ALU.mult))
                V.do(tt(hf[:], hg[:], hf[:], ALU.subtract))
                V.settle()
                for i in range(8):
                    h, t = i // 2, i % 2
                    V.do(v.tensor_tensor_scan(hg[:, h, t * P:(t + 1) * P], ones[:, :], hf[:, h, t * P:(t + 1) * P], 0.0, ALU.mult, ALU.add))
                V.settle()
                for b in (6, 7):
                    src = block_in(b).rearrange("p t (h s e) -> p t h s e", h=H, s=2)
                    dst = rqk[:, :, (b - 6) * 512:(b - 6) * 512 + 512].rearrange("p t (h s e) -> p t h s e", h=H, s=2)
                    tmp = gt[:, 0, :, :].rearrange("p t (h s e) -> p t h s e", h=H, s=2)
                    for t in range(TT):
                        for sd in range(2):
                            V.do(tt(tmp[:, t, :, sd, :], src[:, t, :, 1 - sd, :], mcast(sin[:, t, sd, :], H), ALU.mult))
                            V.do(tt(dst[:, t, :, sd, :], src[:, t, :, sd, :], mcast(cos[:, t, :], H), ALU.mult))
                    V.settle()
                    V.do(tt(rqk[:, :, (b - 6) * 512:(b - 6) * 512 + 512], rqk[:, :, (b - 6) * 512:(b - 6) * 512 + 512], gt[:, 0, :, :], ALU.add),
                         s["rope_done"], lay * 2 + b - 5)
                    V.settle()
                    V.tell(block_read[b % 2])
                need("dt_exp")
                V.do(tt(dt_[:], dt_[:], mcast(upper, 8), ALU.mult))
                V.settle()
                V.do(tt(at[:], at[:], dt_[:], ALU.mult))
                V.do(cp(ti[:], mcast(eye, 8)))
                V.do(cp(ui[:], mcast(eye, 8)))
                V.do(tt(qe[:], gqkv[:, 0:4, P:T], kd, ALU.mult))
                V.do(tt(ke[:], gqkv[:, 4:8, P:T], kd, ALU.mult))
                V.settle()
                core("gkt")
                for h in range(H):
                    ins = ts(kd[:, h, :], pc[:, 0, h * P:(h + 1) * P], dt_[:, h, P - 1:P], None, ALU.mult)
                    V.do(ins) if h < H - 1 else read(ins, "gkt")

                def h_factors(l):
                    V.settle()
                    if l < 8:
                        w = 2 ** l
                        view = lambda ap: ap.rearrange("p h (b s) -> p (h b) s", s=2 * w)
                        g, e, f, kk, qq = (view(a[:]) for a in (hg, he, hf, hk, hq))
                        nb = g.shape[1]
                        mid = g[:, :, w - 1:w].to_broadcast([P, nb, w])
                        V.do(tt(e[:, :, 0:w], mid, g[:, :, 0:w], ALU.subtract))
                        if l < 7:
                            V.do(tt(e[:, :, w:2 * w], g[:, :, w:2 * w], mid, ALU.subtract))
                        else:
                            V.do(cp(e[:, :, w:2 * w], g[:, :, w:2 * w]))
                        V.settle()
                        V.tell(s["h_diff"])
                        need("h_exp", l + 1, 8)
                        if l:
                            core(f"h{l - 1}")
                        V.do(tt(f[:, :, 0:w], e[:, :, 0:w], kk[:, :, 0:w], ALU.mult))
                        give(tt(f[:, :, w:2 * w], e[:, :, w:2 * w], qq[:, :, w:2 * w], ALU.mult), "h_fac", l + 1, 9)
                    else:
                        V.tell(s["h_fac"])

                def h_read(l):
                    if l == 7:
                        return
                    core(f"h{l}")
                    V.hold()
                    mk = mcast(eyeb, 8) if l == 8 else mcast(maskt[:, l, :], 8)
                    read(v.copy_predicated(atth[:], mk, pc[:, 2:4, :].rearrange("p b (h t) -> p (b h) t", h=H)), f"h{l}")

                def inverse_read(l):
                    core(f"yz{l}")
                    V.hold()
                    if l < LEVELS - 1:
                        V.do(v.copy_predicated(ti[:], mcast(mask[:, l, :], 8), pc[:, 0:2, :].rearrange("p b (h t) -> p (b h) t", h=H)))
                    read(v.copy_predicated(ui[:], mcast(maskt[:, l, :], 8), pc[:, 2:4, :].rearrange("p b (h t) -> p (b h) t", h=H)), f"yz{l}")
                    V.settle()
                    V.tell(s["level_t"])

                def gate_bias(i, b):
                    src = block_in(b)
                    dve.wait_ge(mbias_in[i % 2], 16 * (lay * 3 + i // 2 + 1))
                    if i >= 2:
                        need("merged_ready", i - 1, 6)
                    V.do(tt(gate[:, i % 2, :, :], src, mcast(mbias[:, i % 2, :], TT), ALU.add), s["gate_raw"], lay * 6 + i + 1)
                    V.settle()
                    V.tell(block_read[b % 2])

                def merge(i, b, k):
                    src = block_in(b)
                    need("gate_out", i + 1, 6)
                    mg = merged[:, :, k * 512:(k + 1) * 512]
                    if i < 2:
                        V.do(tt(mg, src, gate[:, k, :, :], ALU.mult), s["merged_ready"], lay * 6 + i + 1)
                        V.settle()
                        V.tell(block_read[b % 2])
                    else:
                        block_out(tt(gate[:, k, :, :], src, gate[:, k, :, :], ALU.mult), b)
                        V.settle()
                        V.do(tt(mg, mg, gate[:, k, :, :], ALU.add), s["merged_ready"], lay * 6 + i + 1)

                def gated(i, b0, b1):
                    for b in (b0, b1):
                        dve.wait_ge(block_read[b % 2], lay * (NBLK // 2) + b // 2 + 2)
                    V.settle()
                    for k in range(2):
                        yy = y[:, :, k * 512:(k + 1) * 512]
                        ins = tt(yy, yy, gt[:, k, :, :], ALU.mult)
                        V.do(ins) if k == 0 else give(ins, "y_done", i, 3)

                def rms_scale(name, k, gain):
                    need("rms_rstd", k, 2)
                    for i in range(8):
                        src = pc[:, 2 * (i // 4) + (i % 4) // 2, (i % 2) * HV:(i % 2) * HV + HV]
                        ins = stt(y[:, i // 4, (i % 4) * HV:(i % 4) * HV + HV], src, rstd[:, i:i + 1], gain[:, :], ALU.mult, ALU.mult)
                        V.do(ins) if i < 7 else read(ins, name)

                V.do(v.memset(atth[:], 0.0))
                h_factors(0)
                h_read(0)
                h_factors(1)
                core("rqk")
                V.do(tt(attr, pc[:, 0:2, :].rearrange("p b (h t) -> p (b h) t", h=2), decay[:], ALU.mult))
                read(tt(attr2, pc[:, 2, :].rearrange("p (h t) -> p h t", h=H), decay[:, :, 0:P], ALU.mult), "rqk")
                core("gkk")
                V.do(tt(attg[:], pc[:, 2:4, :].rearrange("p b (h t) -> p (b h) t", h=H), dt_[:], ALU.mult))
                read(tt(at[:], pc[:, 0:2, :].rearrange("p b (h t) -> p (b h) t", h=H), at[:], ALU.mult), "gkk")
                V.settle()
                V.tell(s["gkk_in"])
                h_read(1)
                h_factors(2)
                core("rout")
                for i in range(8):
                    src = pc[:, 2 * (i // 4) + (i % 4) // 2, (i % 2) * HV:(i % 2) * HV + HV]
                    V.do(v.bn_stats(stats[:, i, 0:6], src))
                V.settle()
                for i in range(8):
                    V.do(v.bn_aggr(mv[:, i, :], stats[:, i, 0:6]))
                V.settle()
                give(cp(rstd[:, :], mv[:, :, 1]), "rvar")
                need("rrstd")
                for i in range(8):
                    src = pc[:, 2 * (i // 4) + (i % 4) // 2, (i % 2) * HV:(i % 2) * HV + HV]
                    ins = ts(y[:, i // 4, (i % 4) * HV:(i % 4) * HV + HV], src, mv[:, i, 0:1], rstd[:, i:i + 1], ALU.subtract, ALU.mult)
                    V.do(ins) if i < 7 else read(ins, "rout")
                h_read(2)
                h_factors(3)
                inverse_read(0)
                h_read(3)
                gated(1, 10, 11)
                h_factors(4)
                gate_bias(0, 12)
                h_read(4)
                h_factors(5)
                merge(0, 13, 0)
                inverse_read(1)
                h_read(5)
                h_factors(6)
                gate_bias(1, 14)
                h_read(6)
                h_factors(7)
                merge(1, 15, 1)
                inverse_read(2)
                h_factors(8)
                h_read(8)
                inverse_read(3)
                rms_scale("hout", 1, hng)
                inverse_read(4)
                gated(2, 18, 19)
                gate_bias(2, 20)
                merge(2, 21, 0)
                inverse_read(5)
                gate_bias(3, 22)
                merge(3, 23, 1)
                inverse_read(6)
                gate_bias(4, 24)
                gate_bias(5, 25)
                core("ks")
                for h in range(H):
                    vv = vb[:, 1, h * HV:(h + 1) * HV]
                    ins = stt(vv, pc[:, h // 2, (h % 2) * HV:(h % 2) * HV + HV], small[:, 7, 4 + h:5 + h], vv, ALU.mult, ALU.add)
                    V.do(ins) if h < H - 1 else read(ins, "ks")
                rms_scale("gout", 2, gng)
                gated(3, 26, 27)
                merge(4, 28, 0)
                merge(5, 29, 1)

                def residual(b, k):
                    src = block_in(b)
                    xx = x[:, :, k * 512:(k + 1) * 512]
                    block_out(stt(xx, xx, ALPHA, src, ALU.mult, ALU.add), b)

                def layer_norm(k):
                    V.settle()
                    for t in range(TT):
                        for c in range(2):
                            V.do(v.bn_stats(stats[:, t, 6 * c:6 * c + 6], x[:, t, 512 * c:512 * c + 512]))
                    V.settle()
                    for t in range(TT):
                        V.do(v.bn_aggr(mv[:, t, :], stats[:, t, :]))
                    V.settle()
                    give(cp(rstd[:, 0:2], mv[:, 0:2, 1]), "ln_var", k, 2)
                    dve.wait_ge(s["ln_rstd"], lay * 2 + k)
                    for t in range(TT):
                        V.do(ts(x[:, t, :], x[:, t, :], mv[:, t, 0:1], rstd[:, t:t + 1], ALU.subtract, ALU.mult))
                    V.settle()
                    dve.wait_ge(ln_in, 64 * lay + 32 * k)
                    V.do(tt(x[:], x[:], mcast(lng, TT), ALU.mult))
                    V.settle()
                    give(tt(x[:], x[:], mcast(lnb, TT), ALU.add), "x_ready", k, 2)

                residual(30, 0)
                residual(31, 1)
                layer_norm(1)

                V.do(v.memset(zero[:], 0.0))
                V.do(v.memset(zeros512[:], 0.0))
                need("xh_ready")
                V.do(tt(xl[:], x[:], xh[:].bitcast(F32), ALU.subtract))
                core("router")
                read(cp(scores[:].rearrange("p t e -> p (t e)"), pc[:, 0, 0:TT * NE]), "router")
                V.settle()
                V.tell(s["logits"])
                need("score_out")
                V.do(tt(biased[:], scores[:], mcast(rb, TT), ALU.add))
                V.settle()

                def ranks(dst, vals, groups, width):
                    vv = vals.rearrange("p t (g j) -> p (t g) j", j=width)
                    other = vv[:, :, None, :].to_broadcast([P, groups, width, width])
                    own = vv[:, :, :, None].to_broadcast([P, groups, width, width])
                    c, q = cmp[:, 0:groups], eq[:, 0:groups]
                    V.do(tt(c, other, own, ALU.is_gt))
                    V.do(tt(q, other, own, ALU.is_equal))
                    V.settle()
                    V.do(tt(q, q, tie[:, None, :, :].to_broadcast([P, groups, EG, EG]), ALU.mult))
                    V.settle()
                    V.do(tt(c, c, q, ALU.add))
                    V.settle()
                    V.do(v.tensor_reduce(dst.rearrange("p t (g i) -> p (t g) i", i=width), c, AX.X, ALU.add))
                    V.settle()

                ranks(rank[:], biased[:], TT * NG, EG)
                V.do(ts(rank[:], rank[:], 2.0, None, ALU.is_lt))
                V.settle()
                V.do(tt(chosen[:], biased[:], rank[:], ALU.mult))
                V.settle()
                V.do(v.tensor_reduce(gsum[:], chosen[:].rearrange("p t (g j) -> p t g j", j=EG), AX.X, ALU.add))
                V.settle()
                ranks(best[:], gsum[:], TT, NG)
                V.do(ts(best[:], best[:], 1.0, None, ALU.is_lt))
                V.settle()
                give(tt(chosen[:].rearrange("p t (g j) -> p (t g) j", j=EG), rank[:].rearrange("p t (g j) -> p (t g) j", j=EG),
                        best[:].rearrange("p t g -> p (t g)")[:, :, None].to_broadcast([P, TT * NG, EG]), ALU.mult), "chosen_ready")
                V.settle()
                V.do(tt(comb[:], scores[:], chosen[:], ALU.mult))
                V.settle()
                V.do(v.tensor_reduce(wsum[:, :, 0], comb[:], AX.X, ALU.add))
                V.settle()
                V.do(v.reciprocal(wsum[:, :, 1], wsum[:, :, 0]))
                V.settle()
                for t in range(TT):
                    V.do(ts(comb[:, t, :], comb[:, t, :], wsum[:, t, 1:2], None, ALU.mult))
                core("pos")
                V.do(v.tensor_reduce(wsum[:, 0, 0:1], pc[:, 0, 2 * NE:3 * NE], AX.X, ALU.max))
                read(stt(posm[:].rearrange("p t e -> p (t e)"), pc[:, 0, 0:TT * NE], 1.0, chosen[:].rearrange("p t e -> p (t e)"),
                         ALU.add, ALU.mult), "pos")
                V.settle()
                V.do(ts(posm[:], posm[:], -1.0, None, ALU.add))
                V.do(ts(flag[:], wsum[:, 0, 0:1], float(P), None, ALU.is_gt), flag_ready, lay + 1)
                V.settle()
                V.tell(s["moe_ready"])

                def expert_pass(p):
                    def lo(c, base):
                        dve.wait_ge(split_hi, base + c + 1)
                        V.do(tt(wlo[:, c % SPLIT], raw[:, c % RAW], whi[:, c % SPLIT].bitcast(F32), ALU.subtract), split_lo,
                             base + c + 1 + CREDIT)

                    def choose(n, j, e):
                        V.do(cp(pcol[:, j, :], posm[:, :, e]))
                        V.do(cp(ccol[:, j, :], comb[:, :, e]))
                        V.settle()
                        for t in range(TT):
                            ins = ts(pick[:, j, t, :], iota[:, p * P:(p + 1) * P], pcol[:, j, t:t + 1], None, ALU.is_equal)
                            V.do(ins) if t == 0 else V.do(ins, se["pick_ready"], n + 1)

                    def gathered(n, j):
                        dve.wait_ge(se["gl_done"], n + 1)
                        V.do(cp(xgl[:, j].rearrange("p k t -> p (k t)"), pc[:, 2:4, :].rearrange("p b n -> p (b n)")), se["xgl_ready"], n + 1)

                    def expert(n, base, j, e, last_):
                        g = EXP_UNITS * j
                        V.n = 0
                        if not last_:
                            if e is not None:
                                choose(n + 1, 1 - j, e + 1)
                        lo(g + 4, base)
                        lo(g + 5, base)
                        dve.wait_ge(unit_done, base + g + 4 + CREDIT)
                        dve.wait_ge(se["silu_h"], n + 1)
                        V.do(tt(hs[:, :], hs[:, :], pc[:, 1, :], ALU.mult), se["h_ready"], n + 1)
                        dve.wait_ge(se["turned"], n + 1)
                        V.do(cp(cslot[:, j:j + 1], pc[:, 1, T:T + 1]))
                        V.do(cp(pickt[:, j, :], pc[:, 1, 0:T]), se["pickt_ready"], n + 1)
                        dve.wait_ge(se["hth_ready"], n + 1)
                        V.do(tt(htl[:].rearrange("p k t -> p (k t)"), pc[:, 0, :], hth[:].bitcast(F32).rearrange("p k t -> p (k t)"), ALU.subtract),
                             se["htl_ready"], n + 1)
                        if not last_:
                            gathered(n + 1, 1 - j)
                            lo(g + 6, base)
                            lo(g + 7, base)
                        dve.wait_ge(se["yh_ready"], n + 1)
                        V.do(stt(yl[:, :], pc[:, 2:4, :].rearrange("p b n -> p (b n)"), cslot[:, j:j + 1], yh[:, :].bitcast(F32),
                                 ALU.mult, ALU.subtract), se["yl_ready"], n + 1)
                        if not last_:
                            lo(g + 8, base)
                            lo(g + 9, base)
                        V.settle()
                        V.hold()
                        dve.sem_clear(chain_v)

                    n0 = (lay * 2 + p) * NE
                    u0 = (lay * 2 + p) * PASS_UNITS
                    V.restart()
                    choose(n0, 0, 0)
                    for c in range(4):
                        lo(c, u0)
                    gathered(n0, 0)
                    V.settle()
                    V.hold()
                    dve.sem_clear(chain_v)
                    with dve.Fori(0, NE // 2 - 1) as it:
                        for j in range(2):
                            expert(n0 + it * 2 + j, u0 + it * 2 * EXP_UNITS, j, 2 * it + j, False)
                    expert(n0 + NE - 2, u0 + (NE - 2) * EXP_UNITS, 0, NE - 2, False)
                    expert(n0 + NE - 1, u0 + (NE - 2) * EXP_UNITS, 1, None, True)
                    V.n = 0

                expert_pass(0)
                dve.wait_ge(flag_ready, lay + 1)
                V.hold()
                spill = dve.value_load(flag[0:1, 0:1], min_val=0, max_val=1)
                with dve.If(spill > 0):
                    expert_pass(1)
                with dve.Else():
                    dve.wait_ge(se["yl_ready"], (lay * 2 + 1) * NE)
                    dve.sem_inc(split_lo, PASS_UNITS)
                    for name in ("pick_ready", "xgl_ready", "h_ready", "pickt_ready", "htl_ready", "yl_ready"):
                        dve.sem_inc(se[name], NE)
                V.last = (se["yl_ready"], (lay * 2 + 2) * NE)
                dve.wait_ge(s["acc_done"], lay + 2)
                for t in range(TT):
                    V.do(stt(x[:, t, :], x[:, t, :], ALPHA, pb[:, 2 * t:2 * t + 2, :].rearrange("p b n -> p (b n)"), ALU.mult, ALU.add))
                layer_norm(2)
                V.settle()
                V.tell(s["layer_open"])
                V.restart()


INPUTS = ["x", "positions", "w_in", "gdn_conv_w", "gdn_a_log", "gdn_dt_bias", "gdn_norm_g", "hgrn_lb", "hgrn_norm_g",
          "merge_b", "w_branch", "w_out", "ln1_g", "ln1_b", "router_w", "router_b", "moe_w_gate", "moe_w_up",
          "moe_w_down", "ln2_g", "ln2_b"]


def kernel(**inputs):
    import concourse.bacc as bacc
    from concourse.bass_utils import run_bass_kernel_spmd

    nc = bacc.Bacc("TRN2", target_bir_lowering=False, num_devices=1)
    tables = constants()
    arrays, args = {}, []
    for name in INPUTS + CONSTS:
        a = np.ascontiguousarray(inputs[name] if name in inputs else tables[name])
        arrays[f"in_{name}"] = a
        args.append(nc.dram_tensor(f"in_{name}", a.shape, mybir.dt.from_np(a.dtype), kind="ExternalInput").ap())
    args.append(nc.dram_tensor("decoded", (1, T, D), F32, kind="ExternalOutput").ap())
    build_decoder(nc, *args)
    result = run_bass_kernel_spmd(nc, [arrays], core_ids=[0])
    return result.results[0]["decoded"]
```

```python
from contextlib import ExitStack

import numpy as np
import concourse.bass as bass
from concourse import mybir

F32 = mybir.dt.float32
F32R = mybir.dt.float32r
I32 = mybir.dt.int32
U8 = mybir.dt.uint8
ALU = mybir.AluOpType
ACT = mybir.ActivationFunctionType
AX = mybir.AxisListType

P = 128
D = 1024
T = 256
DEPTH = 2
H = 4
HK = 128
HV = 256
NE = 16
NG = 4
EG = 4
CONV = 4
DX = 512
KD = D // P
TT = T // P
ALPHA = (2 * DEPTH) ** 0.25
KSCALE = HK ** -0.5
LEVELS = 7
TINY = 2.0 ** -60

C_RQ, C_RK, C_RV, C_RG, C_GQKV = 0, 512, 1024, 2048, 3072
C_GZ, C_GB, C_HQ, C_HF, C_HI, C_HG, C_MG = 5120, 6144, 6152, 6664, 7176, 8200, 9224

BLOCKS = ([("in", C_GQKV), ("in", C_GQKV + 512), ("in", C_HQ), ("in", C_HF), ("in", C_RQ), ("in", C_RK),
           ("in", C_RV), ("in", C_RV + 512), ("in", C_MG), ("in", C_RG), ("in", C_RG + 512), ("in", C_HI),
           ("in", C_HI + 512), ("br", 0, 0), ("in", C_MG + 512), ("br", 0, 512), ("in", C_GQKV + 1024),
           ("in", C_GQKV + 1536), ("in", C_HG), ("in", C_HG + 512), ("in", C_MG + 2 * D), ("in", C_GZ), ("br", 2, 0),
           ("in", C_MG + 2 * D + 512), ("br", 2, 512), ("in", C_GZ + 512), ("in", C_MG + D), ("in", C_MG + D + 512),
           ("br", 1, 0), ("br", 1, 512), ("out", 0), ("out", 512)])
NBLK = len(BLOCKS)
MIX_UNITS = 2 * NBLK
EXP_UNITS = 6
PASS_UNITS = EXP_UNITS * NE
LAYER_UNITS = MIX_UNITS + 2 * PASS_UNITS
RAW = 4
SPLIT = 4
CREDIT = 4

ALL = (0, 1, 2, 3)
CORE = ([("conv_w", "v", (0,)), ("ba", "v", (0,)), ("gnorm", "a", ALL), ("gcol", "v", (0,)), ("grow", "va", ALL),
         ("gkt", "v", (0,)), ("rqkt", "a", ALL), ("h0", "v", (2, 3)), ("rqk", "v", (0, 1, 2)), ("gkk", "v", ALL),
         ("h1", "v", (2, 3)), ("x0", "a", (0, 1)), ("rout", "v", ALL), ("h2", "v", (2, 3)), ("yz0", "v", ALL),
         ("h3", "v", (2, 3)), ("x1", "a", (0, 1)), ("yz1", "v", ALL), ("ryt", "va", ALL), ("h4", "v", (2, 3)),
         ("x2", "a", (0, 1)), ("h5", "v", (2, 3)), ("yz2", "v", ALL), ("h6", "v", (2, 3)), ("x3", "a", (0, 1)),
         ("h7", "a", (2,)), ("yz3", "v", ALL), ("h8", "v", (2, 3)), ("x4", "a", (0, 1)), ("yz4", "v", ALL),
         ("hout", "va", ALL), ("x5", "a", (0, 1)), ("yz5", "v", ALL), ("x6", "a", (0, 1)), ("hyt", "va", ALL),
         ("yz6", "v", ALL), ("gvt", "v", ALL), ("vn0", "a", (0, 1)), ("state", "a", (0, 1)), ("ks", "v", (0, 1)),
         ("vn1", "a", (0, 1)), ("gout", "va", ALL), ("gyt", "va", ALL), ("mt", "va", ALL), ("x1t", "va", ALL),
         ("router", "v", (0,)), ("pos", "v", (0,)), ("x2t", "va", ALL)])
NCORE = len(CORE)
TURNS = ["ryt", "hyt", "gyt", "mt", "x1t", "x2t"]
CORE_AT = {name: i + 1 for i, (name, _, _) in enumerate(CORE)}
READ_AT = {e: {name: sum(e in who for _, who, _ in CORE[:i + 1]) for i, (name, _, _) in enumerate(CORE)} for e in "va"}
READS = {e: sum(e in who for _, who, _ in CORE) for e in "va"}

CONST_DMAS = 13
CONSTS = ["c_eye", "c_upper", "c_strict", "c_mask", "c_maskt", "c_eyeb", "c_decay", "c_iota", "c_invf", "c_tie"]


def constants():
    i = np.arange(P)
    rows, cols = i[:, None], i[None, :]
    f = np.float32
    mask = np.zeros((P, LEVELS, P), np.int32)
    for l in range(LEVELS):
        h = 2 ** l
        same = rows // (2 * h) == cols // (2 * h)
        mask[:, l] = same & (rows % (2 * h) >= h) & (cols % (2 * h) < h)
    maskt = np.ascontiguousarray(mask.transpose(2, 1, 0))
    lg = np.log1p(-(2.0 ** (-5.0 - np.arange(H))))
    rel = np.arange(T)[None, None, :] - i[:, None, None]
    decay = np.where(rel >= 0, np.exp(np.maximum(rel, 0) * lg[None, :, None]), 0.0) * KSCALE
    invf = (f(1.0) / (f(10000.0) ** np.linspace(0.0, 1.0, HK // 2, dtype=f))).astype(f)
    tie = np.zeros((P, EG, EG), f)
    tie[:] = np.arange(EG)[None, None, :] < np.arange(EG)[None, :, None]
    return {
        "c_eye": np.eye(P, dtype=f), "c_upper": (rows <= cols).astype(f), "c_strict": (rows < cols).astype(f),
        "c_mask": mask, "c_maskt": maskt, "c_eyeb": np.eye(P, dtype=np.int32),
        "c_decay": decay.astype(f),
        "c_iota": np.broadcast_to(np.arange(2 * P, dtype=f), (P, 2 * P)).copy(),
        "c_invf": np.broadcast_to(invf, (P, HK // 2)).copy(), "c_tie": tie,
    }


def build_decoder(nc, x_in, positions, w_in, conv_w, a_log, dt_bias, gdn_g, hgrn_lb, hgrn_g, merge_b, w_branch,
                  w_out, ln1_g, ln1_b, router_w, router_b, w_gate, w_up, w_down, ln2_g, ln2_b,
                  c_eye, c_upper, c_strict, c_mask, c_maskt, c_eyeb, c_decay, c_iota, c_invf, c_tie, out):
    with ExitStack() as ctx:
        def sb(name, shape, dt=F32, stack=ctx):
            return stack.enter_context(nc.sbuf_tensor(name, shape, dt))

        def sem(name):
            return ctx.enter_context(nc.semaphore(name))

        pb = ctx.enter_context(nc.psum_tensor("pb", [P, 4, 512], F32))
        pc = ctx.enter_context(nc.psum_tensor("pc", [P, 4, 512], F32))

        raw = sb("raw", [P, RAW, 4, 512])
        eye, upper, strict = sb("eye", [P, P]), sb("upper", [P, P]), sb("strict", [P, P])
        ones = sb("ones", [P, P])
        mask, maskt = sb("mask", [P, LEVELS, P], U8), sb("maskt", [P, LEVELS, P], U8)
        eyeb = sb("eyeb", [P, P], U8)
        tie = sb("tie", [P, EG, EG])
        cos, sin = sb("cos", [P, TT, 64]), sb("sin", [P, TT, 2, 64])
        eps = sb("eps", [P, 2])
        x = sb("x", [P, TT, D])
        xth, xtl = sb("xth", [P, KD, T], F32R), sb("xtl", [P, KD, T], F32R)
        lb, omlb = sb("lb", [P, DEPTH, H]), sb("omlb", [P, DEPTH, H])
        lbl, omlbl = sb("lbl", [P, H]), sb("omlbl", [P, H])
        rwh, rwl, rb = sb("rwh", [P, KD, NE], F32R), sb("rwl", [P, KD, NE], F32R), sb("rb", [P, NE])
        stats, mv = sb("stats", [P, 8, 12]), sb("mv", [P, 8, 2])
        rstd = sb("rstd", [P, 8])
        ss = sb("ss", [P, 8])
        flag = sb("flag", [P, 1], I32)

        mix = ExitStack()
        m = lambda name, shape, dt=F32: sb(name, shape, dt, mix)
        convraw, cw = m("convraw", [CONV * 16, P]), m("cw", [P, CONV, 16])
        wba = m("wba", [P, KD, 8])
        wbah, wbal = m("wbah", [P, KD, 8], F32R), m("wbal", [P, KD, 8], F32R)
        alog, dtb = m("alog", [P, H]), m("dtb", [P, H])
        gain = m("gain", [P, HV])
        mbias = m("mbias", [P, 512])
        small = m("small", [P, 8, 8])
        whi_m, wlo_m = m("whi_m", [P, 2, 4, 512], F32R), m("wlo_m", [P, 2, 4, 512], F32R)
        gqkv = m("gqkv", [P, 16, T])
        dt_, at, attg = m("dt", [P, 8, P]), m("at", [P, 8, P]), m("attg", [P, 8, P])
        ti, ui, kd = m("ti", [P, 8, P]), m("ui", [P, 8, P]), m("kd", [P, H, P])
        xi = dt_
        hq_hk = m("hq_hk", [P, 2, H, T])
        hg_hf = m("hg_hf", [P, 2, H, T])
        hq, hk, hg, hf = hq_hk[:, 0], hq_hk[:, 1], hg_hf[:, 0], hg_hf[:, 1]
        vb = hq_hk[:].rearrange("p a h t -> p a (h t)")
        lng1, lnb1 = hg_hf[:, 0].rearrange("p h t -> p (h t)"), hg_hf[:, 1].rearrange("p h t -> p (h t)")
        cin = m("cin", [P, 4, CONV - 1 + T])
        he = cin[:].rearrange("p c t -> p (c t)")[:, 0:H * T].rearrange("p (h t) -> p h t", h=H)
        atth = m("atth", [P, 8, P])
        attr = gqkv[:, 8:12, :]
        attr2 = gqkv[:, 12:14, :].rearrange("p a (b t) -> p (a b) t", b=2)
        atth2 = gqkv[:, 14:16, :].rearrange("p a (b t) -> p (a b) t", b=2)
        val = m("val", [P, TT, D])
        gt = val[:].rearrange("p t d -> p (t d)").rearrange("p (k t n) -> p k t n", k=2, t=TT)
        gate = m("gate", [P, TT, 512])
        decay = gate[:].rearrange("p t n -> p (t n)").rearrange("p (h t) -> p h t", h=H)
        gates = [gate[:]] * 5 + [atth[:].rearrange("p (t i) s -> p t (i s)", t=TT)]
        y = m("y", [P, TT, D])
        erow = y[:, 0, 0:512].rearrange("p (h t) -> p h t", h=H)
        merged = m("merged", [P, TT, D])
        rqk = merged
        state = xi
        early, late = ExitStack(), ExitStack()
        yt = sb("yt", [P, KD, T], F32, early)
        sq = yt
        early.close()
        yth, ytl = sb("yth", [P, KD, T], F32R, late), sb("ytl", [P, KD, T], F32R, late)
        late.close()
        mix.close()

        pre = ExitStack()
        m = lambda name, shape, dt=F32: sb(name, shape, dt, pre)
        lbc = m("lbc", [P, DEPTH, H])
        lbr = m("lbr", [DEPTH * H, P])
        lbt = m("lbt", [P, 4, H])
        mask32, maskt32 = m("mask32", [P, LEVELS, P], I32), m("maskt32", [P, LEVELS, P], I32)
        eyeb32 = m("eyeb32", [P, P], I32)
        rw = m("rw", [P, KD, NE])
        posi, posf = m("posi", [P, TT], I32), m("posf", [P, TT])
        invf = m("invf", [P, 64])
        ang, turns = m("ang", [P, TT, 64]), m("turns", [P, TT, 64])
        pre.close()

        moe = ExitStack()
        m = lambda name, shape, dt=F32: sb(name, shape, dt, moe)
        whi, wlo = m("whi", [P, SPLIT, 4, 512], F32R), m("wlo", [P, SPLIT, 4, 512], F32R)
        xh, xl = m("xh", [P, TT, D], F32R), m("xl", [P, TT, D], F32R)
        xgh, xgl = m("xgh", [P, 2, KD, P], F32R), m("xgl", [P, 2, KD, P], F32R)
        pick, pickt = m("pick", [P, 2, TT, P], F32R), m("pickt", [P, 2, T], F32R)
        hs = m("hs", [P, DX])
        hth, htl = m("hth", [P, 4, P], F32R), m("htl", [P, 4, P], F32R)
        yh, yl = m("yh", [P, D], F32R), m("yl", [P, D], F32R)
        lng2, lnb2 = m("lng2", [P, D]), m("lnb2", [P, D])
        iota = m("iota", [P, 2 * P])
        scores, biased = m("scores", [P, TT, NE]), m("biased", [P, TT, NE])
        cmp, eq = m("cmp", [P, 8, EG, EG]), m("eq", [P, 8, EG, EG])
        rank, best = m("rank", [P, TT, NE]), m("best", [P, TT, NG])
        gsum = m("gsum", [P, TT, NG])
        chosen, wsum = m("chosen", [P, TT, NE]), m("wsum", [P, TT, 2])
        comb, posm = m("comb", [P, TT, NE]), m("posm", [P, TT, NE])
        pcol, ccol = m("pcol", [P, 2, TT]), m("ccol", [P, 2, TT])
        cslot = m("cslot", [P, 2])
        moe.close()

        consts_in = sem("consts_in")
        x_loaded = sem("x_loaded")
        params_in = sem("params_in")
        mbias_in, gain_in, iota_in = sem("mbias_in"), sem("gain_in"), sem("iota_in")
        mix_hi, mix_lo = sem("mix_hi"), sem("mix_lo")
        turn_hi = sem("turn_hi")
        ln_in = sem("ln_in")
        raw_in = [sem(f"raw_in{i}") for i in range(RAW)]
        half_done = sem("half_done")
        block_done = [sem(f"block_done{i}") for i in range(2)]
        block_read = [sem(f"block_read{i}") for i in range(2)]
        core_done = sem("core_done")
        core_read = {"v": sem("core_read_v"), "a": sem("core_read_a")}
        setup_v, setup_a, setup_p = sem("setup_v"), sem("setup_a"), sem("setup_p")
        chain_v, chain_a = sem("chain_v"), sem("chain_a")
        names = ["conv_out", "conv_silu", "gates_small", "sq_ready", "qk_normed", "beta_g", "lnexp_gn", "dt_raw", "dt_exp", "gkk_in",
                 "rope_done", "hf_parts", "hf_exp", "hf_den", "hf_lns", "h_diff", "h_exp", "h_fac",
                 "rvar", "rrstd", "y_done", "gate_raw", "gate_out", "rms_rstd", 
                 "merged_ready", "x_ready", "ln_var", "ln_rstd", "xh_ready", "layer_open", "logits", "score_out", "chosen_ready", "moe_ready",
                 "acc_done", "level_t", "ba_raw", "ba_exp", "wba_ready"]
        s = {name: sem(name) for name in names}
        split_hi, split_lo, unit_done = sem("split_hi"), sem("split_lo"), sem("unit_done")
        e_names = ["pick_ready", "gh_done", "xgh_ready", "gl_done", "xgl_ready", "silu_h", "h_ready", "turned",
                   "hth_ready", "htl_ready", "pickt_ready", "yh_ready", "yl_ready", "scattered"]
        se = {name: sem(name) for name in e_names}
        flag_ready = sem("flag_ready")
        held = {e: sem(f"held_{e}") for e in ("sp", "pool", "pe", "act", "dve")}
        out_done = sem("out_done")

        mcast = lambda ap, n: ap[:, None, :].to_broadcast([P, n, ap.shape[-1]])

        def unit_source(block, half, lay):
            r = slice(512 * half, 512 * half + 512)
            if block[0] == "in":
                src = w_in[lay, r, block[1]:block[1] + 512]
            elif block[0] == "br":
                src = w_branch[lay, block[1], r, block[2]:block[2] + 512]
            else:
                src = w_out[lay, r, block[1]:block[1] + 512]
            return src.rearrange("(k p) n -> p k n", p=P)

        def expert_source(i, lay, e):
            if i < 4:
                src = (w_gate if i < 2 else w_up)[lay, e, 512 * (i % 2):512 * (i % 2) + 512, :]
            else:
                src = w_down[lay, e, :, 512 * (i - 4):512 * (i - 4) + 512]
            return src.rearrange("(k p) n -> p k n", p=P)

        class Engine:

            def __init__(self, eng, chain, held):
                self.held = held
                self.eng, self.chain, self.n, self.last = eng, chain, 0, None

            def do(self, ins, signal=None, value=None):
                if signal is None:
                    self.n += 1
                    signal, value = self.chain, self.n
                ins.then_inc(signal, 1)
                self.last = (signal, value)

            def settle(self):
                self.eng.wait_ge(*self.last)

            def tell(self, signal):
                self.settle()
                self.eng.sem_inc(signal, 1)

            def restart(self):
                self.settle()
                self.hold()
                self.eng.sem_clear(self.chain)
                self.n = 0

            def hold(self):
                self.eng.sem_inc(self.held, 1)

        block = ctx.enter_context(nc.Block())

        @block.sync
        def _(sp):
            sp.dma_start(x[:, :, :], x_in[0].rearrange("(t p) d -> p t d", p=P)).then_inc(x_loaded, 16)
            sp.sem_inc(split_lo, CREDIT)
            with sp.Fori(0, DEPTH) as lay:
                for u in range(MIX_UNITS):
                    if u < RAW:
                        sp.wait_ge(split_lo, lay * 2 * PASS_UNITS + u + 1)
                    else:
                        sp.wait_ge(mix_lo, lay * MIX_UNITS + u - RAW + 1)
                    sp.sem_inc(held["sp"], 1)
                    sp.dma_start(raw[:, u % RAW], unit_source(BLOCKS[u // 2], u % 2, lay)).then_inc(raw_in[u % RAW], 16)
                sp.wait_ge(mix_lo, lay * MIX_UNITS + MIX_UNITS)
                sp.sem_inc(held["sp"], 1)

                def stream_pass(p):
                    with sp.Fori(0, NE // 2) as it:
                        for j in range(2):
                            for i in range(EXP_UNITS):
                                c = EXP_UNITS * j + i
                                sp.wait_ge(split_lo, (lay * 2 + p) * PASS_UNITS + it * 2 * EXP_UNITS + c + CREDIT - RAW + 1)
                                sp.sem_inc(held["sp"], 1)
                                sp.dma_start(raw[:, c % RAW], expert_source(i, lay, 2 * it + j)).then_inc(raw_in[c % RAW], 16)

                stream_pass(0)
                sp.wait_ge(flag_ready, lay + 1)
                sp.sem_inc(held["sp"], 1)
                spill = sp.value_load(flag[0:1, 0:1], min_val=0, max_val=1)
                with sp.If(spill > 0):
                    stream_pass(1)
                with sp.Else():
                    for i in range(RAW):
                        sp.wait_ge(raw_in[i], 16 * (lay * (LAYER_UNITS // RAW) + (MIX_UNITS + PASS_UNITS) // RAW))
                        sp.sem_inc(raw_in[i], 16 * PASS_UNITS // RAW)
            sp.wait_ge(s["x_ready"], 2 * DEPTH)
            sp.dma_start(out[0].rearrange("(t p) d -> p t d", p=P), x[:, :, :]).then_inc(out_done, 16)
            sp.wait_ge(out_done, 16)

        @block.gpsimd
        def _(pool):
            for dst, src in ((eye, c_eye), (upper, c_upper), (strict, c_strict), (mask32, c_mask), (maskt32, c_maskt),
                             (eyeb32, c_eyeb), (invf, c_invf), (tie, c_tie)):
                pool.dma_start(dst[:], src).then_inc(consts_in, 16)
            for t in range(TT):
                pool.dma_start(posi[:, t:t + 1], positions[0, t * P:(t + 1) * P][:, None]).then_inc(consts_in, 16)
            pool.dma_start(lbr[:], hgrn_lb.rearrange("l (h p) -> (l h) p", p=P)).then_inc(consts_in, 16)
            pool.dma_start(rw[:], router_w.rearrange("(k p) e -> p k e", p=P)).then_inc(consts_in, 16)
            pool.dma_start(rb[:], router_b[None, :].partition_broadcast(P)).then_inc(consts_in, 16)
            with pool.Fori(0, DEPTH) as lay:
                pool.wait_ge(setup_v, 1)
                pool.wait_ge(s["acc_done"], lay + 1)
                pool.wait_ge(s["layer_open"], lay + 1)
                pool.sem_inc(held["pool"], 1)
                pool.dma_start(convraw[:], conv_w[lay].rearrange("j (c p) -> (j c) p", p=P)).then_inc(params_in, 16)
                pool.dma_start(wba[:], w_in[lay, :, C_GB:C_GB + 8].rearrange("(k p) n -> p k n", p=P)).then_inc(params_in, 16)
                pool.dma_start(alog[:], a_log[lay][None, :].partition_broadcast(P)).then_inc(params_in, 16)
                pool.dma_start(dtb[:], dt_bias[lay][None, :].partition_broadcast(P)).then_inc(params_in, 16)
                pool.dma_start(decay, c_decay).then_inc(params_in, 16)
                bcast = lambda ap: ap[None, :].partition_broadcast(P)

                def merge_bias(i):
                    base = (0, 512, 2 * D, 2 * D + 512, D, D + 512)[i]
                    if i:
                        pool.wait_ge(s["gate_raw"], lay * 6 + i)
                        pool.sem_inc(held["pool"], 1)
                    pool.dma_start(mbias[:, :], bcast(merge_b[lay, base:base + 512])).then_inc(mbias_in, 16)

                pool.dma_start(gain[:], bcast(hgrn_g[lay])).then_inc(gain_in, 16)
                for i in range(3):
                    merge_bias(i)
                pool.wait_ge(core_done, lay * NCORE + CORE_AT["h8"])
                pool.sem_inc(held["pool"], 1)
                pool.dma_start(lng1, bcast(ln1_g[lay])).then_inc(ln_in, 16)
                pool.dma_start(lnb1, bcast(ln1_b[lay])).then_inc(ln_in, 16)
                pool.wait_ge(core_read["v"], lay * READS["v"] + READ_AT["v"]["hout"])
                pool.sem_inc(held["pool"], 1)
                pool.dma_start(gain[:], bcast(gdn_g[lay])).then_inc(gain_in, 16)
                for i in range(3, 6):
                    merge_bias(i)
                pool.wait_ge(s["x_ready"], 2 * lay + 1)
                pool.sem_inc(held["pool"], 1)
                pool.dma_start(iota[:], c_iota).then_inc(iota_in, 16)
                pool.dma_start(lng2[:], bcast(ln2_g[lay])).then_inc(ln_in, 16)
                pool.dma_start(lnb2[:], bcast(ln2_b[lay])).then_inc(ln_in, 16)

        @block.tensor
        def _(pe):
            mm = nc.tensor.matmul

            def turn(dst, src, n=P):
                return nc.tensor.transpose(dst, src, eye[0:n, 0:n])

            def turn16(src):
                for v in range(KD):
                    for t in range(TT):
                        last = turn(pc[:, v // 2, (v % 2) * T + t * P:(v % 2) * T + t * P + P], src[:, t, v * P:(v + 1) * P])
                return last

            pe.wait_ge(consts_in, 16 * CONST_DMAS)
            pe.wait_ge(x_loaded, 16)
            for i in range(2):
                pe.sem_inc(block_read[i], 1)
            pe.sem_inc(unit_done, CREDIT)
            turn(pc[:, 0, 0:DEPTH * H], lbr[:, :], DEPTH * H).then_inc(setup_p, 1)
            pe.wait_ge(setup_a, 1)
            turn16(x).then_inc(setup_p, 1)
            pe.wait_ge(setup_a, 3)
            pe.wait_ge(setup_v, 6)
            pe.sem_inc(held["pe"], 1)

            with pe.Fori(0, DEPTH) as lay:
                def core(name):
                    i = CORE_AT[name] - 1
                    for e in "va":
                        before = [c for c, who, banks in CORE[:i] if e in who and set(banks) & set(CORE[i][2])]
                        if before:
                            pe.wait_ge(core_read[e], lay * READS[e] + READ_AT[e][before[-1]])

                def need(name, k=1, per=1):
                    pe.wait_ge(s[name], lay * per + k)

                def project(b, src, rows=True, mid=None):
                    pair = b % 2
                    xh_, xl_ = src
                    pe.wait_ge(block_read[pair], lay * (NBLK // 2) + b // 2 + 1)
                    for half in range(2):
                        pe.wait_ge(mix_lo, lay * MIX_UNITS + 2 * b + half + 1)
                        wh, wl = whi_m[:, half], wlo_m[:, half]
                        if rows:
                            for t in range(TT):
                                for k in range(4):
                                    kk = 4 * half + k
                                    ts_ = slice(t * P, (t + 1) * P)
                                    o = pb[:, 2 * pair + t, :]
                                    mm(o, xh_[:, kk, ts_], wh[:, k, :], start=(kk == 0), stop=False)
                                    mm(o, xh_[:, kk, ts_], wl[:, k, :], start=False, stop=False)
                                    last = mm(o, xl_[:, kk, ts_], wh[:, k, :], start=False, stop=(kk == KD - 1))
                        else:
                            for k in range(4):
                                kk = 4 * half + k
                                for c in range(4):
                                    o = pb[:, 2 * pair + c // 2, (c % 2) * T:(c % 2) * T + T]
                                    cs = slice(c * P, (c + 1) * P)
                                    mm(o, wh[:, k, cs], xh_[:, kk, :], start=(kk == 0 and c % 2 == 0), stop=False,
                                       skip_group_check=True)
                                    mm(o, wh[:, k, cs], xl_[:, kk, :], start=False, stop=False, skip_group_check=True)
                                    last = mm(o, wl[:, k, cs], xh_[:, kk, :], start=False, stop=(kk == KD - 1),
                                              skip_group_check=True)
                        last.then_inc(half_done if half == 0 else block_done[pair], 1)
                        if half == 0 and mid:
                            mid()

                def h_level(l):
                    core(f"h{l}")
                    need("h_fac", l + 1, 9)
                    if l == 7:
                        for h in range(H):
                            last = mm(pc[:, 2, h * P:(h + 1) * P], hf[:, h, 0:P], hf[:, h, P:T], start=True, stop=True)
                    else:
                        for t in range(TT):
                            for h in range(H):
                                a = (hk if l == 8 else hf)[:, h, t * P:(t + 1) * P]
                                bb = (hq if l == 8 else hf)[:, h, t * P:(t + 1) * P]
                                last = mm(pc[:, 2 + t, h * P:(h + 1) * P], a, bb, start=True, stop=True)
                    last.then_inc(core_done, 1)

                def inverse_x(l):
                    core(f"x{l}")
                    if l == 0:
                        need("gkk_in")
                    else:
                        need("level_t", l, LEVELS)
                    for i in range(8):
                        last = mm(pc[:, i // 4, (i % 4) * P:(i % 4) * P + P], at[:, i, :], ti[:, i, :], start=True, stop=True)
                    last.then_inc(core_done, 1)

                def inverse_yz(l):
                    core(f"yz{l}")
                    for i in range(8):
                        if l < LEVELS - 1:
                            mm(pc[:, i // 4, (i % 4) * P:(i % 4) * P + P], ui[:, i, :], xi[:, i, :], start=True, stop=True)
                        last = mm(pc[:, 2 + i // 4, (i % 4) * P:(i % 4) * P + P], xi[:, i, :], ui[:, i, :], start=True, stop=True)
                    last.then_inc(core_done, 1)

                xt, yt2 = (xth, xtl), (yth, ytl)
                pe.wait_ge(s["acc_done"], lay + 1)
                core("conv_w")
                pe.wait_ge(params_in, 80 * lay + 80)
                pe.wait_ge(s["layer_open"], lay + 1)
                pe.sem_inc(held["pe"], 1)
                turn(pc[:, 0, 0:64], convraw[:, :], 64).then_inc(core_done, 1)
                project(0, xt, rows=False)
                project(1, xt, rows=False)
                core("ba")
                need("wba_ready")
                for t in range(TT):
                    for k in range(KD):
                        o, ts_ = pc[:, 0, t * 8:t * 8 + 8], slice(t * P, (t + 1) * P)
                        mm(o, xth[:, k, ts_], wbah[:, k, :], start=(t == 0 and k == 0), stop=False, skip_group_check=True)
                        mm(o, xth[:, k, ts_], wbal[:, k, :], start=False, stop=False, skip_group_check=True)
                        last = mm(o, xtl[:, k, ts_], wbah[:, k, :], start=False, stop=(k == KD - 1), skip_group_check=True)
                last.then_inc(core_done, 1)
                project(2, xt, rows=False)
                core("gnorm")
                need("sq_ready")
                for j in range(4):
                    last = mm(pc[:, j, :], ones[:, :], sq[:, 2 * j:2 * j + 2, :], start=True, stop=True)
                last.then_inc(core_done, 1)
                project(3, xt, rows=False)
                core("gcol")
                need("beta_g")
                mm(pc[:, 0, 0:8], upper[:, :], small[:, 0, :], start=True, stop=True).then_inc(core_done, 1)
                project(4, xt)
                core("grow")
                for i in range(8):
                    mm(pc[:, i // 4, (i % 4) * P:(i % 4) * P + P], small[:, 0, i:i + 1].to_broadcast([P, P]), upper[:, :],
                       start=True, stop=True)
                for i in range(8):
                    last = mm(pc[:, 2 + i // 4, (i % 4) * P:(i % 4) * P + P], small[:, 1, i:i + 1].to_broadcast([P, P]), eye[:, :],
                              start=True, stop=True)
                last.then_inc(core_done, 1)
                project(5, xt)
                core("gkt")
                need("qk_normed")
                for h in range(H):
                    last = turn(pc[:, 0, h * P:(h + 1) * P], gqkv[:, 4 + h, 0:P])
                last.then_inc(core_done, 1)
                project(6, xt)
                core("rqkt")
                need("rope_done", 2, 2)
                turn16(rqk).then_inc(core_done, 1)
                h_level(0)
                project(7, xt)
                core("rqk")
                for h in range(H):
                    mm(pc[:, h // 2, (h % 2) * T:(h % 2) * T + T], yt[:, 4 + h, 0:P], yt[:, h, :], start=True, stop=True)
                for h in range(H):
                    last = mm(pc[:, 2, h * P:(h + 1) * P], yt[:, 4 + h, P:T], yt[:, h, P:T], start=True, stop=True)
                last.then_inc(core_done, 1)
                core("gkk")
                for i in range(8):
                    h, t = i % 4, i // 4
                    kt = gqkv[:, 4 + h, t * P:(t + 1) * P]
                    mm(pc[:, t, h * P:(h + 1) * P], kt, kt, start=True, stop=True)
                    last = mm(pc[:, 2 + t, h * P:(h + 1) * P], kt, gqkv[:, h, t * P:(t + 1) * P], start=True, stop=True)
                last.then_inc(core_done, 1)
                h_level(1)
                project(8, xt, mid=lambda: inverse_x(0))

                def attend(name, same, across, v_blocks):
                    core(name)
                    for b in v_blocks:
                        pe.wait_ge(block_read[b % 2], lay * (NBLK // 2) + b // 2 + 2)
                    for h in range(H):
                        mm(pc[:, h // 2, (h % 2) * HV:(h % 2) * HV + HV], same(h, 0), val[:, 0, h * HV:(h + 1) * HV],
                           start=True, stop=True)
                    for h in range(H):
                        o = pc[:, 2 + h // 2, (h % 2) * HV:(h % 2) * HV + HV]
                        mm(o, across(h), val[:, 0, h * HV:(h + 1) * HV], start=True, stop=False)
                        last = mm(o, same(h, 1), val[:, 1, h * HV:(h + 1) * HV], start=False, stop=True)
                    last.then_inc(core_done, 1)

                def turned(name, src, feed, k=1, per=1):
                    core(name)
                    need(feed, k, per)
                    turn16(src).then_inc(core_done, 1)

                def both_parts(name):
                    pe.wait_ge(core_read["v"], lay * READS["v"] + READ_AT["v"][name])

                def heads(name, lhs, rhs):
                    core(name)
                    for h in range(H):
                        last = mm(pc[:, h // 2, (h % 2) * HV:(h % 2) * HV + HV], lhs(h), rhs(h), start=True, stop=True)
                    last.then_inc(core_done, 1)

                attend("rout", lambda h, t: attr[:, h, 0:P] if t == 0 else attr2[:, h, :],
                       lambda h: attr[:, h, P:T], (6, 7))
                project(9, xt, mid=lambda: h_level(2))
                inverse_yz(0)
                project(10, xt, mid=lambda: h_level(3))
                inverse_x(1)
                project(11, xt, mid=lambda: inverse_yz(1))
                turned("ryt", y, "y_done", 1, 3)
                project(12, xt, mid=lambda: h_level(4))
                inverse_x(2)
                both_parts("ryt")
                project(13, yt2, mid=lambda: h_level(5))
                inverse_yz(2)
                project(14, xt, mid=lambda: h_level(6))
                inverse_x(3)
                project(15, yt2, mid=lambda: h_level(7))
                inverse_yz(3)
                project(16, xt, rows=False, mid=lambda: h_level(8))
                inverse_x(4)
                project(17, xt, rows=False, mid=lambda: inverse_yz(4))
                attend("hout", lambda h, t: atth[:, 4 * t + h, :], lambda h: atth2[:, h, :], (11, 12))
                project(18, xt)
                inverse_x(5)
                project(19, xt, mid=lambda: inverse_yz(5))
                project(20, xt, mid=lambda: inverse_x(6))
                turned("hyt", y, "y_done", 2, 3)
                project(21, xt, mid=lambda: inverse_yz(6))
                core("gvt")
                need("conv_silu", 4, 4)
                for c in range(8):
                    for t in range(TT):
                        last = turn(pc[:, 2 * t + c // 4, (c % 4) * P:(c % 4) * P + P], gqkv[:, 8 + c, t * P:(t + 1) * P])
                last.then_inc(core_done, 1)
                both_parts("hyt")
                project(22, yt2)

                def vn0():
                    need("level_t", LEVELS, LEVELS)
                    heads("vn0", lambda h: ui[:, h, :], lambda h: vb[:, 0, h * HV:(h + 1) * HV])

                project(23, xt, mid=vn0)
                project(24, yt2, mid=lambda: heads("state", lambda h: kd[:, h, :], lambda h: vb[:, 0, h * HV:(h + 1) * HV]))
                heads("ks", lambda h: gqkv[:, 4 + h, P:T], lambda h: state[:, 2 * h:2 * h + 2, :])
                project(25, xt, mid=lambda: heads("vn1", lambda h: ui[:, 4 + h, :], lambda h: vb[:, 1, h * HV:(h + 1) * HV]))
                core("gout")
                for h in range(H):
                    mm(pc[:, h // 2, (h % 2) * HV:(h % 2) * HV + HV], attg[:, h, :], vb[:, 0, h * HV:(h + 1) * HV],
                       start=True, stop=True)
                for h in range(H):
                    o = pc[:, 2 + h // 2, (h % 2) * HV:(h % 2) * HV + HV]
                    mm(o, gqkv[:, h, P:T], state[:, 2 * h:2 * h + 2, :], start=True, stop=False)
                    last = mm(o, attg[:, 4 + h, :], vb[:, 1, h * HV:(h + 1) * HV], start=False, stop=True)
                last.then_inc(core_done, 1)
                project(26, xt)
                project(27, xt, mid=lambda: turned("gyt", y, "y_done", 3, 3))
                both_parts("gyt")
                project(28, yt2)
                project(29, yt2)
                turned("mt", merged, "merged_ready", 6, 6)
                both_parts("mt")
                project(30, yt2)
                project(31, yt2)
                turned("x1t", x, "x_ready", 1, 2)
                both_parts("x1t")
                core("router")
                for t in range(TT):
                    for k in range(KD):
                        o, ts_ = pc[:, 0, t * NE:(t + 1) * NE], slice(t * P, (t + 1) * P)
                        mm(o, xth[:, k, ts_], rwh[:, k, :], start=(t == 0 and k == 0), stop=False, skip_group_check=True)
                        mm(o, xth[:, k, ts_], rwl[:, k, :], start=False, stop=False, skip_group_check=True)
                        last = mm(o, xtl[:, k, ts_], rwh[:, k, :], start=False, stop=(k == KD - 1), skip_group_check=True)
                last.then_inc(core_done, 1)
                core("pos")
                need("chosen_ready")
                mm(pc[:, 0, 0:NE], strict[:, :], chosen[:, 0, :], start=True, stop=True)
                mm(pc[:, 0, NE:2 * NE], ones[:, :], chosen[:, 0, :], start=True, stop=False)
                mm(pc[:, 0, NE:2 * NE], strict[:, :], chosen[:, 1, :], start=False, stop=True)
                mm(pc[:, 0, 2 * NE:3 * NE], ones[:, :], chosen[:, 0, :], start=True, stop=False)
                mm(pc[:, 0, 2 * NE:3 * NE], ones[:, :], chosen[:, 1, :], start=False, stop=True).then_inc(core_done, 1)
                def expert_pass(p):
                    def gather(part, n, j):
                        for k in range(KD):
                            for t in range(TT):
                                last = mm(pc[:, 2 + k // 4, (k % 4) * P:(k % 4) * P + P], part[:, t, k * P:(k + 1) * P],
                                          pick[:, j, t, :], start=(t == 0), stop=(t == TT - 1))
                        return last

                    def gather_hi(n, j):
                        pe.wait_ge(se["pick_ready"], n + 1)
                        gather(xh, n, j).then_inc(se["gh_done"], 1)

                    def gather_lo(n, j):
                        pe.wait_ge(se["xgh_ready"], n + 1)
                        gather(xl, n, j).then_inc(se["gl_done"], 1)

                    def passes(dst, ah, al, c, base, first, last_):
                        pe.wait_ge(split_lo, base + c + 1 + CREDIT)
                        for k in range(4):
                            mm(dst, ah(k), whi[:, c % SPLIT, k, :], start=(first and k == 0), stop=False)
                            mm(dst, ah(k), wlo[:, c % SPLIT, k, :], start=False, stop=False)
                            ins = mm(dst, al(k), whi[:, c % SPLIT, k, :], start=False, stop=(last_ and k == 3))
                        ins.then_inc(unit_done, 1)

                    def scatter(n, j, opens=False):
                        pe.wait_ge(se["yl_ready"], n + 1)
                        pe.wait_ge(se["pickt_ready"], n + 1)
                        for t in range(TT):
                            for cb in range(2):
                                for part in (yh, yl):
                                    last = mm(pb[:, 2 * t + cb, :], pickt[:, j, t * P:(t + 1) * P],
                                              part[:, cb * 512:(cb + 1) * 512], start=(opens and part is yh), stop=False,
                                              skip_group_check=True)
                        last.then_inc(se["scattered"], 1)

                    def expert(n, base, j, first=False, second=False, last_=False):
                        g = EXP_UNITS * j
                        pe.wait_ge(se["xgl_ready"], n + 1)
                        if not first:
                            pe.wait_ge(se["hth_ready"], n)
                            pe.wait_ge(se["htl_ready"], n)
                        for i in range(2):
                            passes(pc[:, 0, :], lambda k: xgh[:, j, 4 * i + k, :], lambda k: xgl[:, j, 4 * i + k, :],
                                   g + i, base, i == 0, i == 1)
                        if not last_:
                            if not first:
                                pe.wait_ge(se["yh_ready"], n)
                                pe.wait_ge(se["yl_ready"], n)
                            gather_hi(n + 1, 1 - j)
                        if not first:
                            pe.wait_ge(se["pickt_ready"], n)
                        for i in range(2):
                            passes(pc[:, 1, :], lambda k: xgh[:, j, 4 * i + k, :], lambda k: xgl[:, j, 4 * i + k, :],
                                   g + 2 + i, base, i == 0, i == 1)
                        if not last_:
                            gather_lo(n + 1, 1 - j)
                        pe.wait_ge(se["h_ready"], n + 1)
                        for f in range(4):
                            turn(pc[:, 0, f * P:(f + 1) * P], hs[:, f * P:(f + 1) * P])
                        for t in range(TT):
                            turn(pc[:, 1, t * P:(t + 1) * P], pick[:, j, t, :].bitcast(F32))
                        for t in range(TT):
                            ins = mm(pc[:, 1, T:T + 1], pick[:, j, t, :].bitcast(F32), ccol[:, j, t:t + 1],
                                     start=(t == 0), stop=(t == TT - 1))
                        ins.then_inc(se["turned"], 1)
                        if not first:
                            scatter(n - 1, 1 - j, opens=second and p == 0)
                        pe.wait_ge(se["htl_ready"], n + 1)
                        if not last_:
                            pe.wait_ge(se["xgl_ready"], n + 2)
                        for i in range(2):
                            passes(pc[:, 2 + i, :], lambda k: hth[:, k, :], lambda k: htl[:, k, :], g + 4 + i, base, True, True)

                    n0 = (lay * 2 + p) * NE
                    u0 = (lay * 2 + p) * PASS_UNITS
                    gather_hi(n0, 0)
                    gather_lo(n0, 0)
                    expert(n0, u0, 0, first=True)
                    expert(n0 + 1, u0, 1, second=True)
                    with pe.Fori(1, NE // 2 - 1) as it:
                        for j in range(2):
                            expert(n0 + it * 2 + j, u0 + it * 2 * EXP_UNITS, j)
                    expert(n0 + NE - 2, u0 + (NE - 2) * EXP_UNITS, 0)
                    expert(n0 + NE - 1, u0 + (NE - 2) * EXP_UNITS, 1, last_=True)
                    scatter(n0 + NE - 1, 1)

                expert_pass(0)
                pe.wait_ge(flag_ready, lay + 1)
                pe.sem_inc(held["pe"], 1)
                spill = pe.value_load(flag[0:1, 0:1], min_val=0, max_val=1)
                with pe.If(spill > 0):
                    expert_pass(1)
                with pe.Else():
                    pe.wait_ge(se["scattered"], (lay * 2 + 1) * NE)
                    for name in ("gh_done", "gl_done", "turned", "scattered"):
                        pe.sem_inc(se[name], NE)
                    pe.sem_inc(unit_done, PASS_UNITS)
                pe.wait_ge(se["scattered"], (lay * 2 + 2) * NE)
                pe.sem_inc(s["acc_done"], 1)
                turned("x2t", x, "x_ready", 2, 2)
                both_parts("x2t")

        @block.scalar
        def _(act):
            A = Engine(act, chain_a, held["act"])
            fn = nc.scalar.activation

            act.wait_ge(setup_p, 1)
            fn(lbc[:].rearrange("p l h -> p (l h)"), pc[:, 0, 0:DEPTH * H], ACT.Copy).then_inc(setup_a, 1)
            act.wait_ge(setup_p, 2)
            fn(xth[:].rearrange("p k t -> p (k t)"), pc[:].rearrange("p b n -> p (b n)"), ACT.Copy).then_inc(setup_a, 1)
            act.wait_ge(setup_v, 2)
            fn(lbt[:, 0:DEPTH, :], lbt[:, 0:DEPTH, :], ACT.Exp).then_inc(setup_a, 1)
            act.wait_ge(setup_v, 4)
            fn(cos[:], cos[:], ACT.Sin)
            fn(sin[:, :, 1, :], sin[:, :, 1, :], ACT.Sin).then_inc(setup_a, 1)

            with act.Fori(0, DEPTH) as lay:
                def need(name, k=1, per=1):
                    act.wait_ge(s[name], lay * per + k)

                def give(ins, name, k=1, per=1):
                    A.do(ins, s[name], lay * per + k)

                def core(name):
                    act.wait_ge(core_done, lay * NCORE + CORE_AT[name])

                def read(ins, name):
                    A.do(ins, core_read["a"], lay * READS["a"] + READ_AT["a"][name])

                def block_in(b):
                    act.wait_ge(block_done[b % 2], lay * (NBLK // 2) + b // 2 + 1)
                    return pb[:, 2 * (b % 2):2 * (b % 2) + 2, :]

                def block_out(ins, b):
                    A.do(ins, block_read[b % 2], lay * (NBLK // 2) + b // 2 + 2)

                def whole(dst, name):
                    core(name)
                    read(fn(dst[:].rearrange("p k t -> p (k t)"), pc[:].rearrange("p b n -> p (b n)"), ACT.Copy), name)

                def two(name):
                    core(name)
                    return pc[:, 0:2, :].rearrange("p b n -> p (b n)")

                def unit_hi(u):
                    act.wait_ge(raw_in[u % RAW], 16 * (lay * (LAYER_UNITS // RAW) + u // RAW + 1))
                    if u >= 2:
                        b = (u - 2) // 2
                        if u % 2 == 0:
                            act.wait_ge(half_done, lay * NBLK + b + 1)
                        else:
                            act.wait_ge(block_done[b % 2], lay * (NBLK // 2) + b // 2 + 1)
                    A.do(fn(whi_m[:, u % 2], raw[:, u % RAW], ACT.Copy), mix_hi, lay * MIX_UNITS + u + 1)

                def pre(b):
                    if b < NBLK - 1:
                        unit_hi(2 * b + 2)

                def post(b):
                    if b < NBLK - 1:
                        unit_hi(2 * b + 3)

                def around(b, step=None, mid=None):
                    pre(b)
                    if mid:
                        mid()
                    post(b)
                    if step:
                        step()

                def turn_parts(dst, name):
                    core(name)
                    for i in range(2):
                        ins = fn(dst[:, 4 * i:4 * i + 4, :].rearrange("p k t -> p (k t)"),
                                 pc[:, 2 * i:2 * i + 2, :].rearrange("p b n -> p (b n)"), ACT.Copy)
                        A.do(ins, turn_hi, (lay * len(TURNS) + TURNS.index(name)) * 2 + i + 1)
                    A.tell(core_read["a"])

                def conv_copy(b):
                    src = block_in(b).rearrange("p b (c t) -> p (b c) t", c=2)
                    block_out(fn(cin[:, :, CONV - 1:], src, ACT.Copy), b)

                def conv_act(i):
                    need("conv_out", i + 1, 4)
                    g = gqkv[:, 4 * i:4 * i + 4, :]
                    give(fn(g, g, ACT.Silu), "conv_silu", i + 1, 4)

                act.wait_ge(setup_v, 5)
                act.wait_ge(s["acc_done"], lay + 1)
                act.wait_ge(s["layer_open"], lay + 1)
                unit_hi(0)
                unit_hi(1)
                around(0, lambda: conv_copy(0))
                conv_act(0)
                around(1, lambda: conv_copy(1))
                conv_act(1)
                need("ba_raw")
                A.do(fn(small[:, 2, :], small[:, 2, :], ACT.Exp, scale=-1.0))
                A.do(fn(small[:, 4, :], small[:, 3, :], ACT.Abs))
                A.settle()
                A.do(fn(small[:, 4, :], small[:, 4, :], ACT.Exp, scale=-1.0))
                A.settle()
                A.do(fn(small[:, 4, :], small[:, 4, :], ACT.Ln, bias=1.0))
                give(fn(small[:, 5, 0:H], alog[:, :], ACT.Exp), "ba_exp")
                around(2, lambda: block_out(fn(hq.rearrange("p h t -> p (h t)"), block_in(2).rearrange("p b n -> p (b n)"),
                                               ACT.Copy, scale=KSCALE), 2))
                core("gnorm")
                read(fn(sq[:].rearrange("p k t -> p (k t)"), pc[:].rearrange("p b n -> p (b n)"), ACT.Ln, bias=eps[:, 0:1]), "gnorm")
                A.settle()
                give(fn(sq[:], sq[:], ACT.Exp, scale=-0.5), "lnexp_gn")
                around(3)
                need("hf_parts")
                A.do(fn(hg, hg, ACT.Exp))
                give(fn(he, he, ACT.Exp, scale=-1.0), "hf_exp")
                need("hf_den")
                A.do(fn(hg, hg, ACT.Ln))
                A.do(fn(hf, hf, ACT.Ln, bias=1.0))
                A.settle()
                give(fn(hk, hf, ACT.Exp, scale=-1.0), "hf_lns")
                around(4)
                core("grow")
                read(fn(y[:, 0, 0:512], pc[:, 1, :], ACT.Exp), "grow")
                need("dt_raw")
                give(fn(dt_[:], dt_[:], ACT.Exp), "dt_exp")
                around(5)

                def h_exp(l):
                    need("h_diff", l + 1, 8)
                    give(fn(he, he, ACT.Exp), "h_exp", l + 1, 8)

                def value_block(b, k):
                    src = block_in(b)
                    for t in range(TT):
                        ins = fn(val[:, t, k * 512:(k + 1) * 512], src[:, t, :], ACT.Copy)
                    block_out(ins, b)

                def inverse_x(l):
                    src = two(f"x{l}")
                    read(fn(xi[:].rearrange("p i t -> p (i t)"), src, ACT.Copy), f"x{l}")

                def activate(b, k, func):
                    block_out(fn(gt[:, k, :, :], block_in(b), func), b)

                def gate_sigmoid(i):
                    need("gate_raw", i + 1, 6)
                    give(fn(gates[i], gates[i], ACT.Sigmoid), "gate_out", i + 1, 6)

                def rms(name):
                    core(name)
                    for i in range(8):
                        src = pc[:, 2 * (i // 4) + (i % 4) // 2, (i % 2) * HV:(i % 2) * HV + HV]
                        ins = fn(y[:, i // 4, (i % 4) * HV:(i % 4) * HV + HV], src, ACT.Square, accum_out=ss[:, i:i + 1])
                    read(ins, name)
                    A.settle()
                    A.do(fn(ss[:, :], ss[:, :], ACT.Ln, scale=1.0 / HV, bias=eps[:, 0:1]))
                    A.settle()

                h_exp(0)
                need("rope_done", 2, 2)
                h_exp(1)
                around(6, lambda: value_block(6, 0))
                whole(yt, "rqkt")
                h_exp(2)
                around(7, lambda: value_block(7, 1))
                h_exp(3)
                around(8, mid=lambda: inverse_x(0))
                need("rvar")
                A.do(fn(rstd[:, :], rstd[:, :], ACT.Ln, bias=eps[:, 0:1]))
                A.settle()
                give(fn(rstd[:, :], rstd[:, :], ACT.Exp, scale=-0.5), "rrstd")
                around(9, lambda: activate(9, 0, ACT.Silu))
                h_exp(4)
                around(10, lambda: activate(10, 1, ACT.Silu))
                inverse_x(1)
                h_exp(5)
                gate_sigmoid(0)

                def hgrn_values():
                    need("y_done", 1, 3)
                    value_block(11, 0)

                around(11, hgrn_values)
                turn_parts(yth, "ryt")
                around(12, lambda: value_block(12, 1))
                inverse_x(2)
                h_exp(6)
                around(13)
                h_exp(7)
                around(14)
                inverse_x(3)
                gate_sigmoid(1)

                def h7_copy():
                    core("h7")
                    read(fn(atth2.rearrange("p h t -> p (h t)"), pc[:, 2, :], ACT.Copy), "h7")

                around(15, mid=h7_copy)
                need("h_fac", 8, 9)
                around(16, lambda: conv_copy(16))
                inverse_x(4)
                around(17, lambda: conv_copy(17), mid=lambda: conv_act(2))
                rms("hout")
                give(fn(rstd[:, :], ss[:, :], ACT.Exp, scale=-0.5), "rms_rstd", 1, 2)
                conv_act(3)
                around(18, lambda: activate(18, 0, ACT.Sigmoid))
                inverse_x(5)
                around(19, lambda: activate(19, 1, ACT.Sigmoid))
                around(20, mid=lambda: inverse_x(6))
                turn_parts(yth, "hyt")
                gate_sigmoid(2)
                around(21, lambda: activate(21, 0, ACT.Silu))
                around(22)
                around(23, mid=lambda: read(fn(vb[:, 0, :], two("vn0"), ACT.Copy), "vn0"))
                gate_sigmoid(3)
                around(24, mid=lambda: read(fn(state[:].rearrange("p i t -> p (i t)"), two("state"), ACT.Copy), "state"))
                around(25, lambda: activate(25, 1, ACT.Silu), mid=lambda: read(fn(vb[:, 1, :], two("vn1"), ACT.Copy), "vn1"))
                rms("gout")
                give(fn(rstd[:, :], ss[:, :], ACT.Exp, scale=-0.5), "rms_rstd", 2, 2)
                around(26)
                gate_sigmoid(4)
                around(27, mid=lambda: turn_parts(yth, "gyt"))
                gate_sigmoid(5)
                around(28)
                around(29)
                turn_parts(yth, "mt")
                around(30)

                def norm_scale(k):
                    need("ln_var", k, 2)
                    A.do(fn(rstd[:, 0:2], rstd[:, 0:2], ACT.Ln, bias=eps[:, 1:2]))
                    A.settle()
                    A.do(fn(rstd[:, 0:2], rstd[:, 0:2], ACT.Exp, scale=-0.5), s["ln_rstd"], lay * 2 + k)

                def hi(c, base, raw_base):
                    act.wait_ge(raw_in[c % RAW], raw_base + 16 * (c // RAW) + 16)
                    act.wait_ge(unit_done, base + c + 1)
                    A.do(fn(whi[:, c % SPLIT], raw[:, c % RAW], ACT.Copy), split_hi, base + c + 1)

                norm_scale(1)
                for b in range(2):
                    act.wait_ge(block_done[b], (lay + 1) * (NBLK // 2))
                for c in range(SPLIT):
                    hi(c, lay * 2 * PASS_UNITS, (lay * (LAYER_UNITS // RAW) + MIX_UNITS // RAW) * 16)
                turn_parts(xth, "x1t")
                need("x_ready", 1, 2)
                give(fn(xh[:], x[:], ACT.Copy), "xh_ready")
                need("logits")
                give(fn(scores[:], scores[:], ACT.Sigmoid), "score_out")

                def expert_pass(p):
                    def gathered(n, j):
                        act.wait_ge(se["gh_done"], n + 1)
                        A.do(fn(xgh[:, j].rearrange("p k t -> p (k t)"), pc[:, 2:4, :].rearrange("p b n -> p (b n)"), ACT.Copy),
                             se["xgh_ready"], n + 1)

                    def expert(n, base, raw_base, j, last_=False):
                        g = EXP_UNITS * j
                        act.wait_ge(unit_done, base + g + 2 + CREDIT)
                        A.do(fn(hs[:, :], pc[:, 0, :], ACT.Silu), se["silu_h"], n + 1)
                        hi(g + 5, base, raw_base)
                        if not last_:
                            gathered(n + 1, 1 - j)
                            hi(g + 6, base, raw_base)
                            hi(g + 7, base, raw_base)
                        act.wait_ge(se["turned"], n + 1)
                        A.do(fn(hth[:].rearrange("p k t -> p (k t)"), pc[:, 0, :], ACT.Copy), se["hth_ready"], n + 1)
                        if not last_:
                            hi(g + 8, base, raw_base)
                        act.wait_ge(unit_done, base + g + 6 + CREDIT)
                        act.wait_ge(se["pickt_ready"], n + 1)
                        A.do(fn(yh[:, :], pc[:, 2:4, :].rearrange("p b n -> p (b n)"), ACT.Copy, scale=cslot[:, j:j + 1]),
                             se["yh_ready"], n + 1)
                        if not last_:
                            hi(g + 9, base, raw_base)
                            hi(g + 10, base, raw_base)

                    n0 = (lay * 2 + p) * NE
                    u0 = (lay * 2 + p) * PASS_UNITS
                    r0 = (lay * (LAYER_UNITS // RAW) + (MIX_UNITS + p * PASS_UNITS) // RAW) * 16
                    if p:
                        for c in range(SPLIT):
                            hi(c, u0, r0)
                    gathered(n0, 0)
                    hi(SPLIT, u0, r0)
                    with act.Fori(0, NE // 2 - 1) as it:
                        for j in range(2):
                            expert(n0 + it * 2 + j, u0 + it * 2 * EXP_UNITS, r0 + it * (32 * EXP_UNITS // RAW), j)
                    expert(n0 + NE - 2, u0 + (NE - 2) * EXP_UNITS, r0 + (NE - 2) * EXP_UNITS // RAW * 16, 0)
                    expert(n0 + NE - 1, u0 + (NE - 2) * EXP_UNITS, r0 + (NE - 2) * EXP_UNITS // RAW * 16, 1, last_=True)

                expert_pass(0)
                act.wait_ge(flag_ready, lay + 1)
                act.sem_inc(held["act"], 1)
                spill = act.value_load(flag[0:1, 0:1], min_val=0, max_val=1)
                with act.If(spill > 0):
                    expert_pass(1)
                with act.Else():
                    act.wait_ge(se["yh_ready"], (lay * 2 + 1) * NE)
                    act.sem_inc(split_hi, PASS_UNITS)
                    for name in ("xgh_ready", "silu_h", "hth_ready", "yh_ready"):
                        act.sem_inc(se[name], NE)
                norm_scale(2)
                turn_parts(xth, "x2t")
                A.restart()

        @block.vector
        def _(dve):
            V = Engine(dve, chain_v, held["dve"])
            v = nc.vector
            tt, ts, stt, cp = v.tensor_tensor, v.tensor_scalar, v.scalar_tensor_tensor, v.tensor_copy

            V.do(v.memset(ones[:], 1.0))
            V.do(v.memset(eps[:, 0:1], 1e-6))
            V.do(v.memset(eps[:, 1:2], 1e-5))
            V.tell(setup_v)
            dve.wait_ge(consts_in, 16 * CONST_DMAS)
            V.do(cp(rwh[:], rw[:]))
            V.settle()
            V.do(tt(rwl[:], rw[:], rwh[:].bitcast(F32), ALU.subtract))
            dve.wait_ge(setup_a, 1)
            top = lbt[:, 2, :]
            V.do(cp(top, lbc[:, 0, :]))
            for l in range(1, DEPTH):
                V.settle()
                V.do(tt(top, top, lbc[:, l, :], ALU.max))
            V.settle()
            for l in range(DEPTH):
                ins = tt(lbt[:, l, :], lbc[:, l, :], top, ALU.subtract)
                V.do(ins) if l < DEPTH - 1 else V.do(ins, setup_v, 2)
            dve.wait_ge(setup_a, 3)
            V.do(cp(top, lbt[:, 0, :]))
            for l in range(1, DEPTH):
                V.settle()
                V.do(tt(top, top, lbt[:, l, :], ALU.add))
            V.settle()
            V.do(v.reciprocal(top, top))
            V.settle()
            for l in range(DEPTH):
                V.do(tt(lbt[:, l, :], lbt[:, l, :], top, ALU.mult))
            V.settle()
            for l in range(1, DEPTH):
                V.do(tt(lbt[:, l, :], lbt[:, l, :], lbt[:, l - 1, :], ALU.add))
                V.settle()
            for l in range(DEPTH):
                V.do(tt(lb[:, l, :], lbt[:, l, :], lbt[:, 0, :], ALU.subtract))
            V.settle()
            V.do(ts(omlb[:], lb[:], -1.0, 1.0, ALU.mult, ALU.add))
            V.do(cp(mask[:], mask32[:]))
            V.do(cp(maskt[:], maskt32[:]))
            V.do(cp(eyeb[:], eyeb32[:]))
            V.do(cp(posf[:], posi[:]))
            V.settle()
            for t in range(TT):
                V.do(ts(ang[:, t, :], invf[:, :], posf[:, t:t + 1], None, ALU.mult))
            V.settle()
            magic, two_pi_hi = 12582912.0, 6.28125
            two_pi_lo = 2 * np.pi - two_pi_hi
            for quarter, dst in ((0.25, cos[:]), (0.0, sin[:, :, 1, :])):
                V.do(ts(turns[:], ang[:], float(1 / (2 * np.pi)), quarter, ALU.mult, ALU.add))
                V.settle()
                V.do(ts(turns[:], turns[:], magic, None, ALU.add))
                V.settle()
                V.do(ts(turns[:], turns[:], magic, None, ALU.subtract))
                V.settle()
                V.do(stt(dst, turns[:], -two_pi_hi, ang[:], ALU.mult, ALU.add))
                V.settle()
                V.do(stt(dst, turns[:], -float(two_pi_lo), dst, ALU.mult, ALU.add))
                V.settle()
                V.do(ts(dst, dst, float(quarter * 2 * np.pi), 3.1415925, ALU.add, ALU.min))
                V.settle()
                V.do(ts(dst, dst, -3.1415925, None, ALU.max), setup_v, 3 if quarter else 4)
            dve.wait_ge(setup_a, 4)
            V.do(ts(sin[:, :, 0, :], sin[:, :, 1, :], -1.0, None, ALU.mult), s["acc_done"], 1)
            V.tell(setup_v)
            V.do(tt(xtl[:].rearrange("p k t -> p (k t)"), pc[:].rearrange("p b n -> p (b n)"),
                    xth[:].bitcast(F32).rearrange("p k t -> p (k t)"), ALU.subtract), setup_v, 6)
            V.tell(s["layer_open"])
            V.restart()

            with dve.Fori(0, DEPTH) as lay:
                def need(name, k=1, per=1):
                    dve.wait_ge(s[name], lay * per + k)

                def give(ins, name, k=1, per=1):
                    V.do(ins, s[name], lay * per + k)

                def core(name):
                    dve.wait_ge(core_done, lay * NCORE + CORE_AT[name])

                def read(ins, name):
                    V.do(ins, core_read["v"], lay * READS["v"] + READ_AT["v"][name])

                def block_in(b):
                    dve.wait_ge(block_done[b % 2], lay * (NBLK // 2) + b // 2 + 1)
                    return pb[:, 2 * (b % 2):2 * (b % 2) + 2, :]

                def block_out(ins, b):
                    V.do(ins, block_read[b % 2], lay * (NBLK // 2) + b // 2 + 2)

                def unit_lo(u):
                    dve.wait_ge(mix_hi, lay * MIX_UNITS + u + 1)
                    V.do(tt(wlo_m[:, u % 2], raw[:, u % RAW], whi_m[:, u % 2].bitcast(F32), ALU.subtract), mix_lo,
                         lay * MIX_UNITS + u + 1)

                def pre(b):
                    if b < NBLK - 1:
                        unit_lo(2 * b + 2)

                def post(b):
                    if b < NBLK - 1:
                        unit_lo(2 * b + 3)

                def around(b, step=None, mid=None, after=None):
                    pre(b)
                    if mid:
                        mid()
                    if step:
                        step()
                    post(b)
                    if after:
                        after()

                def turn_parts(dst, hi, name):
                    core(name)
                    for i in range(2):
                        dve.wait_ge(turn_hi, (lay * len(TURNS) + TURNS.index(name)) * 2 + i + 1)
                        ins = tt(dst[:, 4 * i:4 * i + 4, :].rearrange("p k t -> p (k t)"),
                                 pc[:, 2 * i:2 * i + 2, :].rearrange("p b n -> p (b n)"),
                                 hi[:, 4 * i:4 * i + 4, :].bitcast(F32).rearrange("p k t -> p (k t)"), ALU.subtract)
                        V.do(ins) if i == 0 else read(ins, name)

                def conv(b, i):
                    dve.wait_ge(block_read[b % 2], lay * (NBLK // 2) + b // 2 + 2)
                    for j in range(CONV):
                        for c in range(4):
                            ch = 4 * i + c
                            src, dst, w = cin[:, c, j:j + T], gqkv[:, ch, :], cw[:, j, ch:ch + 1]
                            ins = ts(dst, src, w, None, ALU.mult) if j == 0 else stt(dst, src, w, dst, ALU.mult, ALU.add)
                        if j < CONV - 1:
                            V.do(ins)
                            V.settle()
                        else:
                            give(ins, "conv_out", i + 1, 4)

                dve.wait_ge(s["acc_done"], lay + 1)
                V.do(cp(lbl[:], lb[:, lay, :]))
                V.do(cp(omlbl[:], omlb[:, lay, :]))
                V.do(v.memset(cin[:, :, 0:CONV - 1], 0.0))
                unit_lo(0)
                unit_lo(1)
                core("conv_w")
                read(cp(cw[:].rearrange("p j c -> p (j c)"), pc[:, 0, 0:64]), "conv_w")
                V.do(cp(wbah[:], wba[:]))
                V.settle()
                give(tt(wbal[:], wba[:], wbah[:].bitcast(F32), ALU.subtract), "wba_ready")
                around(0, lambda: conv(0, 0))
                around(1, lambda: conv(1, 1))
                core("ba")
                part = lambda i: small[:, i, :].rearrange("p (t h) -> p t h", t=TT)
                bah = pc[:, 0, 0:16].rearrange("p (t n) -> p t n", t=TT)
                V.do(cp(part(2), bah[:, :, 0:H]))
                read(tt(part(3), bah[:, :, H:2 * H], mcast(dtb, TT), ALU.add), "ba")
                V.settle()
                give(ts(small[:, 6, :], small[:, 3, :], 0.0, None, ALU.max), "ba_raw")
                need("conv_silu", 2, 4)
                give(tt(sq[:], gqkv[:, 0:8, :], gqkv[:, 0:8, :], ALU.mult), "sq_ready")
                around(2)
                need("ba_exp")
                V.do(ts(small[:, 1, :], small[:, 2, :], 1.0, None, ALU.add))
                V.do(tt(small[:, 6, :], small[:, 6, :], small[:, 4, :], ALU.add))
                V.settle()
                V.do(v.reciprocal(small[:, 1, :], small[:, 1, :]))
                V.settle()
                V.do(ts(small[:, 7, :], small[:, 1, :], -1.0, None, ALU.mult))
                give(stt(part(0), part(6), -1.0, small[:, 5, None, 0:H].to_broadcast([P, TT, H]), ALU.mult, ALU.mult), "beta_g")

                def forget():
                    src = block_in(3).rearrange("p b (h t) -> p (b h) t", h=2)
                    V.do(ts(hg, src, 0.0, None, ALU.min))
                    block_out(ts(he, src, 0.0, None, ALU.max), 3)
                    V.tell(s["hf_parts"])

                around(3, forget)
                need("lnexp_gn")
                V.do(stt(gqkv[:, 0:4, :], gqkv[:, 0:4, :], KSCALE, sq[:, 0:4, :], ALU.mult, ALU.mult))
                give(tt(gqkv[:, 4:8, :], gqkv[:, 4:8, :], sq[:, 4:8, :], ALU.mult), "qk_normed")
                need("hf_exp")
                V.do(tt(hf, hg, he, ALU.mult))
                V.settle()
                for h in range(H):
                    V.do(stt(hg[:, h, :], he[:, h, :], lbl[:, h:h + 1], hg[:, h, :], ALU.mult, ALU.add))
                V.settle()
                give(ts(hg, hg, TINY, None, ALU.max), "hf_den")
                core("gcol")
                read(cp(small[:, 2, :], pc[:, 0, 0:8]), "gcol")
                V.settle()
                need("hf_lns")
                for h in range(H):
                    V.do(stt(hk[:, h, :], hk[:, h, :], omlbl[:, h:h + 1], he[:, h, :], ALU.mult, ALU.mult))
                V.do(tt(hf, hg, hf, ALU.subtract))
                V.settle()
                for i in range(8):
                    h, t = i // 2, i % 2
                    V.do(v.tensor_tensor_scan(hg[:, h, t * P:(t + 1) * P], ones[:, :], hf[:, h, t * P:(t + 1) * P], 0.0, ALU.mult, ALU.add))
                V.settle()

                def rope(b, i):
                    src = block_in(b).rearrange("p t (h s e) -> p t h s e", h=H, s=2)
                    half = rqk[:, :, i * 512:(i + 1) * 512]
                    dst = half.rearrange("p t (h s e) -> p t h s e", h=H, s=2)
                    tmp = gt[:, 0, :, :].rearrange("p t (h s e) -> p t h s e", h=H, s=2)
                    for t in range(TT):
                        for sd in range(2):
                            V.do(tt(tmp[:, t, :, sd, :], src[:, t, :, 1 - sd, :], mcast(sin[:, t, sd, :], H), ALU.mult))
                            V.do(tt(dst[:, t, :, sd, :], src[:, t, :, sd, :], mcast(cos[:, t, :], H), ALU.mult))
                    V.tell(block_read[b % 2])
                    V.do(tt(half, half, gt[:, 0, :, :], ALU.add), s["rope_done"], lay * 2 + i + 1)
                    V.settle()

                around(4, lambda: rope(4, 0))
                core("grow")
                V.do(stt(at[:], pc[:, 2:4, :].rearrange("p b (h t) -> p (b h) t", h=H), -1.0, mcast(strict, 8), ALU.mult, ALU.mult))
                for i in range(8):
                    if i == 4:
                        dve.wait_ge(core_read["a"], lay * READS["a"] + READ_AT["a"]["grow"])
                    ins = ts(dt_[:, i, :], pc[:, i // 4, (i % 4) * P:(i % 4) * P + P], small[:, 2, i:i + 1], 0.0, ALU.subtract, ALU.min)
                    V.do(ins) if i < 7 else read(ins, "grow")
                V.tell(s["dt_raw"])
                around(5, lambda: rope(5, 1))
                need("dt_exp")
                V.do(tt(dt_[:], dt_[:], mcast(upper, 8), ALU.mult))
                V.settle()
                V.do(tt(at[:], at[:], dt_[:], ALU.mult))
                V.do(cp(ti[:], mcast(eye, 8)))
                V.do(cp(ui[:], mcast(eye, 8)))
                core("gkt")
                for h in range(H):
                    ins = ts(kd[:, h, :], pc[:, 0, h * P:(h + 1) * P], dt_[:, h, P - 1:P], None, ALU.mult)
                    V.do(ins) if h < H - 1 else read(ins, "gkt")

                def h_halves(l):
                    w = 2 ** l
                    return [ap.rearrange("p h (b s) -> p (h b) s", s=2 * w) for ap in (hg, he, hf, hk, hq)] + [w]

                def h_differences(l):
                    V.settle()
                    g, e, _, _, _, w = h_halves(l)
                    mid = g[:, :, w - 1:w].to_broadcast([P, g.shape[1], w])
                    V.do(tt(e[:, :, 0:w], mid, g[:, :, 0:w], ALU.subtract))
                    if l < 7:
                        V.do(tt(e[:, :, w:2 * w], g[:, :, w:2 * w], mid, ALU.subtract))
                    else:
                        V.do(cp(e[:, :, w:2 * w], g[:, :, w:2 * w]))
                    V.tell(s["h_diff"])

                def h_factors(l):
                    if l < 8:
                        _, e, f, kk, qq, w = h_halves(l)
                        need("h_exp", l + 1, 8)
                        if l:
                            core(f"h{l - 1}")
                        V.do(tt(f[:, :, 0:w], e[:, :, 0:w], kk[:, :, 0:w], ALU.mult))
                        give(tt(f[:, :, w:2 * w], e[:, :, w:2 * w], qq[:, :, w:2 * w], ALU.mult), "h_fac", l + 1, 9)
                        if l < 7:
                            h_differences(l + 1)
                    else:
                        V.tell(s["h_fac"])

                def h_read(l):
                    if l == 7:
                        return
                    core(f"h{l}")
                    V.hold()
                    mk = mcast(eyeb, 8) if l == 8 else mcast(maskt[:, l, :], 8)
                    read(v.copy_predicated(atth[:], mk, pc[:, 2:4, :].rearrange("p b (h t) -> p (b h) t", h=H)), f"h{l}")

                def inverse_read(l):
                    core(f"yz{l}")
                    V.hold()
                    if l < LEVELS - 1:
                        V.do(v.copy_predicated(ti[:], mcast(mask[:, l, :], 8), pc[:, 0:2, :].rearrange("p b (h t) -> p (b h) t", h=H)))
                    read(v.copy_predicated(ui[:], mcast(maskt[:, l, :], 8), pc[:, 2:4, :].rearrange("p b (h t) -> p (b h) t", h=H)), f"yz{l}")
                    V.settle()
                    V.tell(s["level_t"])

                def gate_bias(i, b):
                    src = block_in(b)
                    dve.wait_ge(mbias_in, 16 * (lay * 6 + i + 1))
                    V.do(tt(gates[i], src, mcast(mbias, TT), ALU.add), s["gate_raw"], lay * 6 + i + 1)
                    V.tell(block_read[b % 2])

                def merge(i, b, k):
                    src = block_in(b)
                    need("gate_out", i + 1, 6)
                    mg = merged[:, :, k * 512:(k + 1) * 512]
                    if i < 2:
                        V.do(tt(mg, src, gates[i], ALU.mult), s["merged_ready"], lay * 6 + i + 1)
                        V.tell(block_read[b % 2])
                    else:
                        block_out(tt(gates[i], src, gates[i], ALU.mult), b)
                        V.settle()
                        V.do(tt(mg, mg, gates[i], ALU.add), s["merged_ready"], lay * 6 + i + 1)
                    V.settle()

                def gated(i, b0, b1):
                    for b in (b0, b1):
                        dve.wait_ge(block_read[b % 2], lay * (NBLK // 2) + b // 2 + 2)
                    V.settle()
                    for k in range(2):
                        yy = y[:, :, k * 512:(k + 1) * 512]
                        ins = tt(yy, yy, gt[:, k, :, :], ALU.mult)
                        V.do(ins) if k == 0 else give(ins, "y_done", i, 3)

                def rms_scale(name, k):
                    need("rms_rstd", k, 2)
                    dve.wait_ge(gain_in, 16 * (lay * 2 + k))
                    for i in range(8):
                        src = pc[:, 2 * (i // 4) + (i % 4) // 2, (i % 2) * HV:(i % 2) * HV + HV]
                        ins = stt(y[:, i // 4, (i % 4) * HV:(i % 4) * HV + HV], src, rstd[:, i:i + 1], gain[:, :], ALU.mult, ALU.mult)
                        V.do(ins) if i < 7 else read(ins, name)

                V.do(v.memset(atth[:], 0.0))
                h_differences(0)
                h_factors(0)
                around(6)
                h_read(0)
                h_factors(1)
                around(7)
                core("rqk")
                V.do(tt(attr, pc[:, 0:2, :].rearrange("p b (h t) -> p (b h) t", h=2), decay, ALU.mult))
                read(tt(attr2, pc[:, 2, :].rearrange("p (h t) -> p h t", h=H), decay[:, :, 0:P], ALU.mult), "rqk")
                core("gkk")
                V.do(tt(attg[:], pc[:, 2:4, :].rearrange("p b (h t) -> p (b h) t", h=H), dt_[:], ALU.mult))
                read(tt(at[:], pc[:, 0:2, :].rearrange("p b (h t) -> p (b h) t", h=H), at[:], ALU.mult), "gkk")
                V.tell(s["gkk_in"])
                h_read(1)
                for i in range(2):
                    g = gqkv[:, 4 * i:4 * i + 4, P:T]
                    V.do(tt(g, g, erow, ALU.mult))
                V.settle()
                h_factors(2)
                around(8, lambda: gate_bias(0, 8))
                core("rout")
                for i in range(8):
                    src = pc[:, 2 * (i // 4) + (i % 4) // 2, (i % 2) * HV:(i % 2) * HV + HV]
                    V.do(v.bn_stats(stats[:, i, 0:6], src))
                V.settle()
                for i in range(8):
                    V.do(v.bn_aggr(mv[:, i, :], stats[:, i, 0:6]))
                V.settle()
                give(cp(rstd[:, :], mv[:, :, 1]), "rvar")
                need("rrstd")
                for i in range(8):
                    src = pc[:, 2 * (i // 4) + (i % 4) // 2, (i % 2) * HV:(i % 2) * HV + HV]
                    ins = ts(y[:, i // 4, (i % 4) * HV:(i % 4) * HV + HV], src, mv[:, i, 0:1], rstd[:, i:i + 1], ALU.subtract, ALU.mult)
                    V.do(ins) if i < 7 else read(ins, "rout")

                def h_step(l):
                    h_read(l)
                    h_factors(l + 1)

                around(9, mid=lambda: h_step(2))
                inverse_read(0)
                around(10, mid=lambda: h_step(3))
                gated(1, 9, 10)
                around(11, mid=lambda: inverse_read(1))
                turn_parts(ytl, yth, "ryt")
                around(12, mid=lambda: h_step(4))
                around(13, lambda: merge(0, 13, 0), mid=lambda: h_step(5))
                inverse_read(2)
                around(14, lambda: gate_bias(1, 14), mid=lambda: h_step(6))
                V.settle()
                V.do(v.memset(cin[:, :, 0:CONV - 1], 0.0))
                around(15, lambda: merge(1, 15, 1), mid=lambda: h_factors(8))
                inverse_read(3)
                around(16, mid=lambda: h_read(8), after=lambda: conv(16, 2))
                around(17, mid=lambda: inverse_read(4))
                core("hout")
                conv(17, 3)
                rms_scale("hout", 1)
                around(18)
                around(19, mid=lambda: inverse_read(5))
                gated(2, 18, 19)
                around(20, lambda: gate_bias(2, 20))
                turn_parts(ytl, yth, "hyt")
                around(21, mid=lambda: inverse_read(6))
                core("gvt")
                for i in range(8):
                    t, h = i // 4, i % 4
                    ins = ts(vb[:, t, h * HV:(h + 1) * HV], pc[:, 2 * t + h // 2, (h % 2) * HV:(h % 2) * HV + HV],
                             small[:, 1, i:i + 1], None, ALU.mult)
                    V.do(ins) if i < 7 else read(ins, "gvt")
                around(22, lambda: merge(2, 22, 0))
                around(23, lambda: gate_bias(3, 23))
                around(24, lambda: merge(3, 24, 1))
                core("ks")
                for h in range(H):
                    vv = vb[:, 1, h * HV:(h + 1) * HV]
                    ins = stt(vv, pc[:, h // 2, (h % 2) * HV:(h % 2) * HV + HV], small[:, 7, 4 + h:5 + h], vv, ALU.mult, ALU.add)
                    V.do(ins) if h < H - 1 else read(ins, "ks")
                around(25)
                rms_scale("gout", 2)
                gated(3, 21, 25)
                around(26, lambda: gate_bias(4, 26))
                around(27, lambda: gate_bias(5, 27), mid=lambda: turn_parts(ytl, yth, "gyt"))
                around(28, lambda: merge(4, 28, 0))
                around(29, lambda: merge(5, 29, 1))
                turn_parts(ytl, yth, "mt")

                def residual(b, k):
                    src = block_in(b)
                    xx = x[:, :, k * 512:(k + 1) * 512]
                    block_out(stt(xx, xx, ALPHA, src, ALU.mult, ALU.add), b)

                def layer_norm(k, gains, biases):
                    V.settle()
                    for t in range(TT):
                        for c in range(2):
                            V.do(v.bn_stats(stats[:, t, 6 * c:6 * c + 6], x[:, t, 512 * c:512 * c + 512]))
                    V.settle()
                    for t in range(TT):
                        V.do(v.bn_aggr(mv[:, t, :], stats[:, t, :]))
                    V.settle()
                    give(cp(rstd[:, 0:2], mv[:, 0:2, 1]), "ln_var", k, 2)
                    dve.wait_ge(s["ln_rstd"], lay * 2 + k)
                    for t in range(TT):
                        V.do(ts(x[:, t, :], x[:, t, :], mv[:, t, 0:1], rstd[:, t:t + 1], ALU.subtract, ALU.mult))
                    V.settle()
                    dve.wait_ge(ln_in, 64 * lay + 32 * k)
                    V.do(tt(x[:], x[:], mcast(gains, TT), ALU.mult))
                    V.settle()
                    give(tt(x[:], x[:], mcast(biases, TT), ALU.add), "x_ready", k, 2)

                around(30, lambda: residual(30, 0))
                residual(31, 1)
                def lo(c, base):
                    dve.wait_ge(split_hi, base + c + 1)
                    V.do(tt(wlo[:, c % SPLIT], raw[:, c % RAW], whi[:, c % SPLIT].bitcast(F32), ALU.subtract), split_lo,
                         base + c + 1 + CREDIT)

                layer_norm(1, lng1, lnb1)
                for c in range(2):
                    lo(c, lay * 2 * PASS_UNITS)
                turn_parts(xtl, xth, "x1t")

                need("xh_ready")
                V.do(tt(xl[:], x[:], xh[:].bitcast(F32), ALU.subtract))
                for c in range(2, SPLIT):
                    lo(c, lay * 2 * PASS_UNITS)
                core("router")
                read(cp(scores[:].rearrange("p t e -> p (t e)"), pc[:, 0, 0:TT * NE]), "router")
                V.settle()
                V.tell(s["logits"])
                need("score_out")
                V.do(tt(biased[:], scores[:], mcast(rb, TT), ALU.add))
                V.settle()

                def ranks(dst, vals, groups, width):
                    vv = vals.rearrange("p t (g j) -> p (t g) j", j=width)
                    other = vv[:, :, None, :].to_broadcast([P, groups, width, width])
                    own = vv[:, :, :, None].to_broadcast([P, groups, width, width])
                    c, q = cmp[:, 0:groups], eq[:, 0:groups]
                    V.do(tt(c, other, own, ALU.is_gt))
                    V.do(tt(q, other, own, ALU.is_equal))
                    V.settle()
                    V.do(tt(q, q, tie[:, None, :, :].to_broadcast([P, groups, EG, EG]), ALU.mult))
                    V.settle()
                    V.do(tt(c, c, q, ALU.add))
                    V.settle()
                    V.do(v.tensor_reduce(dst.rearrange("p t (g i) -> p (t g) i", i=width), c, AX.X, ALU.add))
                    V.settle()

                ranks(rank[:], biased[:], TT * NG, EG)
                V.do(ts(rank[:], rank[:], 2.0, None, ALU.is_lt))
                V.settle()
                V.do(tt(chosen[:], biased[:], rank[:], ALU.mult))
                V.settle()
                V.do(v.tensor_reduce(gsum[:], chosen[:].rearrange("p t (g j) -> p t g j", j=EG), AX.X, ALU.add))
                V.settle()
                ranks(best[:], gsum[:], TT, NG)
                V.do(ts(best[:], best[:], 1.0, None, ALU.is_lt))
                V.settle()
                give(tt(chosen[:].rearrange("p t (g j) -> p (t g) j", j=EG), rank[:].rearrange("p t (g j) -> p (t g) j", j=EG),
                        best[:].rearrange("p t g -> p (t g)")[:, :, None].to_broadcast([P, TT * NG, EG]), ALU.mult), "chosen_ready")
                V.settle()
                V.do(tt(comb[:], scores[:], chosen[:], ALU.mult))
                V.settle()
                V.do(v.tensor_reduce(wsum[:, :, 0], comb[:], AX.X, ALU.add))
                V.settle()
                V.do(v.reciprocal(wsum[:, :, 1], wsum[:, :, 0]))
                V.settle()
                for t in range(TT):
                    V.do(ts(comb[:, t, :], comb[:, t, :], wsum[:, t, 1:2], None, ALU.mult))
                core("pos")
                V.do(v.tensor_reduce(wsum[:, 0, 0:1], pc[:, 0, 2 * NE:3 * NE], AX.X, ALU.max))
                read(stt(posm[:].rearrange("p t e -> p (t e)"), pc[:, 0, 0:TT * NE], 1.0, chosen[:].rearrange("p t e -> p (t e)"),
                         ALU.add, ALU.mult), "pos")
                V.settle()
                V.do(ts(posm[:], posm[:], -1.0, None, ALU.add))
                V.do(ts(flag[:], wsum[:, 0, 0:1], float(P), None, ALU.is_gt), flag_ready, lay + 1)
                V.settle()
                V.tell(s["moe_ready"])

                def expert_pass(p):
                    def choose(n, j, e):
                        V.do(cp(pcol[:, j, :], posm[:, :, e]))
                        V.do(cp(ccol[:, j, :], comb[:, :, e]))
                        V.settle()
                        for t in range(TT):
                            ins = ts(pick[:, j, t, :], iota[:, p * P:(p + 1) * P], pcol[:, j, t:t + 1], None, ALU.is_equal)
                            V.do(ins) if t == 0 else V.do(ins, se["pick_ready"], n + 1)

                    def gathered(n, j):
                        dve.wait_ge(se["gl_done"], n + 1)
                        V.do(cp(xgl[:, j].rearrange("p k t -> p (k t)"), pc[:, 2:4, :].rearrange("p b n -> p (b n)")), se["xgl_ready"], n + 1)

                    def expert(n, base, j, e=None, last_=False):
                        g = EXP_UNITS * j
                        V.n = 0
                        lo(g + 5, base)
                        dve.wait_ge(unit_done, base + g + 4 + CREDIT)
                        dve.wait_ge(se["silu_h"], n + 1)
                        V.do(tt(hs[:, :], hs[:, :], pc[:, 1, :], ALU.mult), se["h_ready"], n + 1)
                        if not last_:
                            gathered(n + 1, 1 - j)
                        dve.wait_ge(se["turned"], n + 1)
                        V.do(cp(cslot[:, j:j + 1], pc[:, 1, T:T + 1]))
                        V.do(cp(pickt[:, j, :], pc[:, 1, 0:T]), se["pickt_ready"], n + 1)
                        dve.wait_ge(se["hth_ready"], n + 1)
                        V.do(tt(htl[:].rearrange("p k t -> p (k t)"), pc[:, 0, :], hth[:].bitcast(F32).rearrange("p k t -> p (k t)"), ALU.subtract),
                             se["htl_ready"], n + 1)
                        if not last_:
                            for c in range(6, 9):
                                lo(g + c, base)
                        dve.wait_ge(se["yh_ready"], n + 1)
                        V.do(stt(yl[:, :], pc[:, 2:4, :].rearrange("p b n -> p (b n)"), cslot[:, j:j + 1], yh[:, :].bitcast(F32),
                                 ALU.mult, ALU.subtract), se["yl_ready"], n + 1)
                        if e is not None:
                            choose(n + 2, j, e)
                        if not last_:
                            for c in range(9, 11):
                                lo(g + c, base)
                        V.settle()
                        V.hold()
                        dve.sem_clear(chain_v)

                    n0 = (lay * 2 + p) * NE
                    u0 = (lay * 2 + p) * PASS_UNITS
                    V.restart()
                    dve.wait_ge(iota_in, 16 * lay + 16)
                    choose(n0, 0, 0)
                    choose(n0 + 1, 1, 1)
                    if p:
                        for c in range(SPLIT):
                            lo(c, u0)
                    gathered(n0, 0)
                    lo(SPLIT, u0)
                    V.settle()
                    V.hold()
                    dve.sem_clear(chain_v)
                    with dve.Fori(0, NE // 2 - 1) as it:
                        for j in range(2):
                            expert(n0 + it * 2 + j, u0 + it * 2 * EXP_UNITS, j, e=2 * it + j + 2)
                    expert(n0 + NE - 2, u0 + (NE - 2) * EXP_UNITS, 0)
                    expert(n0 + NE - 1, u0 + (NE - 2) * EXP_UNITS, 1, last_=True)
                    V.n = 0

                expert_pass(0)
                dve.wait_ge(flag_ready, lay + 1)
                V.hold()
                spill = dve.value_load(flag[0:1, 0:1], min_val=0, max_val=1)
                with dve.If(spill > 0):
                    expert_pass(1)
                with dve.Else():
                    dve.wait_ge(se["yl_ready"], (lay * 2 + 1) * NE)
                    dve.sem_inc(split_lo, PASS_UNITS)
                    for name in ("pick_ready", "xgl_ready", "h_ready", "pickt_ready", "htl_ready", "yl_ready"):
                        dve.sem_inc(se[name], NE)
                V.last = (se["yl_ready"], (lay * 2 + 2) * NE)
                dve.wait_ge(s["acc_done"], lay + 2)
                for t in range(TT):
                    V.do(stt(x[:, t, :], x[:, t, :], ALPHA, pb[:, 2 * t:2 * t + 2, :].rearrange("p b n -> p (b n)"), ALU.mult, ALU.add))
                layer_norm(2, lng2, lnb2)
                turn_parts(xtl, xth, "x2t")
                V.settle()
                V.tell(s["layer_open"])
                V.restart()


INPUTS = ["x", "positions", "w_in", "gdn_conv_w", "gdn_a_log", "gdn_dt_bias", "gdn_norm_g", "hgrn_lb", "hgrn_norm_g",
          "merge_b", "w_branch", "w_out", "ln1_g", "ln1_b", "router_w", "router_b", "moe_w_gate", "moe_w_up",
          "moe_w_down", "ln2_g", "ln2_b"]


def kernel(**inputs):
    import concourse.bacc as bacc
    from concourse.bass_utils import run_bass_kernel_spmd

    nc = bacc.Bacc("TRN2", target_bir_lowering=False, num_devices=1)
    tables = constants()
    arrays, args = {}, []
    for name in INPUTS + CONSTS:
        a = np.ascontiguousarray(inputs[name] if name in inputs else tables[name])
        arrays[f"in_{name}"] = a
        args.append(nc.dram_tensor(f"in_{name}", a.shape, mybir.dt.from_np(a.dtype), kind="ExternalInput").ap())
    args.append(nc.dram_tensor("decoded", (1, T, D), F32, kind="ExternalOutput").ap())
    build_decoder(nc, *args)
    result = run_bass_kernel_spmd(nc, [arrays], core_ids=[0])
    return result.results[0]["decoded"]
```

```python
from contextlib import ExitStack

import numpy as np
import concourse.bass as bass
from concourse import mybir

F32 = mybir.dt.float32
F32R = mybir.dt.float32r
I32 = mybir.dt.int32
U8 = mybir.dt.uint8
ALU = mybir.AluOpType
ACT = mybir.ActivationFunctionType
AX = mybir.AxisListType

P = 128
D = 1024
T = 256
DEPTH = 2
H = 4
HK = 128
HV = 256
NE = 16
NG = 4
EG = 4
CONV = 4
DX = 512
KD = D // P
TT = T // P
ALPHA = (2 * DEPTH) ** 0.25
KSCALE = HK ** -0.5
LEVELS = 7
TINY = 2.0 ** -60

C_RQ, C_RK, C_RV, C_RG, C_GQKV = 0, 512, 1024, 2048, 3072
C_GZ, C_GB, C_HQ, C_HF, C_HI, C_HG, C_MG = 5120, 6144, 6152, 6664, 7176, 8200, 9224

BLOCKS = ([("in", C_GQKV), ("in", C_HQ), ("in", C_GQKV + 512), ("in", C_RV), ("in", C_HF), ("in", C_RQ),
           ("in", C_RV + 512), ("in", C_RK), ("in", C_MG), ("in", C_RG), ("in", C_RG + 512), ("in", C_HI),
           ("in", C_HI + 512), ("br", 0, 0), ("in", C_MG + 512), ("br", 0, 512), ("in", C_MG + 2 * D),
           ("in", C_GQKV + 1024), ("in", C_HG), ("in", C_HG + 512), ("in", C_GQKV + 1536), ("in", C_MG + 2 * D + 512),
           ("in", C_GZ), ("br", 2, 0), ("br", 2, 512), ("in", C_GZ + 512), ("in", C_MG + D), ("in", C_MG + D + 512),
           ("br", 1, 0), ("br", 1, 512), ("out", 0), ("out", 512)])
NBLK = len(BLOCKS)
MIX_UNITS = 2 * NBLK
EXP_UNITS = 6
PASS_UNITS = EXP_UNITS * NE
LAYER_UNITS = MIX_UNITS + 2 * PASS_UNITS
RAW = 4
SPLIT = 4
CREDIT = 4

ALL = (0, 1, 2, 3)
CORE = ([("xt", "va", ALL), ("conv_w", "v", (0,)), ("ba", "v", (0,)), ("bat", "v", (0,)), ("gcol", "v", (0,)), ("gnorm", "a", ALL),
         ("grow", "va", ALL), ("gkt", "v", (0,)), ("h0", "v", (2, 3)), ("rqkt", "a", ALL),
         ("rqk", "v", (0, 1, 2)), ("gkk", "v", ALL), ("rout", "a", ALL), ("h1", "v", (2, 3)),
         ("x0", "a", (0, 1)), ("h2", "v", (2, 3)), ("yz0", "v", ALL), ("ryt", "va", ALL), ("x1", "a", (0, 1)),
         ("h3", "v", (2, 3)), ("yz1", "v", ALL), ("h4", "v", (2, 3)), ("x2", "a", (0, 1)), ("h5", "v", (2, 3)),
         ("yz2", "v", ALL), ("h6", "v", (2, 3)), ("x3", "a", (0, 1)), ("h7", "a", (2,)), ("yz3", "v", ALL),
         ("h8", "v", (2, 3)), ("hout", "va", ALL), ("x4", "a", (0, 1)), ("yz4", "v", ALL), ("x5", "a", (0, 1)),
         ("yz5", "v", ALL), ("hyt", "va", ALL), ("x6", "a", (0, 1)), ("yz6", "v", ALL), ("gvt", "v", ALL),
         ("vn0", "a", (0, 1)), ("state", "a", (0, 1)), ("ks", "v", (0, 1)), ("vn1", "a", (0, 1)),
         ("gout", "va", ALL), ("gyt", "va", ALL), ("mta", "va", (0, 1)), ("mtb", "va", (2, 3)), ("x1t", "va", ALL), ("router", "v", (0,)), ("routert", "v", (0,)),
         ("pos", "v", (0,))])
NCORE = len(CORE)
TURNS = ["xt", "ryt", "hyt", "gyt", "mt", "x1t"]
CORE_AT = {name: i + 1 for i, (name, _, _) in enumerate(CORE)}
READ_AT = {e: {name: sum(e in who for _, who, _ in CORE[:i + 1]) for i, (name, _, _) in enumerate(CORE)} for e in "va"}
READS = {e: sum(e in who for _, who, _ in CORE) for e in "va"}

CONST_DMAS = 13
CONSTS = ["c_eye", "c_upper", "c_strict", "c_mask", "c_maskt", "c_eyeb", "c_decay", "c_iota", "c_invf", "c_tie"]


def constants():
    i = np.arange(P)
    rows, cols = i[:, None], i[None, :]
    f = np.float32
    mask = np.zeros((P, LEVELS, P), np.int32)
    for l in range(LEVELS):
        h = 2 ** l
        same = rows // (2 * h) == cols // (2 * h)
        mask[:, l] = same & (rows % (2 * h) >= h) & (cols % (2 * h) < h)
    maskt = np.ascontiguousarray(mask.transpose(2, 1, 0))
    lg = np.log1p(-(2.0 ** (-5.0 - np.arange(H))))
    rel = np.arange(T)[None, None, :] - i[:, None, None]
    decay = np.where(rel >= 0, np.exp(np.maximum(rel, 0) * lg[None, :, None]), 0.0) * KSCALE
    invf = (f(1.0) / (f(10000.0) ** np.linspace(0.0, 1.0, HK // 2, dtype=f))).astype(f)
    tie = np.zeros((P, EG, EG), f)
    tie[:] = np.arange(EG)[None, None, :] < np.arange(EG)[None, :, None]
    return {
        "c_eye": np.eye(P, dtype=f), "c_upper": (rows <= cols).astype(f), "c_strict": (rows < cols).astype(f),
        "c_mask": mask, "c_maskt": maskt, "c_eyeb": np.eye(P, dtype=np.int32),
        "c_decay": decay.astype(f),
        "c_iota": np.broadcast_to(np.arange(2 * P, dtype=f), (P, 2 * P)).copy(),
        "c_invf": np.broadcast_to(invf, (P, HK // 2)).copy(), "c_tie": tie,
    }


def build_decoder(nc, x_in, positions, w_in, conv_w, a_log, dt_bias, gdn_g, hgrn_lb, hgrn_g, merge_b, w_branch,
                  w_out, ln1_g, ln1_b, router_w, router_b, w_gate, w_up, w_down, ln2_g, ln2_b,
                  c_eye, c_upper, c_strict, c_mask, c_maskt, c_eyeb, c_decay, c_iota, c_invf, c_tie, out):
    with ExitStack() as ctx:
        def sb(name, shape, dt=F32, stack=ctx):
            return stack.enter_context(nc.sbuf_tensor(name, shape, dt))

        def sem(name):
            return ctx.enter_context(nc.semaphore(name))

        pb = ctx.enter_context(nc.psum_tensor("pb", [P, 4, 512], F32))
        pc = ctx.enter_context(nc.psum_tensor("pc", [P, 4, 512], F32))

        raw = sb("raw", [P, RAW, 4, 512])
        eye, upper, strict = sb("eye", [P, P]), sb("upper", [P, P]), sb("strict", [P, P])
        ones = sb("ones", [P, P])
        mask, maskt = sb("mask", [P, LEVELS, P], U8), sb("maskt", [P, LEVELS, P], U8)
        eyeb = sb("eyeb", [P, P], U8)
        tie = sb("tie", [P, EG, EG])
        cos, sin = sb("cos", [P, TT, 64]), sb("sin", [P, TT, 2, 64])
        eps = sb("eps", [P, 2])
        x = sb("x", [P, TT, D])
        xth, xtl = sb("xth", [P, KD, T], F32R), sb("xtl", [P, KD, T], F32R)
        lb, omlb = sb("lb", [P, DEPTH, H]), sb("omlb", [P, DEPTH, H])
        lbl, omlbl = sb("lbl", [P, H]), sb("omlbl", [P, H])
        rwhl, rb = sb("rwhl", [P, KD, 2 * NE], F32R), sb("rb", [P, NE])
        stats, mv = sb("stats", [P, 8, 12]), sb("mv", [P, 8, 2])
        rstd = sb("rstd", [P, 8])
        ss = sb("ss", [P, 8])
        flag = sb("flag", [P, 1], I32)

        mix = ExitStack()
        m = lambda name, shape, dt=F32: sb(name, shape, dt, mix)
        convraw, cw = m("convraw", [CONV * 16, P]), m("cw", [P, CONV, 16])
        wba = m("wba", [P, KD, 8])
        wbahl = m("wbahl", [P, KD, 16], F32R)
        alog, dtb = m("alog", [P, H]), m("dtb", [P, H])
        gain = m("gain", [P, HV])
        mbias = m("mbias", [P, 512])
        small = m("small", [P, 8, 8])
        whi_m, wlo_m = m("whi_m", [P, 2, 4, 512], F32R), m("wlo_m", [P, 2, 4, 512], F32R)
        gqkv = m("gqkv", [P, 16, T])
        dt_, at, attg = m("dt", [P, 8, P]), m("at", [P, 8, P]), m("attg", [P, 8, P])
        ti, ui, kd = m("ti", [P, 8, P]), m("ui", [P, 8, P]), m("kd", [P, H, P])
        xi = dt_
        hq_hk = m("hq_hk", [P, 2, H, T])
        hg_hf = m("hg_hf", [P, 2, H, T])
        hq, hk, hg, hf = hq_hk[:, 0], hq_hk[:, 1], hg_hf[:, 0], hg_hf[:, 1]
        vb = hq_hk[:].rearrange("p a h t -> p a (h t)")
        lng1, lnb1 = hg_hf[:, 0].rearrange("p h t -> p (h t)"), hg_hf[:, 1].rearrange("p h t -> p (h t)")
        cin = m("cin", [P, 4, CONV - 1 + T])
        he = cin[:].rearrange("p c t -> p (c t)")[:, 0:H * T].rearrange("p (h t) -> p h t", h=H)
        atth = m("atth", [P, 8, P])
        attr = gqkv[:, 8:12, :]
        attr2 = gqkv[:, 12:14, :].rearrange("p a (b t) -> p (a b) t", b=2)
        atth2 = gqkv[:, 14:16, :].rearrange("p a (b t) -> p (a b) t", b=2)
        val = m("val", [P, TT, D])
        gt = val[:].rearrange("p t d -> p (t d)").rearrange("p (k t n) -> p k t n", k=2, t=TT)
        gate = m("gate", [P, TT, 512])
        spare_gate = atth[:].rearrange("p (t i) s -> p t (i s)", t=TT)
        gates = [gate[:], gate[:], gate[:], spare_gate, gate[:], spare_gate]
        y = m("y", [P, TT, D])
        erow = y[:, 0, 0:512].rearrange("p (h t) -> p h t", h=H)
        bat = y[0:16, 0, 512:1024]
        decay = y[:, 1, :].rearrange("p (h t) -> p h t", h=H)
        merged = m("merged", [P, TT, D])
        rqk = merged
        state = xi
        early, late = ExitStack(), ExitStack()
        yt = sb("yt", [P, KD, T], F32, early)
        sq = yt
        early.close()
        yth, ytl = sb("yth", [P, KD, T], F32R, late), sb("ytl", [P, KD, T], F32R, late)
        late.close()
        mix.close()

        pre = ExitStack()
        m = lambda name, shape, dt=F32: sb(name, shape, dt, pre)
        lbc = m("lbc", [P, DEPTH, H])
        lbr = m("lbr", [DEPTH * H, P])
        lbt = m("lbt", [P, 4, H])
        mask32, maskt32 = m("mask32", [P, LEVELS, P], I32), m("maskt32", [P, LEVELS, P], I32)
        eyeb32 = m("eyeb32", [P, P], I32)
        rw = m("rw", [P, KD, NE])
        posi, posf = m("posi", [P, TT], I32), m("posf", [P, TT])
        invf = m("invf", [P, 64])
        ang, turns = m("ang", [P, TT, 64]), m("turns", [P, TT, 64])
        pre.close()

        moe = ExitStack()
        m = lambda name, shape, dt=F32: sb(name, shape, dt, moe)
        whi, wlo = m("whi", [P, SPLIT, 4, 512], F32R), m("wlo", [P, SPLIT, 4, 512], F32R)
        xh, xl = m("xh", [P, TT, D], F32R), m("xl", [P, TT, D], F32R)
        xgh, xgl = m("xgh", [P, 2, KD, P], F32R), m("xgl", [P, 2, KD, P], F32R)
        pick, pickt = m("pick", [P, 2, TT, P], F32R), m("pickt", [P, 2, T], F32R)
        hs = m("hs", [P, DX])
        hth, htl = m("hth", [P, 4, P], F32R), m("htl", [P, 4, P], F32R)
        yh, yl = m("yh", [P, D], F32R), m("yl", [P, D], F32R)
        lng2, lnb2 = m("lng2", [P, D]), m("lnb2", [P, D])
        iota = m("iota", [P, 2 * P])
        rout_t = m("rout_t", [2 * NE, 2 * T])
        scores, biased = m("scores", [P, TT, NE]), m("biased", [P, TT, NE])
        cmp, eq = m("cmp", [P, 8, EG, EG]), m("eq", [P, 8, EG, EG])
        rank, best = m("rank", [P, TT, NE]), m("best", [P, TT, NG])
        gsum = m("gsum", [P, TT, NG])
        chosen, wsum = m("chosen", [P, TT, NE]), m("wsum", [P, TT, 2])
        comb, posm = m("comb", [P, TT, NE]), m("posm", [P, TT, NE])
        pcol, ccol = m("pcol", [P, 2, TT]), m("ccol", [P, 2, TT])
        cslot = m("cslot", [P, 2])
        moe.close()

        consts_in = sem("consts_in")
        x_loaded = sem("x_loaded")
        params_in = sem("params_in")
        erow_used = sem("erow_used")
        inits = sem("inits")
        mbias_in, gain_in, iota_in = sem("mbias_in"), sem("gain_in"), sem("iota_in")
        mix_hi, mix_lo = sem("mix_hi"), sem("mix_lo")
        turn_lo = sem("turn_lo")
        turn_hi = sem("turn_hi")
        ln_in = sem("ln_in")
        raw_in = [sem(f"raw_in{i}") for i in range(RAW)]
        half_done = sem("half_done")
        block_done = [sem(f"block_done{i}") for i in range(2)]
        block_read = [sem(f"block_read{i}") for i in range(2)]
        core_done = sem("core_done")
        core_read = {"v": sem("core_read_v"), "a": sem("core_read_a")}
        setup_v, setup_a, setup_p = sem("setup_v"), sem("setup_a"), sem("setup_p")
        chain_v, chain_a = sem("chain_v"), sem("chain_a")
        names = ["conv_out", "conv_silu", "sq_ready", "qk_normed", "beta_g", "lnexp_gn", "gcol_in", "dt_exp",
                 "gkk_in", "rope_done", "hf_exp", "hf_den", "hf_lns", "h_diff", "h_exp", "h_fac", "rvar", "rrstd",
                 "y_done", "gate_raw", "gate_out", "rms_rstd", "merged_ready", "x_ready", "ln_var", "ln_rstd",
                 "xh_ready", "layer_open", "logits", "score_out", "chosen_ready", "moe_ready", "acc_done", "level_t",
                 "ba_raw", "ba_exp", "wba_ready"]
        s = {name: sem(name) for name in names}
        split_hi, split_lo, unit_done = sem("split_hi"), sem("split_lo"), sem("unit_done")
        e_names = ["pick_ready", "gh_done", "xgh_ready", "gl_done", "xgl_ready", "silu_h", "h_ready", "turned",
                   "hth_ready", "htl_ready", "pickt_ready", "yh_ready", "yl_ready", "scattered"]
        se = {name: sem(name) for name in e_names}
        flag_ready = sem("flag_ready")
        held = {e: sem(f"held_{e}") for e in ("sp", "pool", "pe", "act", "dve")}
        out_done = sem("out_done")

        mcast = lambda ap, n: ap[:, None, :].to_broadcast([P, n, ap.shape[-1]])

        def unit_source(block, half, lay):
            r = slice(512 * half, 512 * half + 512)
            if block[0] == "in":
                src = w_in[lay, r, block[1]:block[1] + 512]
            elif block[0] == "br":
                src = w_branch[lay, block[1], r, block[2]:block[2] + 512]
            else:
                src = w_out[lay, r, block[1]:block[1] + 512]
            return src.rearrange("(k p) n -> p k n", p=P)

        def expert_source(i, lay, e):
            if i < 4:
                src = (w_gate if i < 2 else w_up)[lay, e, 512 * (i % 2):512 * (i % 2) + 512, :]
            else:
                src = w_down[lay, e, :, 512 * (i - 4):512 * (i - 4) + 512]
            return src.rearrange("(k p) n -> p k n", p=P)

        class Engine:

            def __init__(self, eng, chain, held):
                self.held = held
                self.eng, self.chain, self.n, self.last = eng, chain, 0, None

            def do(self, ins, signal=None, value=None):
                if signal is None:
                    self.n += 1
                    signal, value = self.chain, self.n
                ins.then_inc(signal, 1)
                self.last = (signal, value)

            def settle(self):
                self.eng.wait_ge(*self.last)

            def tell(self, signal):
                self.settle()
                self.eng.sem_inc(signal, 1)

            def restart(self):
                self.settle()
                self.hold()
                self.eng.sem_clear(self.chain)
                self.n = 0

            def hold(self):
                self.eng.sem_inc(self.held, 1)

        block = ctx.enter_context(nc.Block())

        @block.sync
        def _(sp):
            for dst, src in ((eye, c_eye), (upper, c_upper), (strict, c_strict), (mask32, c_mask), (maskt32, c_maskt),
                             (eyeb32, c_eyeb), (invf, c_invf), (tie, c_tie)):
                sp.dma_start(dst[:], src).then_inc(consts_in, 16)
            for t in range(TT):
                sp.dma_start(posi[:, t:t + 1], positions[0, t * P:(t + 1) * P][:, None]).then_inc(consts_in, 16)
            sp.dma_start(lbr[:], hgrn_lb.rearrange("l (h p) -> (l h) p", p=P)).then_inc(consts_in, 16)
            sp.dma_start(rw[:], router_w.rearrange("(k p) e -> p k e", p=P)).then_inc(consts_in, 16)
            sp.dma_start(rb[:], router_b[None, :].partition_broadcast(P)).then_inc(consts_in, 16)
            sp.dma_start(x[:, :, :], x_in[0].rearrange("(t p) d -> p t d", p=P)).then_inc(x_loaded, 16)
            sp.sem_inc(split_lo, CREDIT)
            with sp.Fori(0, DEPTH) as lay:
                for u in range(MIX_UNITS):
                    if u < RAW:
                        sp.wait_ge(split_lo, lay * 2 * PASS_UNITS + u + 1)
                    else:
                        sp.wait_ge(mix_lo, lay * MIX_UNITS + u - RAW + 1)
                    sp.sem_inc(held["sp"], 1)
                    sp.dma_start(raw[:, u % RAW], unit_source(BLOCKS[u // 2], u % 2, lay)).then_inc(raw_in[u % RAW], 16)
                sp.wait_ge(mix_lo, lay * MIX_UNITS + MIX_UNITS)
                sp.sem_inc(held["sp"], 1)

                def stream_pass(p):
                    with sp.Fori(0, NE // 2) as it:
                        for j in range(2):
                            for i in range(EXP_UNITS):
                                c = EXP_UNITS * j + i
                                sp.wait_ge(split_lo, (lay * 2 + p) * PASS_UNITS + it * 2 * EXP_UNITS + c + CREDIT - RAW + 1)
                                sp.sem_inc(held["sp"], 1)
                                sp.dma_start(raw[:, c % RAW], expert_source(i, lay, 2 * it + j)).then_inc(raw_in[c % RAW], 16)

                stream_pass(0)
                sp.wait_ge(flag_ready, lay + 1)
                sp.sem_inc(held["sp"], 1)
                spill = sp.value_load(flag[0:1, 0:1], min_val=0, max_val=1)
                with sp.If(spill > 0):
                    stream_pass(1)
                with sp.Else():
                    for i in range(RAW):
                        sp.wait_ge(raw_in[i], 16 * (lay * (LAYER_UNITS // RAW) + (MIX_UNITS + PASS_UNITS) // RAW))
                        sp.sem_inc(raw_in[i], 16 * PASS_UNITS // RAW)
            sp.wait_ge(s["x_ready"], 2 * DEPTH)
            sp.dma_start(out[0].rearrange("(t p) d -> p t d", p=P), x[:, :, :]).then_inc(out_done, 16)
            sp.wait_ge(out_done, 16)

        @block.gpsimd
        def _(pool):
            pool.wait_ge(consts_in, 16 * CONST_DMAS)
            for dst, src in ((mask, mask32), (maskt, maskt32), (eyeb, eyeb32)):
                nc.gpsimd.tensor_copy(dst[:], src[:]).then_inc(inits, 1)
            pool.wait_ge(inits, 3)
            with pool.Fori(0, DEPTH) as lay:
                pool.wait_ge(setup_v, 1)
                pool.wait_ge(s["acc_done"], lay + 1)
                pool.wait_ge(s["layer_open"], lay + 1)
                pool.sem_inc(held["pool"], 1)
                pool.dma_start(convraw[:], conv_w[lay].rearrange("j (c p) -> (j c) p", p=P)).then_inc(params_in, 16)
                pool.dma_start(wba[:], w_in[lay, :, C_GB:C_GB + 8].rearrange("(k p) n -> p k n", p=P)).then_inc(params_in, 16)
                pool.dma_start(alog[:], a_log[lay][None, :].partition_broadcast(P)).then_inc(params_in, 16)
                pool.dma_start(dtb[:], dt_bias[lay][None, :].partition_broadcast(P)).then_inc(params_in, 16)
                pool.dma_start(decay, c_decay).then_inc(params_in, 16)
                nc.gpsimd.tensor_copy(ti[:], mcast(eye, 8)).then_inc(inits, 1)
                nc.gpsimd.tensor_copy(ui[:], mcast(eye, 8)).then_inc(inits, 1)
                nc.gpsimd.memset(atth[:], 0.0).then_inc(inits, 1)
                bcast = lambda ap: ap[None, :].partition_broadcast(P)

                def merge_bias(i):
                    base = (0, 512, 2 * D, 2 * D + 512, D, D + 512)[i]
                    if i:
                        pool.wait_ge(s["gate_raw"], lay * 6 + i)
                        pool.sem_inc(held["pool"], 1)
                    pool.dma_start(mbias[:, :], bcast(merge_b[lay, base:base + 512])).then_inc(mbias_in, 16)

                pool.dma_start(gain[:], bcast(hgrn_g[lay])).then_inc(gain_in, 16)
                for i in range(3):
                    merge_bias(i)
                pool.wait_ge(core_done, lay * NCORE + CORE_AT["h8"])
                pool.sem_inc(held["pool"], 1)
                pool.dma_start(lng1, bcast(ln1_g[lay])).then_inc(ln_in, 16)
                pool.dma_start(lnb1, bcast(ln1_b[lay])).then_inc(ln_in, 16)
                pool.wait_ge(core_read["v"], lay * READS["v"] + READ_AT["v"]["hout"])
                pool.sem_inc(held["pool"], 1)
                pool.dma_start(gain[:], bcast(gdn_g[lay])).then_inc(gain_in, 16)
                for i in range(3, 6):
                    merge_bias(i)
                pool.wait_ge(s["x_ready"], 2 * lay + 1)
                pool.sem_inc(held["pool"], 1)
                pool.dma_start(iota[:], c_iota).then_inc(iota_in, 16)
                pool.dma_start(lng2[:], bcast(ln2_g[lay])).then_inc(ln_in, 16)
                pool.dma_start(lnb2[:], bcast(ln2_b[lay])).then_inc(ln_in, 16)

        @block.tensor
        def _(pe):
            mm = nc.tensor.matmul

            def turn(dst, src, n=P):
                return nc.tensor.transpose(dst, src, eye[0:n, 0:n])

            def turn16(src):
                for v in range(KD):
                    for t in range(TT):
                        last = turn(pc[:, v // 2, (v % 2) * T + t * P:(v % 2) * T + t * P + P], src[:, t, v * P:(v + 1) * P])
                return last

            pe.wait_ge(consts_in, 16 * CONST_DMAS)
            for i in range(2):
                pe.sem_inc(block_read[i], 1)
            pe.sem_inc(unit_done, CREDIT)
            turn(pc[:, 0, 0:DEPTH * H], lbr[:, :], DEPTH * H).then_inc(setup_p, 1)
            pe.wait_ge(setup_a, 1)
            pe.wait_ge(x_loaded, 16)
            pe.sem_inc(held["pe"], 1)

            with pe.Fori(0, DEPTH) as lay:
                def core(name):
                    i = CORE_AT[name] - 1
                    for e in "va":
                        before = [c for c, who, banks in CORE[:i] if e in who and set(banks) & set(CORE[i][2])]
                        if before:
                            pe.wait_ge(core_read[e], lay * READS[e] + READ_AT[e][before[-1]])

                def need(name, k=1, per=1):
                    pe.wait_ge(s[name], lay * per + k)

                def both_parts(name):
                    pe.wait_ge(core_read["v"], lay * READS["v"] + READ_AT["v"][name])

                def project(b, src, rows=True, mid=None, parts=None):
                    if parts:
                        pe.wait_ge(turn_lo, lay * len(TURNS) + TURNS.index(parts) + 1)
                    pair = b % 2
                    xh_, xl_ = src
                    pe.wait_ge(block_read[pair], lay * (NBLK // 2) + b // 2 + 1)
                    for half in range(2):
                        if half and parts:
                            both_parts("mtb" if parts == "mt" else parts)
                        pe.wait_ge(mix_lo, lay * MIX_UNITS + 2 * b + half + 1)
                        wh, wl = whi_m[:, half], wlo_m[:, half]
                        if rows:
                            for t in range(TT):
                                for k in range(4):
                                    kk = 4 * half + k
                                    ts_ = slice(t * P, (t + 1) * P)
                                    o = pb[:, 2 * pair + t, :]
                                    mm(o, xh_[:, kk, ts_], wh[:, k, :], start=(kk == 0), stop=False)
                                    mm(o, xh_[:, kk, ts_], wl[:, k, :], start=False, stop=False)
                                    last = mm(o, xl_[:, kk, ts_], wh[:, k, :], start=False, stop=(kk == KD - 1))
                        else:
                            for k in range(4):
                                kk = 4 * half + k
                                for c in range(4):
                                    o = pb[:, 2 * pair + c // 2, (c % 2) * T:(c % 2) * T + T]
                                    cs = slice(c * P, (c + 1) * P)
                                    mm(o, wh[:, k, cs], xh_[:, kk, :], start=(kk == 0 and c % 2 == 0), stop=False,
                                       skip_group_check=True)
                                    mm(o, wh[:, k, cs], xl_[:, kk, :], start=False, stop=False, skip_group_check=True)
                                    last = mm(o, wl[:, k, cs], xh_[:, kk, :], start=False, stop=(kk == KD - 1),
                                              skip_group_check=True)
                        last.then_inc(half_done if half == 0 else block_done[pair], 1)
                        if half == 0 and mid:
                            mid()

                def h_level(l):
                    core(f"h{l}")
                    need("h_fac", l + 1, 9)
                    if l == 7:
                        for h in range(H):
                            last = mm(pc[:, 2, h * P:(h + 1) * P], hf[:, h, 0:P], hf[:, h, P:T], start=True, stop=True)
                    else:
                        for t in range(TT):
                            for h in range(H):
                                a = (hk if l == 8 else hf)[:, h, t * P:(t + 1) * P]
                                bb = (hq if l == 8 else hf)[:, h, t * P:(t + 1) * P]
                                last = mm(pc[:, 2 + t, h * P:(h + 1) * P], a, bb, start=True, stop=True)
                    last.then_inc(core_done, 1)

                def inverse_x(l):
                    core(f"x{l}")
                    if l == 0:
                        need("gkk_in")
                    else:
                        need("level_t", l, LEVELS)
                    for i in range(8):
                        last = mm(pc[:, i // 4, (i % 4) * P:(i % 4) * P + P], at[:, i, :], ti[:, i, :], start=True, stop=True)
                    last.then_inc(core_done, 1)

                def inverse_yz(l):
                    core(f"yz{l}")
                    for i in range(8):
                        if l < LEVELS - 1:
                            mm(pc[:, i // 4, (i % 4) * P:(i % 4) * P + P], ui[:, i, :], xi[:, i, :], start=True, stop=True)
                        last = mm(pc[:, 2 + i // 4, (i % 4) * P:(i % 4) * P + P], xi[:, i, :], ui[:, i, :], start=True, stop=True)
                    last.then_inc(core_done, 1)

                xt, yt2 = (xth, xtl), (yth, ytl)
                pe.wait_ge(s["layer_open"], lay + 1)
                pe.sem_inc(held["pe"], 1)
                turn16(x).then_inc(core_done, 1)
                project(0, xt, rows=False, parts="xt")
                core("conv_w")
                pe.wait_ge(params_in, 80 * lay + 80)
                pe.sem_inc(held["pe"], 1)
                turn(pc[:, 0, 0:64], convraw[:, :], 64).then_inc(core_done, 1)

                def thin(name, w, n):
                    core(name)
                    for k in range(KD):
                        mm(pc[0:2 * n, 0, 0:T], w[:, k, :], xth[:, k, :], start=(k == 0), stop=(k == KD - 1))
                    for k in range(KD):
                        last = mm(pc[0:n, 0, T:2 * T], w[:, k, 0:n], xtl[:, k, :], start=(k == 0), stop=(k == KD - 1))
                    last.then_inc(core_done, 1)

                def thin_turned(name, src, n):
                    core(name)
                    for t in range(TT):
                        o, ts_ = pc[:, 0, t * n:(t + 1) * n], slice(t * P, (t + 1) * P)
                        mm(o, src[0:2 * n, ts_], eye[0:2 * n, 0:n], start=(t == 0), stop=False, skip_group_check=True)
                        mm(o, src[0:2 * n, ts_], eye[0:2 * n, n:2 * n], start=False, stop=False, skip_group_check=True)
                        last = mm(o, src[0:n, T + t * P:T + (t + 1) * P], eye[0:n, 0:n], start=False, stop=True,
                                  skip_group_check=True)
                    last.then_inc(core_done, 1)

                def small_projection():
                    need("wba_ready")
                    thin("ba", wbahl, 8)

                project(1, xt, rows=False, mid=small_projection)
                project(2, xt, rows=False, mid=lambda: thin_turned("bat", bat, 8))
                project(3, xt)

                def decay_sums():
                    core("gcol")
                    need("beta_g")
                    mm(pc[:, 0, 0:8], upper[:, :], small[:, 0, :], start=True, stop=True).then_inc(core_done, 1)

                project(4, xt, rows=False, mid=decay_sums)
                core("gnorm")
                need("sq_ready")
                for j in range(4):
                    last = mm(pc[:, j, :], ones[:, :], sq[:, 2 * j:2 * j + 2, :], start=True, stop=True)
                last.then_inc(core_done, 1)
                project(5, xt)
                core("grow")
                for i in range(8):
                    mm(pc[:, i // 4, (i % 4) * P:(i % 4) * P + P], small[:, 0, i:i + 1].to_broadcast([P, P]), upper[:, :],
                       start=True, stop=True)
                for i in range(8):
                    last = mm(pc[:, 2 + i // 4, (i % 4) * P:(i % 4) * P + P], small[:, 1, i:i + 1].to_broadcast([P, P]), eye[:, :],
                              start=True, stop=True)
                last.then_inc(core_done, 1)
                project(6, xt)

                def keys():
                    core("gkt")
                    need("qk_normed")
                    for h in range(H):
                        last = turn(pc[:, 0, h * P:(h + 1) * P], gqkv[:, 4 + h, 0:P])
                    last.then_inc(core_done, 1)

                project(7, xt)
                keys()
                h_level(0)

                def rotated():
                    core("rqkt")
                    need("rope_done", 2, 2)
                    turn16(rqk).then_inc(core_done, 1)

                project(8, xt)
                rotated()

                def ret_scores():
                    core("rqk")
                    for h in range(H):
                        mm(pc[:, h // 2, (h % 2) * T:(h % 2) * T + T], yt[:, 4 + h, 0:P], yt[:, h, :], start=True, stop=True)
                    for h in range(H):
                        last = mm(pc[:, 2, h * P:(h + 1) * P], yt[:, 4 + h, P:T], yt[:, h, P:T], start=True, stop=True)
                    last.then_inc(core_done, 1)

                def gkk():
                    core("gkk")
                    for i in range(8):
                        h, t = i % 4, i // 4
                        kt = gqkv[:, 4 + h, t * P:(t + 1) * P]
                        mm(pc[:, t, h * P:(h + 1) * P], kt, kt, start=True, stop=True)
                        last = mm(pc[:, 2 + t, h * P:(h + 1) * P], kt, gqkv[:, h, t * P:(t + 1) * P], start=True, stop=True)
                    last.then_inc(core_done, 1)

                project(9, xt, mid=ret_scores)
                gkk()

                def attend(name, same, across, v_blocks):
                    core(name)
                    for b in v_blocks:
                        pe.wait_ge(block_read[b % 2], lay * (NBLK // 2) + b // 2 + 2)
                    for h in range(H):
                        mm(pc[:, h // 2, (h % 2) * HV:(h % 2) * HV + HV], same(h, 0), val[:, 0, h * HV:(h + 1) * HV],
                           start=True, stop=True)
                    for h in range(H):
                        o = pc[:, 2 + h // 2, (h % 2) * HV:(h % 2) * HV + HV]
                        mm(o, across(h), val[:, 0, h * HV:(h + 1) * HV], start=True, stop=False)
                        last = mm(o, same(h, 1), val[:, 1, h * HV:(h + 1) * HV], start=False, stop=True)
                    last.then_inc(core_done, 1)

                def turned(name, src, feed, k=1, per=1):
                    core(name)
                    need(feed, k, per)
                    turn16(src).then_inc(core_done, 1)

                def heads(name, lhs, rhs):
                    core(name)
                    for h in range(H):
                        last = mm(pc[:, h // 2, (h % 2) * HV:(h % 2) * HV + HV], lhs(h), rhs(h), start=True, stop=True)
                    last.then_inc(core_done, 1)

                project(10, xt, mid=lambda: attend("rout", lambda h, t: attr[:, h, 0:P] if t == 0 else attr2[:, h, :],
                                                   lambda h: attr[:, h, P:T], (3, 6)))
                h_level(1)
                inverse_x(0)
                project(11, xt, mid=lambda: h_level(2))
                inverse_yz(0)
                project(12, xt, mid=lambda: turned("ryt", y, "y_done", 1, 3))
                inverse_x(1)
                both_parts("ryt")
                project(13, yt2, mid=lambda: h_level(3))
                inverse_yz(1)
                project(14, xt, mid=lambda: h_level(4))
                inverse_x(2)
                project(15, yt2, mid=lambda: h_level(5))
                inverse_yz(2)
                project(16, xt, mid=lambda: h_level(6))
                inverse_x(3)
                project(17, xt, rows=False, mid=lambda: h_level(7))
                inverse_yz(3)
                project(18, xt, mid=lambda: h_level(8))
                attend("hout", lambda h, t: atth[:, 4 * t + h, :], lambda h: atth2[:, h, :], (11, 12))
                project(19, xt)
                inverse_x(4)
                project(20, xt, rows=False, mid=lambda: inverse_yz(4))
                inverse_x(5)
                project(21, xt, mid=lambda: inverse_yz(5))
                turned("hyt", y, "y_done", 2, 3)
                project(22, xt, mid=lambda: inverse_x(6))
                inverse_yz(6)
                both_parts("hyt")

                def gdn_values():
                    core("gvt")
                    need("conv_silu", 4, 4)
                    for c in range(8):
                        for t in range(TT):
                            last = turn(pc[:, 2 * t + c // 4, (c % 4) * P:(c % 4) * P + P], gqkv[:, 8 + c, t * P:(t + 1) * P])
                    last.then_inc(core_done, 1)

                project(23, yt2, mid=gdn_values)
                need("level_t", LEVELS, LEVELS)
                heads("vn0", lambda h: ui[:, h, :], lambda h: vb[:, 0, h * HV:(h + 1) * HV])
                project(24, yt2, mid=lambda: heads("state", lambda h: kd[:, h, :], lambda h: vb[:, 0, h * HV:(h + 1) * HV]))
                heads("ks", lambda h: gqkv[:, 4 + h, P:T], lambda h: state[:, 2 * h:2 * h + 2, :])
                project(25, xt, mid=lambda: heads("vn1", lambda h: ui[:, 4 + h, :], lambda h: vb[:, 1, h * HV:(h + 1) * HV]))
                core("gout")
                for h in range(H):
                    mm(pc[:, h // 2, (h % 2) * HV:(h % 2) * HV + HV], attg[:, h, :], vb[:, 0, h * HV:(h + 1) * HV],
                       start=True, stop=True)
                for h in range(H):
                    o = pc[:, 2 + h // 2, (h % 2) * HV:(h % 2) * HV + HV]
                    mm(o, gqkv[:, h, P:T], state[:, 2 * h:2 * h + 2, :], start=True, stop=False)
                    last = mm(o, attg[:, 4 + h, :], vb[:, 1, h * HV:(h + 1) * HV], start=False, stop=True)
                last.then_inc(core_done, 1)
                project(26, xt)
                project(27, xt, mid=lambda: turned("gyt", y, "y_done", 3, 3))
                both_parts("gyt")
                project(28, yt2)

                def merged_half(i):
                    core("mta" if i == 0 else "mtb")
                    need("merged_ready", 5 + i, 6)
                    for v in range(4 * i, 4 * i + 4):
                        for t in range(TT):
                            last = turn(pc[:, v // 2, (v % 2) * T + t * P:(v % 2) * T + t * P + P], merged[:, t, v * P:(v + 1) * P])
                    last.then_inc(core_done, 1)

                project(29, yt2, mid=lambda: merged_half(0))
                merged_half(1)
                project(30, yt2, parts="mt")
                project(31, yt2)
                turned("x1t", x, "x_ready", 1, 2)
                both_parts("x1t")
                thin("router", rwhl, NE)
                thin_turned("routert", rout_t, NE)
                core("pos")
                need("chosen_ready")
                mm(pc[:, 0, 0:NE], strict[:, :], chosen[:, 0, :], start=True, stop=True)
                mm(pc[:, 0, NE:2 * NE], ones[:, :], chosen[:, 0, :], start=True, stop=False)
                mm(pc[:, 0, NE:2 * NE], strict[:, :], chosen[:, 1, :], start=False, stop=True)
                mm(pc[:, 0, 2 * NE:3 * NE], ones[:, :], chosen[:, 0, :], start=True, stop=False)
                mm(pc[:, 0, 2 * NE:3 * NE], ones[:, :], chosen[:, 1, :], start=False, stop=True).then_inc(core_done, 1)
                def expert_pass(p):
                    def gather(part, n, j):
                        for k in range(KD):
                            for t in range(TT):
                                last = mm(pc[:, 2 + k // 4, (k % 4) * P:(k % 4) * P + P], part[:, t, k * P:(k + 1) * P],
                                          pick[:, j, t, :], start=(t == 0), stop=(t == TT - 1))
                        return last

                    def gather_hi(n, j):
                        pe.wait_ge(se["pick_ready"], n + 1)
                        gather(xh, n, j).then_inc(se["gh_done"], 1)

                    def gather_lo(n, j):
                        pe.wait_ge(se["xgh_ready"], n + 1)
                        gather(xl, n, j).then_inc(se["gl_done"], 1)

                    def passes(dst, ah, al, c, base, first, last_):
                        pe.wait_ge(split_lo, base + c + 1 + CREDIT)
                        for k in range(4):
                            mm(dst, ah(k), whi[:, c % SPLIT, k, :], start=(first and k == 0), stop=False)
                            mm(dst, ah(k), wlo[:, c % SPLIT, k, :], start=False, stop=False)
                            ins = mm(dst, al(k), whi[:, c % SPLIT, k, :], start=False, stop=(last_ and k == 3))
                        ins.then_inc(unit_done, 1)

                    def scatter(n, j, opens=False):
                        pe.wait_ge(se["yl_ready"], n + 1)
                        pe.wait_ge(se["pickt_ready"], n + 1)
                        for t in range(TT):
                            for cb in range(2):
                                for part in (yh, yl):
                                    last = mm(pb[:, 2 * t + cb, :], pickt[:, j, t * P:(t + 1) * P],
                                              part[:, cb * 512:(cb + 1) * 512], start=(opens and part is yh), stop=False,
                                              skip_group_check=True)
                        last.then_inc(se["scattered"], 1)

                    def expert(n, base, j, first=False, second=False, last_=False):
                        g = EXP_UNITS * j
                        pe.wait_ge(se["xgl_ready"], n + 1)
                        if not first:
                            pe.wait_ge(se["hth_ready"], n)
                            pe.wait_ge(se["htl_ready"], n)
                        for i in range(2):
                            passes(pc[:, 0, :], lambda k: xgh[:, j, 4 * i + k, :], lambda k: xgl[:, j, 4 * i + k, :],
                                   g + i, base, i == 0, i == 1)
                        if not last_:
                            if not first:
                                pe.wait_ge(se["yh_ready"], n)
                                pe.wait_ge(se["yl_ready"], n)
                            gather_hi(n + 1, 1 - j)
                        if not first:
                            pe.wait_ge(se["pickt_ready"], n)
                        for i in range(2):
                            passes(pc[:, 1, :], lambda k: xgh[:, j, 4 * i + k, :], lambda k: xgl[:, j, 4 * i + k, :],
                                   g + 2 + i, base, i == 0, i == 1)
                        if not last_:
                            gather_lo(n + 1, 1 - j)
                        pe.wait_ge(se["h_ready"], n + 1)
                        for f in range(4):
                            turn(pc[:, 0, f * P:(f + 1) * P], hs[:, f * P:(f + 1) * P])
                        for t in range(TT):
                            turn(pc[:, 1, t * P:(t + 1) * P], pick[:, j, t, :].bitcast(F32))
                        for t in range(TT):
                            ins = mm(pc[:, 1, T:T + 1], pick[:, j, t, :].bitcast(F32), ccol[:, j, t:t + 1],
                                     start=(t == 0), stop=(t == TT - 1))
                        ins.then_inc(se["turned"], 1)
                        if not first:
                            scatter(n - 1, 1 - j, opens=second and p == 0)
                        pe.wait_ge(se["htl_ready"], n + 1)
                        if not last_:
                            pe.wait_ge(se["xgl_ready"], n + 2)
                        for i in range(2):
                            passes(pc[:, 2 + i, :], lambda k: hth[:, k, :], lambda k: htl[:, k, :], g + 4 + i, base, True, True)

                    n0 = (lay * 2 + p) * NE
                    u0 = (lay * 2 + p) * PASS_UNITS
                    gather_hi(n0, 0)
                    gather_lo(n0, 0)
                    expert(n0, u0, 0, first=True)
                    expert(n0 + 1, u0, 1, second=True)
                    with pe.Fori(1, NE // 2 - 1) as it:
                        for j in range(2):
                            expert(n0 + it * 2 + j, u0 + it * 2 * EXP_UNITS, j)
                    expert(n0 + NE - 2, u0 + (NE - 2) * EXP_UNITS, 0)
                    expert(n0 + NE - 1, u0 + (NE - 2) * EXP_UNITS, 1, last_=True)
                    scatter(n0 + NE - 1, 1)

                expert_pass(0)
                pe.wait_ge(flag_ready, lay + 1)
                pe.sem_inc(held["pe"], 1)
                spill = pe.value_load(flag[0:1, 0:1], min_val=0, max_val=1)
                with pe.If(spill > 0):
                    expert_pass(1)
                with pe.Else():
                    pe.wait_ge(se["scattered"], (lay * 2 + 1) * NE)
                    for name in ("gh_done", "gl_done", "turned", "scattered"):
                        pe.sem_inc(se[name], NE)
                    pe.sem_inc(unit_done, PASS_UNITS)
                pe.wait_ge(se["scattered"], (lay * 2 + 2) * NE)
                pe.sem_inc(s["acc_done"], 1)

        @block.scalar
        def _(act):
            A = Engine(act, chain_a, held["act"])
            fn = nc.scalar.activation

            act.wait_ge(setup_p, 1)
            fn(lbc[:].rearrange("p l h -> p (l h)"), pc[:, 0, 0:DEPTH * H], ACT.Copy).then_inc(setup_a, 1)
            act.wait_ge(setup_v, 2)
            fn(lbt[:, 0:DEPTH, :], lbt[:, 0:DEPTH, :], ACT.Exp).then_inc(setup_a, 1)
            act.wait_ge(setup_v, 4)
            fn(cos[:], cos[:], ACT.Sin)
            fn(sin[:, :, 1, :], sin[:, :, 1, :], ACT.Sin).then_inc(setup_a, 1)

            with act.Fori(0, DEPTH) as lay:
                def need(name, k=1, per=1):
                    act.wait_ge(s[name], lay * per + k)

                def give(ins, name, k=1, per=1):
                    A.do(ins, s[name], lay * per + k)

                def core(name):
                    act.wait_ge(core_done, lay * NCORE + CORE_AT[name])

                def read(ins, name):
                    A.do(ins, core_read["a"], lay * READS["a"] + READ_AT["a"][name])

                def block_in(b):
                    act.wait_ge(block_done[b % 2], lay * (NBLK // 2) + b // 2 + 1)
                    return pb[:, 2 * (b % 2):2 * (b % 2) + 2, :]

                def block_out(ins, b):
                    A.do(ins, block_read[b % 2], lay * (NBLK // 2) + b // 2 + 2)

                def whole(dst, name):
                    core(name)
                    read(fn(dst[:].rearrange("p k t -> p (k t)"), pc[:].rearrange("p b n -> p (b n)"), ACT.Copy), name)

                def two(name):
                    core(name)
                    return pc[:, 0:2, :].rearrange("p b n -> p (b n)")

                def unit_hi(u):
                    act.wait_ge(raw_in[u % RAW], 16 * (lay * (LAYER_UNITS // RAW) + u // RAW + 1))
                    if u >= 2:
                        b = (u - 2) // 2
                        if u % 2 == 0:
                            act.wait_ge(half_done, lay * NBLK + b + 1)
                        else:
                            act.wait_ge(block_done[b % 2], lay * (NBLK // 2) + b // 2 + 1)
                    A.do(fn(whi_m[:, u % 2], raw[:, u % RAW], ACT.Copy), mix_hi, lay * MIX_UNITS + u + 1)

                def pre(b):
                    if b < NBLK - 1:
                        unit_hi(2 * b + 2)

                def post(b):
                    if b < NBLK - 1:
                        unit_hi(2 * b + 3)

                def around(b, step=None, mid=None):
                    pre(b)
                    if mid:
                        mid()
                    post(b)
                    if step:
                        step()

                def turn_parts(dst, name):
                    core(name)
                    for i in range(2):
                        ins = fn(dst[:, 4 * i:4 * i + 4, :].rearrange("p k t -> p (k t)"),
                                 pc[:, 2 * i:2 * i + 2, :].rearrange("p b n -> p (b n)"), ACT.Copy)
                        A.do(ins, turn_hi, (lay * len(TURNS) + TURNS.index(name)) * 2 + i + 1)
                    A.tell(core_read["a"])

                def conv_copy(b):
                    src = block_in(b).rearrange("p b (c t) -> p (b c) t", c=2)
                    block_out(fn(cin[:, :, CONV - 1:], src, ACT.Copy), b)

                def conv_act(i):
                    need("conv_out", i + 1, 4)
                    g = gqkv[:, 4 * i:4 * i + 4, :]
                    give(fn(g, g, ACT.Silu), "conv_silu", i + 1, 4)

                def h_exp(l):
                    need("h_diff", l + 1, 8)
                    give(fn(he, he, ACT.Exp), "h_exp", l + 1, 8)

                def value_block(b, k):
                    src = block_in(b)
                    for t in range(TT):
                        ins = fn(val[:, t, k * 512:(k + 1) * 512], src[:, t, :], ACT.Copy)
                    block_out(ins, b)

                def inverse_x(l):
                    src = two(f"x{l}")
                    read(fn(xi[:].rearrange("p i t -> p (i t)"), src, ACT.Copy), f"x{l}")

                def activate(b, k, func):
                    block_out(fn(gt[:, k, :, :], block_in(b), func), b)

                def gate_sigmoid(i):
                    need("gate_raw", i + 1, 6)
                    give(fn(gates[i], gates[i], ACT.Sigmoid), "gate_out", i + 1, 6)

                def rms(name):
                    core(name)
                    for i in range(8):
                        src = pc[:, 2 * (i // 4) + (i % 4) // 2, (i % 2) * HV:(i % 2) * HV + HV]
                        ins = fn(y[:, i // 4, (i % 4) * HV:(i % 4) * HV + HV], src, ACT.Square, accum_out=ss[:, i:i + 1])
                    read(ins, name)
                    A.settle()
                    A.do(fn(ss[:, :], ss[:, :], ACT.Ln, scale=1.0 / HV, bias=eps[:, 0:1]))
                    A.settle()

                act.wait_ge(setup_v, 5)
                act.wait_ge(inits, 3)
                act.wait_ge(s["acc_done"], lay + 1)
                unit_hi(0)
                unit_hi(1)
                turn_parts(xth, "xt")
                act.wait_ge(s["layer_open"], lay + 1)
                around(0, lambda: conv_copy(0))
                around(1, lambda: block_out(fn(hq.rearrange("p h t -> p (h t)"), block_in(1).rearrange("p b n -> p (b n)"),
                                               ACT.Copy, scale=KSCALE), 1))
                conv_act(0)
                around(2, lambda: conv_copy(2))
                need("ba_raw")
                A.do(fn(small[:, 2, :], small[:, 2, :], ACT.Exp, scale=-1.0))
                A.do(fn(small[:, 4, :], small[:, 3, :], ACT.Abs))
                A.settle()
                A.do(fn(small[:, 4, :], small[:, 4, :], ACT.Exp, scale=-1.0))
                A.settle()
                A.do(fn(small[:, 4, :], small[:, 4, :], ACT.Ln, bias=1.0))
                give(fn(small[:, 5, 0:H], alog[:, :], ACT.Exp), "ba_exp")
                around(3, lambda: value_block(3, 0))
                conv_act(1)
                A.settle()
                give(fn(sq[:], gqkv[:, 0:8, :], ACT.Square), "sq_ready")
                def forget_parts():
                    src = block_in(4).rearrange("p b n -> p (b n)")
                    A.do(fn(hg.rearrange("p h t -> p (h t)"), src, ACT.Relu, scale=-1.0))
                    block_out(fn(he.rearrange("p h t -> p (h t)"), src, ACT.Relu), 4)

                def forget_exps():
                    A.settle()
                    A.do(fn(hg, hg, ACT.Exp, scale=-1.0))
                    give(fn(he, he, ACT.Exp, scale=-1.0), "hf_exp")
                    core("gnorm")
                    read(fn(sq[:].rearrange("p k t -> p (k t)"), pc[:].rearrange("p b n -> p (b n)"), ACT.Ln, bias=eps[:, 0:1]), "gnorm")

                around(4, forget_parts)
                around(5, mid=forget_exps)
                need("hf_den")
                A.do(fn(hg, hg, ACT.Ln))
                A.do(fn(hf, hf, ACT.Ln, bias=1.0))
                A.settle()
                give(fn(hk, hf, ACT.Exp, scale=-1.0), "hf_lns")
                give(fn(sq[:], sq[:], ACT.Exp, scale=-0.5), "lnexp_gn")

                def row_exp():
                    core("grow")
                    need("gcol_in")
                    for i in range(8):
                        A.do(fn(dt_[:, i, :], pc[:, i // 4, (i % 4) * P:(i % 4) * P + P], ACT.Relu, scale=-1.0,
                                bias=small[:, 2, i:i + 1]))
                    read(fn(y[:, 0, 0:512], pc[:, 1, :], ACT.Exp), "grow")
                    A.settle()
                    give(fn(dt_[:], dt_[:], ACT.Exp, scale=-1.0), "dt_exp")

                around(6, lambda: value_block(6, 1), mid=row_exp)
                h_exp(0)
                around(7)
                h_exp(1)
                around(8)
                whole(yt, "rqkt")
                h_exp(2)
                around(9)

                def retained():
                    core("rout")
                    act.wait_ge(erow_used, lay + 1)
                    read(fn(y[:].rearrange("p t d -> p (t d)"), pc[:].rearrange("p b n -> p (b n)"), ACT.Copy), "rout")
                    activate(9, 0, ACT.Silu)

                around(10, lambda: activate(10, 1, ACT.Silu), mid=retained)
                need("rvar")
                A.do(fn(rstd[:, :], rstd[:, :], ACT.Ln, bias=eps[:, 0:1]))
                A.settle()
                give(fn(rstd[:, :], rstd[:, :], ACT.Exp, scale=-0.5), "rrstd")
                inverse_x(0)
                h_exp(3)

                def hgrn_values():
                    need("y_done", 1, 3)
                    value_block(11, 0)

                around(11)
                h_exp(4)
                gate_sigmoid(0)
                hgrn_values()
                around(12, lambda: value_block(12, 1), mid=lambda: turn_parts(yth, "ryt"))
                inverse_x(1)
                around(13)
                h_exp(5)
                around(14)
                inverse_x(2)
                h_exp(6)
                gate_sigmoid(1)
                around(15)
                h_exp(7)
                around(16)
                inverse_x(3)
                gate_sigmoid(2)

                def h7_copy():
                    core("h7")
                    read(fn(atth2.rearrange("p h t -> p (h t)"), pc[:, 2, :], ACT.Copy), "h7")

                def padded(b):
                    need("h_fac", 8, 9)
                    conv_copy(b)

                around(17, lambda: padded(17), mid=h7_copy)
                around(18)
                rms("hout")
                give(fn(rstd[:, :], ss[:, :], ACT.Exp, scale=-0.5), "rms_rstd", 1, 2)
                activate(18, 0, ACT.Sigmoid)
                conv_act(2)
                around(19, lambda: activate(19, 1, ACT.Sigmoid))
                inverse_x(4)
                around(20, lambda: conv_copy(20))
                inverse_x(5)
                around(21)
                turn_parts(yth, "hyt")
                conv_act(3)
                gate_sigmoid(3)
                need("y_done", 2, 3)
                around(22, lambda: activate(22, 0, ACT.Silu), mid=lambda: inverse_x(6))
                around(23)
                read(fn(vb[:, 0, :], two("vn0"), ACT.Copy), "vn0")
                around(24, mid=lambda: read(fn(state[:].rearrange("p i t -> p (i t)"), two("state"), ACT.Copy), "state"))
                around(25, lambda: activate(25, 1, ACT.Silu), mid=lambda: read(fn(vb[:, 1, :], two("vn1"), ACT.Copy), "vn1"))
                rms("gout")
                give(fn(rstd[:, :], ss[:, :], ACT.Exp, scale=-0.5), "rms_rstd", 2, 2)
                around(26)
                gate_sigmoid(4)
                around(27, mid=lambda: turn_parts(yth, "gyt"))
                gate_sigmoid(5)
                around(28)

                def merged_high(i):
                    name = "mta" if i == 0 else "mtb"
                    core(name)
                    A.do(fn(yth[:, 4 * i:4 * i + 4, :].rearrange("p k t -> p (k t)"),
                            pc[:, 2 * i:2 * i + 2, :].rearrange("p b n -> p (b n)"), ACT.Copy),
                         turn_hi, (lay * len(TURNS) + TURNS.index("mt")) * 2 + i + 1)
                    A.tell(core_read["a"])

                around(29, mid=lambda: merged_high(0))
                merged_high(1)
                around(30)

                def norm_scale(k):
                    need("ln_var", k, 2)
                    A.do(fn(rstd[:, 0:2], rstd[:, 0:2], ACT.Ln, bias=eps[:, 1:2]))
                    A.settle()
                    A.do(fn(rstd[:, 0:2], rstd[:, 0:2], ACT.Exp, scale=-0.5), s["ln_rstd"], lay * 2 + k)

                def hi(c, base, raw_base):
                    act.wait_ge(raw_in[c % RAW], raw_base + 16 * (c // RAW) + 16)
                    act.wait_ge(unit_done, base + c + 1)
                    A.do(fn(whi[:, c % SPLIT], raw[:, c % RAW], ACT.Copy), split_hi, base + c + 1)

                norm_scale(1)
                for b in range(2):
                    act.wait_ge(block_done[b], (lay + 1) * (NBLK // 2))
                for c in range(SPLIT):
                    hi(c, lay * 2 * PASS_UNITS, (lay * (LAYER_UNITS // RAW) + MIX_UNITS // RAW) * 16)
                turn_parts(xth, "x1t")
                need("x_ready", 1, 2)
                give(fn(xh[:], x[:], ACT.Copy), "xh_ready")
                need("logits")
                give(fn(scores[:], scores[:], ACT.Sigmoid), "score_out")

                def expert_pass(p):
                    def gathered(n, j):
                        act.wait_ge(se["gh_done"], n + 1)
                        A.do(fn(xgh[:, j].rearrange("p k t -> p (k t)"), pc[:, 2:4, :].rearrange("p b n -> p (b n)"), ACT.Copy),
                             se["xgh_ready"], n + 1)

                    def expert(n, base, raw_base, j, last_=False):
                        g = EXP_UNITS * j
                        act.wait_ge(unit_done, base + g + 2 + CREDIT)
                        A.do(fn(hs[:, :], pc[:, 0, :], ACT.Silu), se["silu_h"], n + 1)
                        hi(g + 5, base, raw_base)
                        if not last_:
                            gathered(n + 1, 1 - j)
                            hi(g + 6, base, raw_base)
                            hi(g + 7, base, raw_base)
                        act.wait_ge(se["turned"], n + 1)
                        A.do(fn(hth[:].rearrange("p k t -> p (k t)"), pc[:, 0, :], ACT.Copy), se["hth_ready"], n + 1)
                        if not last_:
                            hi(g + 8, base, raw_base)
                        act.wait_ge(unit_done, base + g + 6 + CREDIT)
                        act.wait_ge(se["pickt_ready"], n + 1)
                        A.do(fn(yh[:, :], pc[:, 2:4, :].rearrange("p b n -> p (b n)"), ACT.Copy, scale=cslot[:, j:j + 1]),
                             se["yh_ready"], n + 1)
                        if not last_:
                            hi(g + 9, base, raw_base)
                            hi(g + 10, base, raw_base)

                    n0 = (lay * 2 + p) * NE
                    u0 = (lay * 2 + p) * PASS_UNITS
                    r0 = (lay * (LAYER_UNITS // RAW) + (MIX_UNITS + p * PASS_UNITS) // RAW) * 16
                    if p:
                        for c in range(SPLIT):
                            hi(c, u0, r0)
                    gathered(n0, 0)
                    hi(SPLIT, u0, r0)
                    with act.Fori(0, NE // 2 - 1) as it:
                        for j in range(2):
                            expert(n0 + it * 2 + j, u0 + it * 2 * EXP_UNITS, r0 + it * (32 * EXP_UNITS // RAW), j)
                    expert(n0 + NE - 2, u0 + (NE - 2) * EXP_UNITS, r0 + (NE - 2) * EXP_UNITS // RAW * 16, 0)
                    expert(n0 + NE - 1, u0 + (NE - 2) * EXP_UNITS, r0 + (NE - 2) * EXP_UNITS // RAW * 16, 1, last_=True)

                expert_pass(0)
                act.wait_ge(flag_ready, lay + 1)
                act.sem_inc(held["act"], 1)
                spill = act.value_load(flag[0:1, 0:1], min_val=0, max_val=1)
                with act.If(spill > 0):
                    expert_pass(1)
                with act.Else():
                    act.wait_ge(se["yh_ready"], (lay * 2 + 1) * NE)
                    act.sem_inc(split_hi, PASS_UNITS)
                    for name in ("xgh_ready", "silu_h", "hth_ready", "yh_ready"):
                        act.sem_inc(se[name], NE)
                norm_scale(2)
                A.restart()

        @block.vector
        def _(dve):
            V = Engine(dve, chain_v, held["dve"])
            v = nc.vector
            tt, ts, stt, cp = v.tensor_tensor, v.tensor_scalar, v.scalar_tensor_tensor, v.tensor_copy

            V.do(v.memset(ones[:], 1.0))
            V.do(v.memset(eps[:, 0:1], 1e-6))
            V.do(v.memset(eps[:, 1:2], 1e-5))
            V.tell(setup_v)
            V.tell(s["layer_open"])
            dve.wait_ge(consts_in, 16 * CONST_DMAS)
            V.do(cp(rwhl[:, :, 0:NE], rw[:]))
            V.settle()
            V.do(tt(rwhl[:, :, NE:2 * NE], rw[:], rwhl[:, :, 0:NE].bitcast(F32), ALU.subtract))
            dve.wait_ge(setup_a, 1)
            top = lbt[:, 2, :]
            V.do(cp(top, lbc[:, 0, :]))
            for l in range(1, DEPTH):
                V.settle()
                V.do(tt(top, top, lbc[:, l, :], ALU.max))
            V.settle()
            for l in range(DEPTH):
                ins = tt(lbt[:, l, :], lbc[:, l, :], top, ALU.subtract)
                V.do(ins) if l < DEPTH - 1 else V.do(ins, setup_v, 2)
            dve.wait_ge(setup_a, 2)
            V.do(cp(top, lbt[:, 0, :]))
            for l in range(1, DEPTH):
                V.settle()
                V.do(tt(top, top, lbt[:, l, :], ALU.add))
            V.settle()
            V.do(v.reciprocal(top, top))
            V.settle()
            for l in range(DEPTH):
                V.do(tt(lbt[:, l, :], lbt[:, l, :], top, ALU.mult))
            V.settle()
            for l in range(1, DEPTH):
                V.do(tt(lbt[:, l, :], lbt[:, l, :], lbt[:, l - 1, :], ALU.add))
                V.settle()
            for l in range(DEPTH):
                V.do(tt(lb[:, l, :], lbt[:, l, :], lbt[:, 0, :], ALU.subtract))
            V.settle()
            V.do(ts(omlb[:], lb[:], -1.0, 1.0, ALU.mult, ALU.add))
            V.do(cp(posf[:], posi[:]))
            V.settle()
            for t in range(TT):
                V.do(ts(ang[:, t, :], invf[:, :], posf[:, t:t + 1], None, ALU.mult))
            V.settle()
            magic, two_pi_hi = 12582912.0, 6.28125
            two_pi_lo = 2 * np.pi - two_pi_hi
            for quarter, dst in ((0.25, cos[:]), (0.0, sin[:, :, 1, :])):
                V.do(ts(turns[:], ang[:], float(1 / (2 * np.pi)), quarter, ALU.mult, ALU.add))
                V.settle()
                V.do(ts(turns[:], turns[:], magic, None, ALU.add))
                V.settle()
                V.do(ts(turns[:], turns[:], magic, None, ALU.subtract))
                V.settle()
                V.do(stt(dst, turns[:], -two_pi_hi, ang[:], ALU.mult, ALU.add))
                V.settle()
                V.do(stt(dst, turns[:], -float(two_pi_lo), dst, ALU.mult, ALU.add))
                V.settle()
                V.do(ts(dst, dst, float(quarter * 2 * np.pi), 3.1415925, ALU.add, ALU.min))
                V.settle()
                V.do(ts(dst, dst, -3.1415925, None, ALU.max), setup_v, 3 if quarter else 4)
            dve.wait_ge(setup_a, 3)
            V.do(ts(sin[:, :, 0, :], sin[:, :, 1, :], -1.0, None, ALU.mult), s["acc_done"], 1)
            V.tell(setup_v)
            dve.wait_ge(inits, 3)
            V.restart()

            with dve.Fori(0, DEPTH) as lay:
                def need(name, k=1, per=1):
                    dve.wait_ge(s[name], lay * per + k)

                def give(ins, name, k=1, per=1):
                    V.do(ins, s[name], lay * per + k)

                def core(name):
                    dve.wait_ge(core_done, lay * NCORE + CORE_AT[name])

                def read(ins, name):
                    V.do(ins, core_read["v"], lay * READS["v"] + READ_AT["v"][name])

                def block_in(b):
                    dve.wait_ge(block_done[b % 2], lay * (NBLK // 2) + b // 2 + 1)
                    return pb[:, 2 * (b % 2):2 * (b % 2) + 2, :]

                def block_out(ins, b):
                    V.do(ins, block_read[b % 2], lay * (NBLK // 2) + b // 2 + 2)

                def unit_lo(u):
                    dve.wait_ge(mix_hi, lay * MIX_UNITS + u + 1)
                    V.do(tt(wlo_m[:, u % 2], raw[:, u % RAW], whi_m[:, u % 2].bitcast(F32), ALU.subtract), mix_lo,
                         lay * MIX_UNITS + u + 1)

                def pre(b):
                    if b < NBLK - 1:
                        unit_lo(2 * b + 2)

                def post(b):
                    if b < NBLK - 1:
                        unit_lo(2 * b + 3)

                def around(b, step=None, mid=None, after=None):
                    pre(b)
                    if mid:
                        mid()
                    if step:
                        step()
                    post(b)
                    if after:
                        after()

                def turn_parts(dst, hi, name):
                    core(name)
                    for i in range(2):
                        dve.wait_ge(turn_hi, (lay * len(TURNS) + TURNS.index(name)) * 2 + i + 1)
                        ins = tt(dst[:, 4 * i:4 * i + 4, :].rearrange("p k t -> p (k t)"),
                                 pc[:, 2 * i:2 * i + 2, :].rearrange("p b n -> p (b n)"),
                                 hi[:, 4 * i:4 * i + 4, :].bitcast(F32).rearrange("p k t -> p (k t)"), ALU.subtract)
                        V.do(ins, turn_lo, lay * len(TURNS) + TURNS.index(name) + 1) if i == 0 else read(ins, name)

                def conv(b, i, taps):
                    for j in taps:
                        if j == 0:
                            dve.wait_ge(block_read[b % 2], lay * (NBLK // 2) + b // 2 + 2)
                        else:
                            V.settle()
                        for c in range(4):
                            ch = 4 * i + c
                            src, dst, w = cin[:, c, j:j + T], gqkv[:, ch, :], cw[:, j, ch:ch + 1]
                            ins = ts(dst, src, w, None, ALU.mult) if j == 0 else stt(dst, src, w, dst, ALU.mult, ALU.add)
                        if j < CONV - 1:
                            V.do(ins)
                        else:
                            give(ins, "conv_out", i + 1, 4)

                dve.wait_ge(s["acc_done"], lay + 1)
                unit_lo(0)
                unit_lo(1)
                turn_parts(xtl, xth, "xt")
                V.do(cp(lbl[:], lb[:, lay, :]))
                V.do(cp(omlbl[:], omlb[:, lay, :]))
                V.do(v.memset(cin[:, :, 0:CONV - 1], 0.0))
                pre(0)
                core("conv_w")
                read(cp(cw[:].rearrange("p j c -> p (j c)"), pc[:, 0, 0:64]), "conv_w")
                V.do(cp(wbahl[:, :, 0:8], wba[:]))
                V.settle()
                give(tt(wbahl[:, :, 8:16], wba[:], wbahl[:, :, 0:8].bitcast(F32), ALU.subtract), "wba_ready")
                post(0)
                conv(0, 0, (0, 1))
                part = lambda i: small[:, i, :].rearrange("p (t h) -> p t h", t=TT)

                def small_parts():
                    core("bat")
                    bah = pc[:, 0, 0:16].rearrange("p (t n) -> p t n", t=TT)
                    V.do(cp(part(2), bah[:, :, 0:H]))
                    read(tt(part(3), bah[:, :, H:2 * H], mcast(dtb, TT), ALU.add), "bat")
                    V.settle()
                    give(ts(small[:, 6, :], small[:, 3, :], 0.0, None, ALU.max), "ba_raw")

                def thin_out(name, dst, n):
                    core(name)
                    V.do(cp(dst[0:2 * n, 0:T], pc[0:2 * n, 0, 0:T]))
                    read(cp(dst[0:n, T:2 * T], pc[0:n, 0, T:2 * T]), name)

                def first():
                    conv(0, 0, (2, 3))
                    thin_out("ba", bat, 8)

                around(1, mid=first)
                around(2, mid=small_parts, after=lambda: conv(2, 1, (0, 1)))

                def beta_decay():
                    need("ba_exp")
                    V.do(ts(small[:, 1, :], small[:, 2, :], 1.0, None, ALU.add))
                    V.do(tt(small[:, 6, :], small[:, 6, :], small[:, 4, :], ALU.add))
                    V.settle()
                    V.do(v.reciprocal(small[:, 1, :], small[:, 1, :]))
                    V.settle()
                    V.do(ts(small[:, 7, :], small[:, 1, :], -1.0, None, ALU.mult))
                    give(stt(part(0), part(6), -1.0, small[:, 5, None, 0:H].to_broadcast([P, TT, H]), ALU.mult, ALU.mult), "beta_g")

                around(3, mid=lambda: conv(2, 1, (2, 3)))
                beta_decay()

                def columns():
                    core("gcol")
                    read(cp(small[:, 2, :], pc[:, 0, 0:8]), "gcol")
                    V.tell(s["gcol_in"])

                around(4, mid=columns)

                def forget_den():
                    need("hf_exp")
                    V.do(tt(hf, hg, he, ALU.mult))
                    V.settle()
                    for h in range(H):
                        V.do(stt(hg[:, h, :], he[:, h, :], lbl[:, h:h + 1], hg[:, h, :], ALU.mult, ALU.add))
                    V.settle()
                    give(ts(hg, hg, TINY, None, ALU.max), "hf_den")

                def rope(b, i):
                    src = block_in(b).rearrange("p t (h s e) -> p t h s e", h=H, s=2)
                    half = rqk[:, :, i * 512:(i + 1) * 512]
                    dst = half.rearrange("p t (h s e) -> p t h s e", h=H, s=2)
                    tmp = gate[:].rearrange("p t (h s e) -> p t h s e", h=H, s=2)
                    for t in range(TT):
                        for sd in range(2):
                            V.do(tt(tmp[:, t, :, sd, :], src[:, t, :, 1 - sd, :], mcast(sin[:, t, sd, :], H), ALU.mult))
                            V.do(tt(dst[:, t, :, sd, :], src[:, t, :, sd, :], mcast(cos[:, t, :], H), ALU.mult))
                    V.tell(block_read[b % 2])
                    V.do(tt(half, half, gate[:], ALU.add), s["rope_done"], lay * 2 + i + 1)
                    V.settle()

                def h_halves(l):
                    w = 2 ** l
                    return [ap.rearrange("p h (b s) -> p (h b) s", s=2 * w) for ap in (hg, he, hf, hk, hq)] + [w]

                def h_differences(l):
                    V.settle()
                    g, e, _, _, _, w = h_halves(l)
                    mid = g[:, :, w - 1:w].to_broadcast([P, g.shape[1], w])
                    V.do(tt(e[:, :, 0:w], mid, g[:, :, 0:w], ALU.subtract))
                    if l < 7:
                        V.do(tt(e[:, :, w:2 * w], g[:, :, w:2 * w], mid, ALU.subtract))
                    else:
                        V.do(cp(e[:, :, w:2 * w], g[:, :, w:2 * w]))
                    V.tell(s["h_diff"])

                def h_factors(l):
                    if l < 8:
                        _, e, f, kk, qq, w = h_halves(l)
                        need("h_exp", l + 1, 8)
                        if l:
                            core(f"h{l - 1}")
                        V.do(tt(f[:, :, 0:w], e[:, :, 0:w], kk[:, :, 0:w], ALU.mult))
                        give(tt(f[:, :, w:2 * w], e[:, :, w:2 * w], qq[:, :, w:2 * w], ALU.mult), "h_fac", l + 1, 9)
                        if l < 7:
                            h_differences(l + 1)
                    else:
                        V.tell(s["h_fac"])

                def h_read(l):
                    if l == 7:
                        return
                    core(f"h{l}")
                    V.hold()
                    mk = mcast(eyeb, 8) if l == 8 else mcast(maskt[:, l, :], 8)
                    read(v.copy_predicated(atth[:], mk, pc[:, 2:4, :].rearrange("p b (h t) -> p (b h) t", h=H)), f"h{l}")

                def inverse_read(l):
                    core(f"yz{l}")
                    V.hold()
                    if l < LEVELS - 1:
                        V.do(v.copy_predicated(ti[:], mcast(mask[:, l, :], 8), pc[:, 0:2, :].rearrange("p b (h t) -> p (b h) t", h=H)))
                    read(v.copy_predicated(ui[:], mcast(maskt[:, l, :], 8), pc[:, 2:4, :].rearrange("p b (h t) -> p (b h) t", h=H)), f"yz{l}")
                    V.settle()
                    V.tell(s["level_t"])

                def gate_bias(i, b):
                    src = block_in(b)
                    dve.wait_ge(mbias_in, 16 * (lay * 6 + i + 1))
                    V.do(tt(gates[i], src, mcast(mbias, TT), ALU.add), s["gate_raw"], lay * 6 + i + 1)
                    V.tell(block_read[b % 2])

                def merge(i, b, k):
                    src = block_in(b)
                    need("gate_out", i + 1, 6)
                    mg = merged[:, :, k * 512:(k + 1) * 512]
                    if i < 2:
                        V.do(tt(mg, src, gates[i], ALU.mult), s["merged_ready"], lay * 6 + i + 1)
                        V.tell(block_read[b % 2])
                    else:
                        block_out(tt(gates[i], src, gates[i], ALU.mult), b)
                        V.settle()
                        V.do(tt(mg, mg, gates[i], ALU.add), s["merged_ready"], lay * 6 + i + 1)
                    V.settle()

                def gated(i, b0, b1):
                    for b in (b0, b1):
                        dve.wait_ge(block_read[b % 2], lay * (NBLK // 2) + b // 2 + 2)
                    V.settle()
                    for k in range(2):
                        yy = y[:, :, k * 512:(k + 1) * 512]
                        ins = tt(yy, yy, gt[:, k, :, :], ALU.mult)
                        V.do(ins) if k == 0 else give(ins, "y_done", i, 3)

                def rms_scale(name, k):
                    need("rms_rstd", k, 2)
                    dve.wait_ge(gain_in, 16 * (lay * 2 + k))
                    for i in range(8):
                        src = pc[:, 2 * (i // 4) + (i % 4) // 2, (i % 2) * HV:(i % 2) * HV + HV]
                        ins = stt(y[:, i // 4, (i % 4) * HV:(i % 4) * HV + HV], src, rstd[:, i:i + 1], gain[:, :], ALU.mult, ALU.mult)
                        V.do(ins) if i < 7 else read(ins, name)

                around(5, mid=forget_den, after=lambda: rope(5, 0))

                def row_beta():
                    core("grow")
                    read(stt(at[:], pc[:, 2:4, :].rearrange("p b (h t) -> p (b h) t", h=H), -1.0, mcast(strict, 8), ALU.mult, ALU.mult),
                         "grow")
                    need("hf_lns")
                    for h in range(H):
                        V.do(stt(hk[:, h, :], hk[:, h, :], omlbl[:, h:h + 1], he[:, h, :], ALU.mult, ALU.mult))
                    V.do(tt(hf, hg, hf, ALU.subtract))
                    V.settle()
                    for i in range(8):
                        h, t = i // 2, i % 2
                        V.do(v.tensor_tensor_scan(hg[:, h, t * P:(t + 1) * P], ones[:, :], hf[:, h, t * P:(t + 1) * P], 0.0, ALU.mult, ALU.add))
                    h_differences(0)

                around(6, mid=row_beta)
                need("lnexp_gn")
                V.do(stt(gqkv[:, 0:4, :], gqkv[:, 0:4, :], KSCALE, sq[:, 0:4, :], ALU.mult, ALU.mult))
                give(tt(gqkv[:, 4:8, :], gqkv[:, 4:8, :], sq[:, 4:8, :], ALU.mult), "qk_normed")
                h_factors(0)

                def masked_decay():
                    need("dt_exp")
                    V.do(tt(dt_[:], dt_[:], mcast(upper, 8), ALU.mult))
                    V.settle()
                    V.do(tt(at[:], at[:], dt_[:], ALU.mult))

                around(7, mid=masked_decay, after=lambda: rope(7, 1))
                dve.wait_ge(inits, lay * 3 + 6)
                V.hold()

                def h_step(l):
                    h_read(l)
                    h_factors(l + 1)

                def keys_and_step():
                    core("gkt")
                    for h in range(H):
                        ins = ts(kd[:, h, :], pc[:, 0, h * P:(h + 1) * P], dt_[:, h, P - 1:P], None, ALU.mult)
                        V.do(ins) if h < H - 1 else read(ins, "gkt")
                    h_step(0)

                around(8, mid=keys_and_step, after=lambda: gate_bias(0, 8))

                def ret_scores():
                    core("rqk")
                    V.do(tt(attr, pc[:, 0:2, :].rearrange("p b (h t) -> p (b h) t", h=2), decay, ALU.mult))
                    read(tt(attr2, pc[:, 2, :].rearrange("p (h t) -> p h t", h=H), decay[:, :, 0:P], ALU.mult), "rqk")

                around(9, mid=ret_scores)
                core("gkk")
                V.do(tt(attg[:], pc[:, 2:4, :].rearrange("p b (h t) -> p (b h) t", h=H), dt_[:], ALU.mult))
                read(tt(at[:], pc[:, 0:2, :].rearrange("p b (h t) -> p (b h) t", h=H), at[:], ALU.mult), "gkk")
                V.tell(s["gkk_in"])
                for i in range(2):
                    g = gqkv[:, 4 * i:4 * i + 4, P:T]
                    V.do(tt(g, g, erow, ALU.mult))
                V.tell(erow_used)

                def ret_stats():
                    dve.wait_ge(core_read["a"], lay * READS["a"] + READ_AT["a"]["rout"])
                    for i in range(8):
                        V.do(v.bn_stats(stats[:, i, 0:6], y[:, i // 4, (i % 4) * HV:(i % 4) * HV + HV]))
                    V.settle()
                    for i in range(8):
                        V.do(v.bn_aggr(mv[:, i, :], stats[:, i, 0:6]))
                    V.settle()
                    give(cp(rstd[:, :], mv[:, :, 1]), "rvar")

                around(10, mid=ret_stats)
                h_step(1)
                need("rrstd")
                for i in range(8):
                    yy = y[:, i // 4, (i % 4) * HV:(i % 4) * HV + HV]
                    V.do(ts(yy, yy, mv[:, i, 0:1], rstd[:, i:i + 1], ALU.subtract, ALU.mult))

                def gated_step():
                    gated(1, 9, 10)
                    h_step(2)

                around(11, mid=gated_step)
                inverse_read(0)
                around(12, mid=lambda: turn_parts(ytl, yth, "ryt"))
                around(13, lambda: merge(0, 13, 0), mid=lambda: h_step(3))
                inverse_read(1)
                around(14, lambda: gate_bias(1, 14), mid=lambda: h_step(4))
                around(15, lambda: merge(1, 15, 1), mid=lambda: h_step(5))
                inverse_read(2)
                around(16, lambda: gate_bias(2, 16), mid=lambda: h_step(6))
                V.settle()
                V.do(v.memset(cin[:, :, 0:CONV - 1], 0.0))
                around(17, mid=lambda: h_factors(8))
                inverse_read(3)
                conv(17, 2, (0, 1))

                def last_scores():
                    h_read(8)
                    conv(17, 2, (2, 3))

                around(18, mid=last_scores)
                around(19, mid=lambda: rms_scale("hout", 1))
                gated(2, 18, 19)
                around(20, mid=lambda: inverse_read(4), after=lambda: conv(20, 3, (0, 1)))

                def fifth_inverse():
                    inverse_read(5)
                    conv(20, 3, (2, 3))

                around(21, lambda: gate_bias(3, 21), mid=fifth_inverse)
                turn_parts(ytl, yth, "hyt")
                around(22)
                inverse_read(6)

                def values_in():
                    core("gvt")
                    for i in range(8):
                        t, h = i // 4, i % 4
                        ins = ts(vb[:, t, h * HV:(h + 1) * HV], pc[:, 2 * t + h // 2, (h % 2) * HV:(h % 2) * HV + HV],
                                 small[:, 1, i:i + 1], None, ALU.mult)
                        V.do(ins) if i < 7 else read(ins, "gvt")

                around(23, lambda: merge(2, 23, 0), mid=values_in)
                around(24, lambda: merge(3, 24, 1))
                core("ks")
                for h in range(H):
                    vv = vb[:, 1, h * HV:(h + 1) * HV]
                    ins = stt(vv, pc[:, h // 2, (h % 2) * HV:(h % 2) * HV + HV], small[:, 7, 4 + h:5 + h], vv, ALU.mult, ALU.add)
                    V.do(ins) if h < H - 1 else read(ins, "ks")
                around(25)
                rms_scale("gout", 2)
                around(26, lambda: gate_bias(4, 26), mid=lambda: gated(3, 22, 25))
                around(27, lambda: gate_bias(5, 27), mid=lambda: turn_parts(ytl, yth, "gyt"))
                around(28, lambda: merge(4, 28, 0))

                def merged_low(i):
                    name = "mta" if i == 0 else "mtb"
                    core(name)
                    dve.wait_ge(turn_hi, (lay * len(TURNS) + TURNS.index("mt")) * 2 + i + 1)
                    read(tt(ytl[:, 4 * i:4 * i + 4, :].rearrange("p k t -> p (k t)"),
                            pc[:, 2 * i:2 * i + 2, :].rearrange("p b n -> p (b n)"),
                            yth[:, 4 * i:4 * i + 4, :].bitcast(F32).rearrange("p k t -> p (k t)"), ALU.subtract), name)
                    if i == 0:
                        V.tell(turn_lo)

                around(29, lambda: merge(5, 29, 1), mid=lambda: merged_low(0))
                merged_low(1)

                def residual(b, k):
                    src = block_in(b)
                    xx = x[:, :, k * 512:(k + 1) * 512]
                    block_out(stt(xx, xx, ALPHA, src, ALU.mult, ALU.add), b)

                def norm_stats(c):
                    V.settle()
                    for t in range(TT):
                        V.do(v.bn_stats(stats[:, t, 6 * c:6 * c + 6], x[:, t, 512 * c:512 * c + 512]))

                def layer_norm(k, gains, biases):
                    norm_stats(1)
                    V.settle()
                    for t in range(TT):
                        V.do(v.bn_aggr(mv[:, t, :], stats[:, t, :]))
                    V.settle()
                    give(cp(rstd[:, 0:2], mv[:, 0:2, 1]), "ln_var", k, 2)
                    dve.wait_ge(ln_in, 64 * lay + 32 * k)
                    for t in range(TT):
                        V.do(stt(x[:, t, :], x[:, t, :], mv[:, t, 0:1], gains, ALU.subtract, ALU.mult))
                    V.settle()
                    dve.wait_ge(s["ln_rstd"], lay * 2 + k)
                    for t in range(TT):
                        ins = stt(x[:, t, :], x[:, t, :], rstd[:, t:t + 1], biases, ALU.mult, ALU.add)
                        V.do(ins) if t == 0 else give(ins, "x_ready", k, 2)

                around(30, lambda: residual(30, 0))
                norm_stats(0)
                residual(31, 1)
                def lo(c, base):
                    dve.wait_ge(split_hi, base + c + 1)
                    V.do(tt(wlo[:, c % SPLIT], raw[:, c % RAW], whi[:, c % SPLIT].bitcast(F32), ALU.subtract), split_lo,
                         base + c + 1 + CREDIT)

                layer_norm(1, lng1, lnb1)
                for c in range(2):
                    lo(c, lay * 2 * PASS_UNITS)
                turn_parts(xtl, xth, "x1t")

                need("xh_ready")
                V.do(tt(xl[:], x[:], xh[:].bitcast(F32), ALU.subtract))
                lo(2, lay * 2 * PASS_UNITS)
                thin_out("router", rout_t, NE)
                for c in range(3, SPLIT):
                    lo(c, lay * 2 * PASS_UNITS)
                core("routert")
                read(cp(scores[:].rearrange("p t e -> p (t e)"), pc[:, 0, 0:TT * NE]), "routert")
                V.settle()
                V.tell(s["logits"])
                need("score_out")
                V.do(tt(biased[:], scores[:], mcast(rb, TT), ALU.add))
                V.settle()

                def ranks(dst, vals, groups, width):
                    vv = vals.rearrange("p t (g j) -> p (t g) j", j=width)
                    other = vv[:, :, None, :].to_broadcast([P, groups, width, width])
                    own = vv[:, :, :, None].to_broadcast([P, groups, width, width])
                    c, q = cmp[:, 0:groups], eq[:, 0:groups]
                    V.do(tt(c, other, own, ALU.is_gt))
                    V.do(tt(q, other, own, ALU.is_equal))
                    V.settle()
                    V.do(tt(q, q, tie[:, None, :, :].to_broadcast([P, groups, EG, EG]), ALU.mult))
                    V.settle()
                    V.do(tt(c, c, q, ALU.add))
                    V.settle()
                    V.do(v.tensor_reduce(dst.rearrange("p t (g i) -> p (t g) i", i=width), c, AX.X, ALU.add))
                    V.settle()

                ranks(rank[:], biased[:], TT * NG, EG)
                V.do(ts(rank[:], rank[:], 2.0, None, ALU.is_lt))
                V.settle()
                V.do(tt(chosen[:], biased[:], rank[:], ALU.mult))
                V.settle()
                V.do(v.tensor_reduce(gsum[:], chosen[:].rearrange("p t (g j) -> p t g j", j=EG), AX.X, ALU.add))
                V.settle()
                ranks(best[:], gsum[:], TT, NG)
                V.do(ts(best[:], best[:], 1.0, None, ALU.is_lt))
                V.settle()
                give(tt(chosen[:].rearrange("p t (g j) -> p (t g) j", j=EG), rank[:].rearrange("p t (g j) -> p (t g) j", j=EG),
                        best[:].rearrange("p t g -> p (t g)")[:, :, None].to_broadcast([P, TT * NG, EG]), ALU.mult), "chosen_ready")
                V.settle()
                V.do(tt(comb[:], scores[:], chosen[:], ALU.mult))
                V.settle()
                V.do(v.tensor_reduce(wsum[:, :, 0], comb[:], AX.X, ALU.add))
                V.settle()
                V.do(v.reciprocal(wsum[:, :, 1], wsum[:, :, 0]))
                V.settle()
                for t in range(TT):
                    V.do(ts(comb[:, t, :], comb[:, t, :], wsum[:, t, 1:2], None, ALU.mult))
                core("pos")
                V.do(v.tensor_reduce(wsum[:, 0, 0:1], pc[:, 0, 2 * NE:3 * NE], AX.X, ALU.max))
                read(stt(posm[:].rearrange("p t e -> p (t e)"), pc[:, 0, 0:TT * NE], 1.0, chosen[:].rearrange("p t e -> p (t e)"),
                         ALU.add, ALU.mult), "pos")
                V.settle()
                V.do(ts(posm[:], posm[:], -1.0, None, ALU.add))
                V.do(ts(flag[:], wsum[:, 0, 0:1], float(P), None, ALU.is_gt), flag_ready, lay + 1)
                V.settle()
                V.tell(s["moe_ready"])

                def expert_pass(p):
                    def choose(n, j, e):
                        V.do(cp(pcol[:, j, :], posm[:, :, e]))
                        V.do(cp(ccol[:, j, :], comb[:, :, e]))
                        V.settle()
                        for t in range(TT):
                            ins = ts(pick[:, j, t, :], iota[:, p * P:(p + 1) * P], pcol[:, j, t:t + 1], None, ALU.is_equal)
                            V.do(ins) if t == 0 else V.do(ins, se["pick_ready"], n + 1)

                    def gathered(n, j):
                        dve.wait_ge(se["gl_done"], n + 1)
                        V.do(cp(xgl[:, j].rearrange("p k t -> p (k t)"), pc[:, 2:4, :].rearrange("p b n -> p (b n)")), se["xgl_ready"], n + 1)

                    def expert(n, base, j, e=None, last_=False):
                        g = EXP_UNITS * j
                        V.n = 0
                        lo(g + 5, base)
                        dve.wait_ge(unit_done, base + g + 4 + CREDIT)
                        dve.wait_ge(se["silu_h"], n + 1)
                        V.do(tt(hs[:, :], hs[:, :], pc[:, 1, :], ALU.mult), se["h_ready"], n + 1)
                        if not last_:
                            gathered(n + 1, 1 - j)
                        dve.wait_ge(se["turned"], n + 1)
                        V.do(cp(cslot[:, j:j + 1], pc[:, 1, T:T + 1]))
                        V.do(cp(pickt[:, j, :], pc[:, 1, 0:T]), se["pickt_ready"], n + 1)
                        dve.wait_ge(se["hth_ready"], n + 1)
                        V.do(tt(htl[:].rearrange("p k t -> p (k t)"), pc[:, 0, :], hth[:].bitcast(F32).rearrange("p k t -> p (k t)"), ALU.subtract),
                             se["htl_ready"], n + 1)
                        if not last_:
                            for c in range(6, 9):
                                lo(g + c, base)
                        dve.wait_ge(se["yh_ready"], n + 1)
                        V.do(stt(yl[:, :], pc[:, 2:4, :].rearrange("p b n -> p (b n)"), cslot[:, j:j + 1], yh[:, :].bitcast(F32),
                                 ALU.mult, ALU.subtract), se["yl_ready"], n + 1)
                        if e is not None:
                            choose(n + 2, j, e)
                        if not last_:
                            for c in range(9, 11):
                                lo(g + c, base)
                        V.settle()
                        V.hold()
                        dve.sem_clear(chain_v)

                    n0 = (lay * 2 + p) * NE
                    u0 = (lay * 2 + p) * PASS_UNITS
                    V.restart()
                    dve.wait_ge(iota_in, 16 * lay + 16)
                    choose(n0, 0, 0)
                    choose(n0 + 1, 1, 1)
                    if p:
                        for c in range(SPLIT):
                            lo(c, u0)
                    gathered(n0, 0)
                    lo(SPLIT, u0)
                    V.settle()
                    V.hold()
                    dve.sem_clear(chain_v)
                    with dve.Fori(0, NE // 2 - 1) as it:
                        for j in range(2):
                            expert(n0 + it * 2 + j, u0 + it * 2 * EXP_UNITS, j, e=2 * it + j + 2)
                    expert(n0 + NE - 2, u0 + (NE - 2) * EXP_UNITS, 0)
                    expert(n0 + NE - 1, u0 + (NE - 2) * EXP_UNITS, 1, last_=True)
                    V.n = 0

                expert_pass(0)
                dve.wait_ge(flag_ready, lay + 1)
                V.hold()
                spill = dve.value_load(flag[0:1, 0:1], min_val=0, max_val=1)
                with dve.If(spill > 0):
                    expert_pass(1)
                with dve.Else():
                    dve.wait_ge(se["yl_ready"], (lay * 2 + 1) * NE)
                    dve.sem_inc(split_lo, PASS_UNITS)
                    for name in ("pick_ready", "xgl_ready", "h_ready", "pickt_ready", "htl_ready", "yl_ready"):
                        dve.sem_inc(se[name], NE)
                V.last = (se["yl_ready"], (lay * 2 + 2) * NE)
                dve.wait_ge(s["acc_done"], lay + 2)
                for t in range(TT):
                    V.do(stt(x[:, t, :], x[:, t, :], ALPHA, pb[:, 2 * t:2 * t + 2, :].rearrange("p b n -> p (b n)"), ALU.mult, ALU.add))
                norm_stats(0)
                layer_norm(2, lng2[:], lnb2[:])
                V.settle()
                V.tell(s["layer_open"])
                V.restart()


INPUTS = ["x", "positions", "w_in", "gdn_conv_w", "gdn_a_log", "gdn_dt_bias", "gdn_norm_g", "hgrn_lb", "hgrn_norm_g",
          "merge_b", "w_branch", "w_out", "ln1_g", "ln1_b", "router_w", "router_b", "moe_w_gate", "moe_w_up",
          "moe_w_down", "ln2_g", "ln2_b"]


def kernel(**inputs):
    import concourse.bacc as bacc
    from concourse.bass_utils import run_bass_kernel_spmd

    nc = bacc.Bacc("TRN2", target_bir_lowering=False, num_devices=1)
    tables = constants()
    arrays, args = {}, []
    for name in INPUTS + CONSTS:
        a = np.ascontiguousarray(inputs[name] if name in inputs else tables[name])
        arrays[f"in_{name}"] = a
        args.append(nc.dram_tensor(f"in_{name}", a.shape, mybir.dt.from_np(a.dtype), kind="ExternalInput").ap())
    args.append(nc.dram_tensor("decoded", (1, T, D), F32, kind="ExternalOutput").ap())
    build_decoder(nc, *args)
    result = run_bass_kernel_spmd(nc, [arrays], core_ids=[0])
    return result.results[0]["decoded"]
```
